# Optimizing a Trainium2 kernel written in Bass

```python
import math
import jax, jax.numpy as jnp
from jax import lax
import numpy as np

D_MODEL = 1024
BATCH = 1
SEQ = 1024
DEPTH = 1
DEC_BATCH = 8
DEC_SEQ = 8
PAST_LEN = 8192
PAGE_SIZE = 128

N_META = 16
SC_WIDTH = D_MODEL
SC_TAPS = 3
GDN_HEADS = 8
GDN_DK = 128
GDN_DV = 128
GDN_KEY = GDN_HEADS * GDN_DK
GDN_VAL = GDN_HEADS * GDN_DV
GDN_QKV = 2 * GDN_KEY + GDN_VAL
GDN_TAPS = 4
GDN_CHUNK = 64
D_FF = 2816
IN_COLS = 3 * SC_WIDTH + GDN_QKV + 2 * GDN_HEADS + GDN_VAL + 2 * D_MODEL
EPS = 1e-6
L2_EPS = 1e-6

kernel_name = 'macaron_gated_shortconv_deltanet_step'

def rmsnorm(x, g):
    xf = x.astype(jnp.float32)
    y = xf * lax.rsqrt(jnp.mean(xf * xf, axis=-1, keepdims=True) + EPS)
    return (y * g.astype(jnp.float32)).astype(x.dtype)

def l2norm(x):
    return x * lax.rsqrt(jnp.sum(x * x, axis=-1, keepdims=True) + L2_EPS)

def swiglu(x, w_gate, w_up, w_down):
    return (jax.nn.silu(x @ w_gate) * (x @ w_up)) @ w_down

def causal_dwconv(x, buf, w):
    taps = w.shape[0]
    l = x.shape[1]
    xp = jnp.concatenate([buf.astype(x.dtype), x], axis=1)
    y = xp[:, 0:l] * w[0]
    for j in range(1, taps):
        y = y + xp[:, j:j + l] * w[j]
    return y, xp[:, l:]

def split_columns(proj):
    sizes = (SC_WIDTH, SC_WIDTH, SC_WIDTH, GDN_QKV, GDN_HEADS, GDN_HEADS, GDN_VAL, D_MODEL, D_MODEL)
    offs = np.cumsum(sizes)[:-1].tolist()
    return jnp.split(proj, offs, axis=-1)

def gdn_chunked(q, k, v, log_a, beta, s0, chunk):
    b, l, h, dk = q.shape
    dv = v.shape[-1]
    n = l // chunk

    def blk(t):
        t = t.reshape((b, n, chunk, h) + t.shape[3:])
        return jnp.moveaxis(t, 3, 2)

    q, k, v, log_a, beta = blk(q), blk(k), blk(v), blk(log_a), blk(beta)
    g = jnp.cumsum(log_a, axis=-1)
    diff = g[..., :, None] - g[..., None, :]
    idx = jnp.arange(chunk)
    strict = idx[:, None] > idx[None, :]
    incl = idx[:, None] >= idx[None, :]
    dec_strict = jnp.exp(jnp.where(strict, diff, -jnp.inf))
    dec_incl = jnp.exp(jnp.where(incl, diff, -jnp.inf))
    a_kk = beta[..., :, None] * jnp.einsum('bnhid,bnhjd->bnhij', k, k) * dec_strict
    rhs = jnp.concatenate([beta[..., None] * v, (beta * jnp.exp(g))[..., None] * k], axis=-1)
    sol = lax.linalg.triangular_solve(a_kk, rhs, left_side=True, lower=True, unit_diagonal=True)
    u, w = sol[..., :dv], sol[..., dv:]
    a_qk = jnp.einsum('bnhid,bnhjd->bnhij', q, k) * dec_incl
    q_dec = q * jnp.exp(g)[..., None]
    g_last = g[..., -1]
    k_dec = k * jnp.exp(g_last[..., None] - g)[..., None]

    def step(s, xs):
        u_c, w_c, aqk_c, qd_c, kd_c, gl_c = xs
        nu = u_c - jnp.einsum('bhcd,bhde->bhce', w_c, s)
        o = jnp.einsum('bhcd,bhde->bhce', qd_c, s) + jnp.einsum('bhij,bhje->bhie', aqk_c, nu)
        s = jnp.exp(gl_c)[..., None, None] * s + jnp.einsum('bhcd,bhce->bhde', kd_c, nu)
        return s, o

    xs = tuple(jnp.moveaxis(t, 1, 0) for t in (u, w, a_qk, q_dec, k_dec, g_last))
    s_fin, o = lax.scan(step, s0, xs)
    o = jnp.transpose(o, (1, 0, 3, 2, 4)).reshape(b, l, h, dv)
    return o, s_fin

def gdn_mixer(qkv_pre, a_raw, b_raw, z, conv_buf, s0, conv_w, a_log, dt_bias, norm_g, segments):
    bsz, l, _ = qkv_pre.shape
    f32 = jnp.float32
    qkv, conv_buf = causal_dwconv(qkv_pre, conv_buf, conv_w)
    qkv = jax.nn.silu(qkv).astype(f32)
    q, k, v = jnp.split(qkv, [GDN_KEY, 2 * GDN_KEY], axis=-1)
    q = l2norm(q.reshape(bsz, l, GDN_HEADS, GDN_DK)) * (GDN_DK ** -0.5)
    k = l2norm(k.reshape(bsz, l, GDN_HEADS, GDN_DK))
    v = v.reshape(bsz, l, GDN_HEADS, GDN_DV)
    beta = jax.nn.sigmoid(b_raw.astype(f32))
    log_a = -jnp.exp(a_log.astype(f32)) * jax.nn.softplus(a_raw.astype(f32) + dt_bias.astype(f32))
    s = s0.astype(f32)
    outs = []
    start = 0
    for seg_len, chunk in segments:
        sl = slice(start, start + seg_len)
        o_seg, s = gdn_chunked(q[:, sl], k[:, sl], v[:, sl], log_a[:, sl], beta[:, sl], s, chunk)
        outs.append(o_seg)
        start += seg_len
    o = jnp.concatenate(outs, axis=1)
    zh = z.astype(f32).reshape(bsz, l, GDN_HEADS, GDN_DV)
    o = rmsnorm(o, norm_g) * jax.nn.silu(zh)
    return o.reshape(bsz, l, GDN_VAL).astype(qkv_pre.dtype), conv_buf, s.astype(s0.dtype)

def layer(x, sc_buf, gdn_buf, gdn_s, segments, w):
    (n_f1, f1_g, f1_u, f1_d, n_mix, w_in, sc_w, gc_w, a_log, dt_bias, g_norm,
     w_a, w_b, w_o, n_f2, f2_g, f2_u, f2_d) = w
    x = x + 0.5 * swiglu(rmsnorm(x, n_f1), f1_g, f1_u, f1_d)
    h = rmsnorm(x, n_mix)
    proj = h @ w_in
    sc_b, sc_c, sc_x, qkv_pre, a_raw, b_raw, z, gate_a, gate_b = split_columns(proj)
    conv_out, sc_buf = causal_dwconv(sc_c * sc_x, sc_buf, sc_w)
    y_a = sc_b * conv_out
    y_b, gdn_buf, gdn_s = gdn_mixer(qkv_pre, a_raw, b_raw, z, gdn_buf, gdn_s, gc_w,
                                    a_log, dt_bias, g_norm, segments)
    merged = jax.nn.sigmoid(gate_a) * (y_a @ w_a) + jax.nn.sigmoid(gate_b) * (y_b @ w_b)
    x = x + merged @ w_o
    x = x + 0.5 * swiglu(rmsnorm(x, n_f2), f2_g, f2_u, f2_d)
    return x, sc_buf, gdn_buf, gdn_s

def trunk(x, sc_bufs, gdn_bufs, gdn_states, segments, weights, norm_final):
    new_sc, new_gc, new_gs = [], [], []
    for i in range(DEPTH):
        x, sc, gc, gs = layer(x, sc_bufs[i], gdn_bufs[i], gdn_states[i], segments,
                              tuple(wt[i] for wt in weights))
        new_sc.append(sc)
        new_gc.append(gc)
        new_gs.append(gs)
    return rmsnorm(x, norm_final), jnp.stack(new_sc), jnp.stack(new_gc), jnp.stack(new_gs)

def setup_inputs(seed: int = 0) -> dict:
    key = jax.random.key(seed)
    ks = jax.random.split(key, 32)
    f32 = jnp.float32

    def nrm(k, shape, scale):
        return jax.random.normal(k, shape, f32) * scale

    def gain(k, shape):
        return 1.0 + 0.02 * jax.random.normal(k, shape, f32)

    dt = jnp.exp(jax.random.uniform(ks[14], (DEPTH, GDN_HEADS), f32, math.log(1e-3), math.log(1e-1)))
    dt_bias = dt + jnp.log(-jnp.expm1(-dt))
    a_log = jnp.log(jax.random.uniform(ks[13], (DEPTH, GDN_HEADS), f32, 1.0, 16.0))
    return {
        'x_prompt': nrm(ks[0], (BATCH, SEQ, D_MODEL), 1.0),
        'x_sample': nrm(ks[1], (DEC_BATCH, DEC_SEQ, D_MODEL), 1.0),
        'state_sconv': nrm(ks[2], (DEPTH, DEC_BATCH, SC_TAPS - 1, SC_WIDTH), 1.0),
        'state_gdn_conv': nrm(ks[3], (DEPTH, DEC_BATCH, GDN_TAPS - 1, GDN_QKV), 1.0),
        'state_gdn': nrm(ks[4], (DEPTH, DEC_BATCH, GDN_HEADS, GDN_DK, GDN_DV), 0.1),
        'meta_tokens': nrm(ks[5], (N_META, D_MODEL), 1.0),
        'norm_ffn1': gain(ks[6], (DEPTH, D_MODEL)),
        'ffn1_w_gate': nrm(ks[7], (DEPTH, D_MODEL, D_FF), D_MODEL ** -0.5),
        'ffn1_w_up': nrm(ks[8], (DEPTH, D_MODEL, D_FF), D_MODEL ** -0.5),
        'ffn1_w_down': nrm(ks[9], (DEPTH, D_FF, D_MODEL), D_FF ** -0.5),
        'norm_mix': gain(ks[10], (DEPTH, D_MODEL)),
        'w_in': nrm(ks[11], (DEPTH, D_MODEL, IN_COLS), D_MODEL ** -0.5),
        'sconv_w': nrm(ks[12], (DEPTH, SC_TAPS, SC_WIDTH), SC_TAPS ** -0.5),
        'gdn_conv_w': nrm(ks[15], (DEPTH, GDN_TAPS, GDN_QKV), GDN_TAPS ** -0.5),
        'gdn_a_log': a_log,
        'gdn_dt_bias': dt_bias,
        'gdn_norm': gain(ks[16], (DEPTH, GDN_DV)),
        'w_a_out': nrm(ks[17], (DEPTH, SC_WIDTH, D_MODEL), SC_WIDTH ** -0.5),
        'w_b_out': nrm(ks[18], (DEPTH, GDN_VAL, D_MODEL), GDN_VAL ** -0.5),
        'w_o': nrm(ks[19], (DEPTH, D_MODEL, D_MODEL), D_MODEL ** -0.5),
        'norm_ffn2': gain(ks[20], (DEPTH, D_MODEL)),
        'ffn2_w_gate': nrm(ks[21], (DEPTH, D_MODEL, D_FF), D_MODEL ** -0.5),
        'ffn2_w_up': nrm(ks[22], (DEPTH, D_MODEL, D_FF), D_MODEL ** -0.5),
        'ffn2_w_down': nrm(ks[23], (DEPTH, D_FF, D_MODEL), D_FF ** -0.5),
        'norm_final': gain(ks[24], (D_MODEL,)),
    }

def reference(x_prompt, x_sample, state_sconv, state_gdn_conv, state_gdn, meta_tokens,
              norm_ffn1, ffn1_w_gate, ffn1_w_up, ffn1_w_down, norm_mix, w_in, sconv_w,
              gdn_conv_w, gdn_a_log, gdn_dt_bias, gdn_norm, w_a_out, w_b_out, w_o,
              norm_ffn2, ffn2_w_gate, ffn2_w_up, ffn2_w_down, norm_final):
    weights = (norm_ffn1, ffn1_w_gate, ffn1_w_up, ffn1_w_down, norm_mix, w_in, sconv_w,
               gdn_conv_w, gdn_a_log, gdn_dt_bias, gdn_norm, w_a_out, w_b_out, w_o,
               norm_ffn2, ffn2_w_gate, ffn2_w_up, ffn2_w_down)
    bsz, seq = x_prompt.shape[0], x_prompt.shape[1]
    dt = x_prompt.dtype
    meta = jnp.broadcast_to(meta_tokens.astype(dt)[None], (bsz, N_META, D_MODEL))
    xp = jnp.concatenate([meta, x_prompt], axis=1)
    zero_sc = jnp.zeros((DEPTH, bsz, SC_TAPS - 1, SC_WIDTH), dt)
    zero_gc = jnp.zeros((DEPTH, bsz, GDN_TAPS - 1, GDN_QKV), dt)
    zero_gs = jnp.zeros((DEPTH, bsz, GDN_HEADS, GDN_DK, GDN_DV), dt)
    seg_prompt = ((N_META, N_META), (seq, GDN_CHUNK))
    yp, p_sc, p_gc, p_gs = trunk(xp, zero_sc, zero_gc, zero_gs, seg_prompt, weights, norm_final)
    y_prompt = yp[:, N_META:]
    dec_len = x_sample.shape[1]
    seg_sample = ((dec_len, dec_len),)
    y_sample, s_sc, s_gc, s_gs = trunk(x_sample, state_sconv, state_gdn_conv, state_gdn,
                                       seg_sample, weights, norm_final)
    return (y_prompt, y_sample, p_sc, p_gc, p_gs, s_sc, s_gc, s_gs)


_drawn_inputs = setup_inputs


def setup_inputs(seed=0):
    import zlib

    import numpy as np

    out = dict(_drawn_inputs(seed))
    spreads = {}
    factors = {'norm_ffn1': 4.212,
     'gdn_norm': 42.261,
     'norm_ffn2': 8.0,
     'norm_final': 22.963,
     'state_sconv': 3.15}
    for name, (base, spread) in spreads.items():
        noise = np.random.default_rng([zlib.crc32(name.encode()), seed]).standard_normal(out[name].shape)
        drawn = base * np.exp(spread * noise) if base else spread * noise
        out[name] = __import__('jax').numpy.asarray(drawn.astype(out[name].dtype))
    for name, factor in factors.items():
        out[name] = (out[name] * factor).astype(out[name].dtype)
    return out
```

```python
from contextlib import ExitStack

import numpy as np
import concourse.bass as bass
from concourse import mybir

F32 = mybir.dt.float32
F32R = mybir.dt.float32r
ALU = mybir.AluOpType
ACT = mybir.ActivationFunctionType

P = 128
D = 1024
KC = D // P
FF = 2816
N_META = 16
SEQ = 1024
NS = 8
LS = 8
H = 8
PT = N_META + SEQ
T = PT + NS * LS
TH = T // 3
NB = 3
EPS = 1e-6
SC_T = 3
GC_T = 4
QKV = 3 * H * P
COL_B, COL_C, COL_X = 0, D, 2 * D
COL_QKV = 3 * D
COL_AB = COL_QKV + QKV
COL_Z = COL_AB + 2 * H
COL_GA = COL_Z + D
COL_GB = COL_GA + D
NT = T // P
TAIL = T - NT * P
NSEG = 1 + NS
PT_TAIL = PT - NT * P
LEVELS = 7
TAIL_LEVELS = 4


class Chain:

    def __init__(self, sem, base=0, turn=0, per=0):
        self.sem, self.base, self.turn, self.per, self.n = sem, base, turn, per, 0

    def link(self, eng, ins):
        ins.then_inc(self.sem, 1)
        self.n += 1
        eng.wait_ge(self.sem, self.turn * self.per + (self.base + self.n))

    def end(self):
        assert self.per in (0, self.n), (self.per, self.n)
        return self.base + self.n


class Scope:

    def __init__(self, nc, ctx, phase):
        self.nc, self.ctx, self.phase, self.sems = nc, ctx, phase, []

    def sb(self, name, shape, dt=F32):
        return self.ctx.enter_context(self.nc.sbuf_tensor(f"{self.phase}_{name}", shape, dt))

    def ps(self, name, shape):
        return self.ctx.enter_context(self.nc.psum_tensor(f"{self.phase}_{name}", shape, F32))

    def sem(self, name):
        handle = self.ctx.enter_context(self.nc.semaphore(f"{self.phase}_{name}"))
        self.sems.append(handle.num)
        return handle

    def block(self):
        self.ctx.callback(self.clear)
        return self.ctx.enter_context(self.nc.Block())

    def clear(self):
        numbers = sorted(self.sems)
        while numbers:
            first = last = numbers.pop(0)
            while numbers and numbers[0] == last + 1:
                last = numbers.pop(0)
            self.nc.gpsimd.sem_clear(range(first, last + 1))
        self.nc.all_engine_barrier()


def third(b):
    return slice(b * TH, (b + 1) * TH)


class WeightStream:

    def __init__(self, s, slots):
        self.slots = slots
        self.raw = s.sb("w_raw", [P, slots, KC, P])
        self.hi = s.sb("w_hi", [P, slots, KC, P], F32R)
        self.lo = s.sb("w_lo", [P, slots, KC, P], F32R)
        self.raw_loaded = [s.sem(f"w_raw_loaded{k}") for k in range(slots)]
        self.raw_free = s.sem("w_raw_free")
        self.hi_done = s.sem("w_hi_done")
        self.lo_done = s.sem("w_lo_done")
        self.split_free = s.sem("w_split_free")

    def load(self, sp, i, per, j, src, shape=None):
        sp.wait_ge(self.raw_free, i * per + (j + 1))
        k = j % self.slots
        dst = self.raw[:, k, :, :]
        if shape is not None:
            dst = dst.rearrange("p k n -> p (k n)").rearrange("p (a b) -> p a b", a=shape)
        sp.dma_start(dst, src).then_inc(self.raw_loaded[k], 16)

    def split_hi(self, act, i, per, j):
        k = j % self.slots
        act.wait_ge(self.raw_loaded[k], i * (16 * per // self.slots) + 16 * (j // self.slots + 1))
        act.wait_ge(self.split_free, i * per + (j + 1))
        act.activation(self.hi[:, k, :, :], self.raw[:, k, :, :], ACT.Copy).then_inc(self.hi_done, 1)

    def split_lo(self, pool, i, per, j):
        k = j % self.slots
        pool.wait_ge(self.hi_done, i * per + (j + 1))
        pool.tensor_tensor(self.lo[:, k, :, :], self.raw[:, k, :, :], self.hi[:, k, :, :].bitcast(F32),
                           ALU.subtract).then_inc(self.lo_done, 1)
        pool.wait_ge(self.lo_done, i * per + (j + 1))
        pool.sem_inc(self.raw_free, 1)

    def credit_raw(self, pool):
        pool.sem_inc(self.raw_free, self.slots)

    def credit_split(self, pe):
        pe.sem_inc(self.split_free, self.slots - 1)


def three_passes(pe, out, w_hi, w_lo, x_hi, x_lo, first, last):
    pe.matmul(out, w_hi, x_hi, start=first, stop=False)
    pe.matmul(out, w_hi, x_lo, start=False, stop=False)
    return pe.matmul(out, w_lo, x_hi, start=False, stop=last)


def transpose_inputs(nc, c, x, ident, ones, eps, gains, taps, sc_hist, gc_hist):
    x_prompt, x_sample, meta = c["x_prompt"], c["x_sample"], c["meta_tokens"]
    state_sconv, state_gdn_conv = c["state_sconv"], c["state_gdn_conv"]
    with ExitStack() as ctx:
        s = Scope(nc, ctx, "tr")
        NJ = 9
        rows = s.sb("rows", [P, 3, D])
        hist = s.sb("hist", [P, QKV + D])
        ps = [s.ps(f"ps{k}", [P, 4, P]) for k in range(6)]
        rows_loaded = [s.sem(f"rows_loaded{k}") for k in range(3)]
        ident_loaded, hist_loaded, tables_loaded = s.sem("ident_loaded"), s.sem("hist_loaded"), s.sem("tables_loaded")
        turned = s.sem("turned")
        vec_out, act_out = s.sem("vec_out"), s.sem("act_out")
        NHIST = (QKV + D) // P
        tail_rows = N_META + NS * LS
        block = s.block()

        @block.sync
        def _(sp):
            sp.dma_start(ident[:], c["identity"]).then_inc(ident_loaded, 16)
            for j in range(NJ):
                if j >= 3:
                    sp.wait_ge(turned, 2 * (j - 2))
                if j < 8:
                    sp.dma_start(rows[:, j % 3, :], x_prompt[0, j * P:(j + 1) * P, :]).then_inc(rows_loaded[j % 3], 16)
                else:
                    sp.dma_start(rows[0:N_META, j % 3, :], meta).then_inc(rows_loaded[j % 3], 16)
                    sp.dma_start(rows[N_META:tail_rows, j % 3, :],
                                 x_sample.rearrange("b t d -> (b t) d")).then_inc(rows_loaded[j % 3], 16)
            sp.dma_start(hist[0:NS * (GC_T - 1), 0:QKV],
                         state_gdn_conv[0].rearrange("s t c -> (s t) c")).then_inc(hist_loaded, 16)
            sp.dma_start(hist[0:NS * (SC_T - 1), QKV:QKV + D],
                         state_sconv[0].rearrange("s t c -> (s t) c")).then_inc(hist_loaded, 16)
            sp.dma_start(gains[:, :, :], c["gains"].rearrange("p (a k) -> p a k", a=4)).then_inc(tables_loaded, 16)
            sp.dma_start(taps[:, :], c["taps"]).then_inc(tables_loaded, 16)
            sp.wait_ge(tables_loaded, 32)

        @block.tensor
        def _(pe):
            pe.wait_ge(ident_loaded, 16)
            for j in range(NJ):
                n = P if j < 8 else tail_rows
                pe.wait_ge(rows_loaded[j % 3], 16 * (j // 3 + 1) + (16 if j == 8 else 0))
                for hf in range(2):
                    q = 2 * j + hf
                    if q >= 6:
                        pe.wait_ge(vec_out if hf == 0 else act_out, (q - 6) // 2 + 1)
                    for c in range(4):
                        k = 4 * hf + c
                        mm = pe.transpose(ps[q % 6][:, c, 0:n], rows[0:n, j % 3, k * P:(k + 1) * P], ident[0:n, 0:n])
                    mm.then_inc(turned, 1)
            pe.wait_ge(hist_loaded, 32)
            for g in range(NHIST // 4):
                q = 2 * NJ + g
                pe.wait_ge(vec_out if q % 2 == 0 else act_out, (q - 6) // 2 + 1)
                n = NS * (GC_T - 1) if g < 6 else NS * (SC_T - 1)
                for c in range(4):
                    k = 4 * g + c
                    mm = pe.transpose(ps[q % 6][:, c, 0:n], hist[0:n, k * P:(k + 1) * P], ident[0:n, 0:n])
                mm.then_inc(turned, 1)

        def copies(eng, odd, done):
            copy = eng.copy if odd else eng.tensor_copy
            for q in range(odd, 2 * NJ + NHIST // 4, 2):
                eng.wait_ge(turned, q + 1)
                b = ps[q % 6]
                if q < 2 * NJ:
                    j, k = q // 2, 4 * (q % 2)
                    if j < 8:
                        copy(x[:, k:k + 4, N_META + j * P:N_META + (j + 1) * P], b[:, :, :]).then_inc(done, 1)
                    else:
                        copy(x[:, k:k + 4, 0:N_META], b[:, :, 0:N_META])
                        copy(x[:, k:k + 4, PT:T], b[:, :, N_META:tail_rows]).then_inc(done, 1)
                elif q < 2 * NJ + 6:
                    g = q - 2 * NJ
                    copy(gc_hist[:, 4 * g:4 * g + 4, :], b[:, :, 0:NS * (GC_T - 1)]).then_inc(done, 1)
                else:
                    g = q - 2 * NJ - 6
                    copy(sc_hist[:, 4 * g:4 * g + 4, :], b[:, :, 0:NS * (SC_T - 1)]).then_inc(done, 1)

        @block.vector
        def _(dve):
            dve.memset(ones[:, :], 1.0)
            dve.memset(eps[:, :], EPS)
            copies(dve, 0, vec_out)

        @block.scalar
        def _(act):
            copies(act, 1, act_out)


class Norm:

    def __init__(self, s, x, gain, ones, eps_col, sq, ps):
        self.x, self.gain, self.ones, self.eps_col, self.sq, self.ps = x, gain, ones, eps_col, sq, ps
        self.rstd = s.sb("rstd", [P, T])
        self.squared = s.sem("nrm_squared")
        self.summed = s.sem("nrm_summed")
        self.sq_used = s.sem("nrm_sq_used")
        self.rooted = s.sem("nrm_rooted")
        self.factor = s.sem("nrm_factor")

    def squares(self, act):
        for k in range(KC):
            if k >= 2:
                act.wait_ge(self.sq_used, k - 1)
            act.activation(self.sq[:, k % 2, :], self.x[:, k, :], ACT.Square).then_inc(self.squared, 1)
        for b in range(NB):
            act.wait_ge(self.summed, 1)
            act.activation(self.rstd[:, third(b)], self.ps[b][:, 0:TH], ACT.Sqrt, bias=self.eps_col,
                           scale=1.0 / D).then_inc(self.rooted, 1)

    def sums(self, pe):
        for k in range(KC):
            pe.wait_ge(self.squared, k + 1)
            for b in range(NB):
                mm = pe.matmul(self.ps[b][:, 0:TH], self.ones, self.sq[:, k % 2, third(b)],
                               start=(k == 0), stop=(k == KC - 1))
            mm.then_inc(self.summed if k == KC - 1 else self.sq_used, 1)

    def factors(self, dve):
        for b in range(NB):
            dve.wait_ge(self.rooted, b + 1)
            dve.reciprocal(self.rstd[:, third(b)], self.rstd[:, third(b)]).then_inc(self.factor, 1)
        dve.wait_ge(self.factor, NB)


def ffn(nc, name, x, gains, g_at, ones, eps_col, w_gate, w_up, w_down):
    GROUPS = FF // (2 * P)
    TURNS = (GROUPS - 1) // 2
    PER = 6
    with ExitStack() as ctx:
        s = Scope(nc, ctx, name)
        h_hi = s.sb("h_hi", [P, KC, T], F32R)
        h_lo = s.sb("h_lo", [P, KC, T], F32R)
        mid_hi = s.sb("mid_hi", [P, 2, 2, T], F32R)
        mid_lo = s.sb("mid_lo", [P, 2, 2, T], F32R)
        w = WeightStream(s, 3)
        hid = s.sb("hid", [P, 2, T])
        bank = [s.ps(f"bank{k}", [P, 512]) for k in range(6)]
        nrm = Norm(s, x, gains[:, g_at, :], ones, eps_col, hid, bank)
        bank_free = [s.sem(f"bank_free{k}") for k in range(6)]
        h_scaled, h_hi_done, h_ready = s.sem("h_scaled"), s.sem("h_hi_done"), s.sem("h_ready")
        gu_done, down_done = s.sem("gu_done"), s.sem("down_done")
        mid_hi_done, mid_ready = s.sem("mid_hi_done"), s.sem("mid_ready")
        block = s.block()
        TURN = 12

        def first_block(par):
            return 0 if par == 0 else 4 + PER * (par - 1)

        def gu_use(par, a):
            return a if par == 0 else 6 * par - 4 + a

        @block.sync
        def _(sp):
            def gate_up(i, par):
                for a in range(2):
                    for q, src in enumerate((w_gate, w_up)):
                        w.load(sp, i, TURN, first_block(par) + 2 * a + q,
                               src[:, bass.ds(i * (4 * P) + (2 * par + a) * P, P)].rearrange("(k p) n -> p k n", p=P))

            def down(i, par, j0):
                for a in range(2):
                    w.load(sp, i, TURN, j0 + a,
                           w_down[bass.ds(i * (4 * P) + (2 * par + a) * P, P), :].rearrange("p (k n) -> p k n", n=P))

            gate_up(0, 0)
            with sp.Fori(0, TURNS) as i:
                for par in (1, 2):
                    gate_up(i, par)
                    down(i, par - 1, first_block(par) + 4)
            down(TURNS, 0, 4)

        @block.gpsimd
        def _(pool):
            w.credit_raw(pool)
            for j in range(4):
                w.split_lo(pool, 0, TURN, j)
            with pool.Fori(0, TURNS) as i:
                for j in range(4, 4 + TURN):
                    w.split_lo(pool, i, TURN, j)
            for j in (4, 5):
                w.split_lo(pool, TURNS, TURN, j)

        @block.tensor
        def _(pe):
            w.credit_split(pe)
            nrm.sums(pe)
            pe.wait_ge(nrm.factor, NB)
            for k in range(6):
                pe.sem_inc(bank_free[k], 1)

            def gate_up(i, par):
                for j in range(4):
                    a, q = divmod(j, 2)
                    n = first_block(par) + j
                    pe.wait_ge(w.lo_done, i * TURN + (n + 1))
                    for b in range(NB):
                        k6 = 3 * q + b
                        pe.wait_ge(bank_free[k6], i * TURN + (gu_use(par, a) + 1))
                        for k in range(KC):
                            if par == 0 and j == 0 and b == 0:
                                pe.wait_ge(h_ready, k + 1)
                            mm = three_passes(pe, bank[k6][:, 0:TH], w.hi[:, n % 3, k, :], w.lo[:, n % 3, k, :],
                                              h_hi[:, k, third(b)], h_lo[:, k, third(b)], k == 0, k == KC - 1)
                        mm.then_inc(gu_done, 1)
                        if b == 1 and par + j:
                            pe.wait_ge(gu_done, i * 24 + (12 * par + 3 * j + 1))
                            pe.sem_inc(w.split_free, 1 if j else 2)

            def down(i, par, n, use, after):
                m = par % 2
                pe.wait_ge(w.lo_done, i * TURN + (n + 2))
                pe.wait_ge(mid_ready, i * 12 + (6 * par + 6))
                for c in range(KC):
                    for b in range(NB):
                        k6 = 3 * (c % 2) + b
                        pe.wait_ge(bank_free[k6], i * TURN + (use + c // 2 + 1))
                        for a in range(2):
                            mm = three_passes(pe, bank[k6][:, 0:TH], w.hi[:, (n + a) % 3, c, :],
                                              w.lo[:, (n + a) % 3, c, :], mid_hi[:, m, a, third(b)],
                                              mid_lo[:, m, a, third(b)], a == 0, a == 1)
                        mm.then_inc(down_done, 1)
                        if after and c == 0 and b == 0:
                            pe.wait_ge(gu_done, i * 24 + 12 * (par + 2))
                            pe.sem_inc(w.split_free, 1)

            gate_up(0, 0)
            with pe.Fori(0, TURNS) as i:
                gate_up(i, 1)
                down(i, 0, first_block(1) + 4, 4, True)
                gate_up(i, 2)
                down(i, 1, first_block(2) + 4, 10, True)
            pe.wait_ge(down_done, 24 * 2 * TURNS)
            pe.sem_inc(w.split_free, 2)
            down(TURNS, 0, 4, 2, False)

        @block.scalar
        def _(act):
            w.split_hi(act, 0, TURN, 0)
            nrm.squares(act)
            for k in range(KC):
                act.wait_ge(h_scaled, k + 1)
                act.copy(h_hi[:, k, :], hid[:, k % 2, :]).then_inc(h_hi_done, 1)

            def gate_up(i, par):
                n = first_block(par)
                for a in range(2):
                    w.split_hi(act, i, TURN, n + 2 * a + 1)
                    for b in range(NB):
                        act.wait_ge(gu_done, i * 24 + (12 * par + 6 * a + b + 1))
                        if par == 0:
                            act.wait_ge(h_ready, KC)
                        else:
                            act.wait_ge(mid_ready, i * 12 + (6 * (par - 1) + 3 * a + b + 1))
                        act.activation(hid[:, a, third(b)], bank[b][:, 0:TH], ACT.Silu).then_inc(bank_free[b], 1)
                    w.split_hi(act, i, TURN, n + 2 * a + 2)
                    for b in range(NB):
                        act.wait_ge(bank_free[3 + b], i * TURN + (gu_use(par, a) + 2))
                        act.copy(mid_hi[:, par % 2, a, third(b)], hid[:, a, third(b)]).then_inc(mid_hi_done, 1)

            gate_up(0, 0)
            with act.Fori(0, TURNS) as i:
                for par in (1, 2):
                    gate_up(i, par)
                    w.split_hi(act, i, TURN, first_block(par) + 5)
                    w.split_hi(act, i, TURN, first_block(par) + 6)
            w.split_hi(act, TURNS, TURN, 5)

        @block.vector
        def _(dve):
            nrm.factors(dve)
            for k in range(KC):
                if k >= 2:
                    dve.wait_ge(h_ready, k - 1)
                dve.scalar_tensor_tensor(hid[:, k % 2, :], x[:, k, :], gains[:, g_at, k:k + 1], nrm.rstd[:, :],
                                         ALU.mult, ALU.mult).then_inc(h_scaled, 1)
                dve.wait_ge(h_hi_done, k + 1)
                dve.tensor_tensor(h_lo[:, k, :], hid[:, k % 2, :], h_hi[:, k, :].bitcast(F32),
                                  ALU.subtract).then_inc(h_ready, 1)

            def gate_up(i, par):
                for a in range(2):
                    for b in range(NB):
                        dve.wait_ge(gu_done, i * 24 + (12 * par + 6 * a + 3 + b + 1))
                        dve.wait_ge(bank_free[b], i * TURN + (gu_use(par, a) + 2))
                        dve.tensor_tensor(hid[:, a, third(b)], bank[3 + b][:, 0:TH], hid[:, a, third(b)],
                                          ALU.mult).then_inc(bank_free[3 + b], 1)
                        dve.wait_ge(mid_hi_done, i * 12 + (6 * par + 3 * a + b + 1))
                        dve.tensor_tensor(mid_lo[:, par % 2, a, third(b)], hid[:, a, third(b)],
                                          mid_hi[:, par % 2, a, third(b)].bitcast(F32),
                                          ALU.subtract).then_inc(mid_ready, 1)

            def down(i, par):
                for c in range(KC):
                    for b in range(NB):
                        k6 = 3 * (c % 2) + b
                        dve.wait_ge(down_done, i * 48 + (24 * par + 3 * c + b + 1))
                        dve.scalar_tensor_tensor(x[:, c, third(b)], bank[k6][:, 0:TH], 0.5, x[:, c, third(b)],
                                                 ALU.mult, ALU.add).then_inc(bank_free[k6], 1)

            gate_up(0, 0)
            with dve.Fori(0, TURNS) as i:
                gate_up(i, 1)
                down(i, 0)
                gate_up(i, 2)
                down(i, 1)
            down(TURNS, 0)


def final_output(nc, x, gains, g_at, ones, eps_col, ident, y_prompt, y_sample):
    with ExitStack() as ctx:
        s = Scope(nc, ctx, "fin")
        sq = s.sb("sq", [P, 2, T])
        y = s.sb("y", [P, KC, T])
        rows = s.sb("rows", [P, 3, D])
        bank = [s.ps(f"bank{k}", [P, 512]) for k in range(6)]
        nrm = Norm(s, x, gains[:, g_at, :], ones, eps_col, sq, bank)
        scaled, turned = s.sem("scaled"), s.sem("turned")
        vec_out, act_out, stored = s.sem("vec_out"), s.sem("act_out"), [s.sem(f"stored{k}") for k in range(3)]
        block = s.block()
        NJ = 9

        @block.tensor
        def _(pe):
            nrm.sums(pe)
            pe.wait_ge(scaled, KC)
            for q in range(2 * NJ):
                j, k = q // 2, 4 * (q % 2)
                n = P if j < 8 else NS * LS
                if q >= 6:
                    pe.wait_ge(vec_out if q % 2 == 0 else act_out, (q - 6) // 2 + 1)
                for c in range(4):
                    mm = pe.transpose(bank[q % 6][0:n, c * P:(c + 1) * P],
                                      y[:, k + c, N_META + j * P:N_META + j * P + n], ident[:, :])
                mm.then_inc(turned, 1)

        def copies(eng, odd, done):
            copy = eng.copy if odd else eng.tensor_copy
            for q in range(odd, 2 * NJ, 2):
                j = q // 2
                n = P if j < 8 else NS * LS
                eng.wait_ge(turned, q + 1)
                if j >= 3:
                    eng.wait_ge(stored[j % 3], 16 * (j // 3))
                copy(rows[0:n, j % 3, 512 * odd:512 * odd + 512], bank[q % 6][0:n, :]).then_inc(done, 1)

        @block.scalar
        def _(act):
            nrm.squares(act)
            copies(act, 1, act_out)

        @block.vector
        def _(dve):
            nrm.factors(dve)
            for k in range(KC):
                dve.scalar_tensor_tensor(y[:, k, :], x[:, k, :], gains[:, g_at, k:k + 1], nrm.rstd[:, :],
                                         ALU.mult, ALU.mult).then_inc(scaled, 1)
            copies(dve, 0, vec_out)

        @block.sync
        def _(sp):
            for j in range(NJ):
                sp.wait_ge(vec_out, j + 1)
                sp.wait_ge(act_out, j + 1)
                if j < 8:
                    sp.dma_start(y_prompt[0, j * P:(j + 1) * P, :], rows[:, j % 3, :]).then_inc(stored[j % 3], 16)
                else:
                    sp.dma_start(y_sample.rearrange("b t d -> (b t) d"),
                                 rows[0:NS * LS, j % 3, :]).then_inc(stored[j % 3], 16)
            for k in range(3):
                sp.wait_ge(stored[k], 16 * (NJ // 3))


def input_projections(nc, x, gains, ones, eps_col, w_in, sc_taps, gc_taps, sc_hist, gc_hist, sc_tail, gc_tail,
                      ab_rows, scratch):
    GP, SPD = GC_T - 1, SC_T - 1
    GL = GP + PT + NS * (GP + LS)
    SL = SPD + PT + NS * (SPD + LS)
    with ExitStack() as ctx:
        s = Scope(nc, ctx, "inp")
        h_hi = s.sb("h_hi", [P, KC, T], F32R)
        h_lo = s.sb("h_lo", [P, KC, T], F32R)
        w = WeightStream(s, 3)
        pre = s.sb("pre", [P, 3, GL])
        conv = s.sb("conv", [P, 3, GL])
        out = s.sb("out", [P, 3, T])
        sc_w = s.sb("sc_w", [P, SC_T])
        gc_w = s.sb("gc_w", [P, 3, GC_T])
        bank = [s.ps(f"bank{k}", [P, 512]) for k in range(3)]
        nrm = Norm(s, x, gains[:, 1, :], ones, eps_col, out, bank)
        bank_free = [s.sem(f"bank_free{k}") for k in range(3)]
        unit_done = s.sem("unit_done")
        h_scaled, h_hi_done, h_ready = s.sem("h_scaled"), s.sem("h_hi_done"), s.sem("h_ready")
        stored = [s.sem(f"stored{k}") for k in range(3)]
        y_ready, conv_done, silu_done = s.sem("y_ready"), s.sem("conv_done"), s.sem("silu_done")
        zsig_done, z_ready, pads_zero = s.sem("zsig_done"), s.sem("z_ready"), s.sem("pads_zero")
        vec = s.sem("vec")
        block = s.block()
        NBLK = 72
        cols = lambda n0, i: w_in[:, bass.ds(n0 + i * P, P)].rearrange("(k p) n -> p k n", p=P)

        @block.sync
        def _(sp):
            for k in range(3):
                sp.sem_inc(stored[k], 16)

            def loads(loop, i, ahead):
                starts = ((COL_B, COL_C, COL_X), (COL_QKV, COL_QKV + D, COL_QKV + 2 * D), (COL_Z, COL_GA, COL_GB))
                for j in range(3):
                    w.load(sp, i, 3, 24 * loop + 3 * ahead + j, cols(starts[loop][j] + ahead * P, i))

            def store_y(i):
                sp.wait_ge(y_ready, i + 2)
                sp.dma_start(scratch["y_a"][bass.ds(i, 1)].rearrange("c p t -> p (c t)"), out[:, 0, :]).then_inc(stored[0], 16)

            def store_qkv(i):
                for j in range(3):
                    sp.wait_ge(silu_done, i * 3 + (j + 1 + 3))
                    sp.dma_start(scratch["qkv"][j][bass.ds(i, 1)].rearrange("c p t -> p (c t)"), out[:, j, :]).then_inc(stored[j], 16)

            def store_gates(i):
                sp.wait_ge(z_ready, i * 3 + 6)
                sp.dma_start(scratch["z"][bass.ds(i, 1)].rearrange("c p t -> p (c t)"), out[:, 0, :]).then_inc(stored[0], 16)
                for j, name in ((1, "sig_a"), (2, "sig_b")):
                    sp.wait_ge(bank_free[2], i * 3 + (48 + j + 2))
                    sp.dma_start(scratch[name][bass.ds(i, 1)].rearrange("c p t -> p (c t)"), out[:, j, :]).then_inc(stored[j], 16)

            loads(0, 0, 0)
            for loop, store in enumerate((store_y, store_qkv, store_gates)):
                with sp.Fori(0, KC - 1) as i:
                    loads(loop, i, 1)
                    store(i)
                if loop < 2:
                    loads(loop + 1, 0, 0)
                else:
                    w.load(sp, 0, 3, NBLK, cols(COL_AB, 0))
                store(KC - 1)
            for k in range(3):
                sp.wait_ge(stored[k], 16 * (1 + (3 if k == 0 else 2) * KC))

        @block.gpsimd
        def _(pool):
            w.credit_raw(pool)
            with pool.Fori(0, NBLK // 3) as i:
                for j in range(3):
                    w.split_lo(pool, i, 3, j)
            w.split_lo(pool, 0, 3, NBLK)

        @block.tensor
        def _(pe):
            w.credit_split(pe)
            nrm.sums(pe)
            pe.wait_ge(nrm.factor, NB)
            for b in range(NB):
                pe.sem_inc(bank_free[b], 1)
            pe.wait_ge(h_ready, KC)

            def project(i, j):
                pe.wait_ge(w.lo_done, i * 3 + (j + 1))
                for b in range(NB):
                    pe.wait_ge(bank_free[b], i * 3 + (j + 1))
                    for k in range(KC):
                        mm = three_passes(pe, bank[b][:, 0:TH], w.hi[:, j % 3, k, :], w.lo[:, j % 3, k, :],
                                          h_hi[:, k, third(b)], h_lo[:, k, third(b)], k == 0, k == KC - 1)
                    mm.then_inc(unit_done, 1)
                    if b == 1:
                        pe.wait_ge(unit_done, i * 9 + (3 * j + 1))
                        pe.sem_inc(w.split_free, 1)

            with pe.Fori(0, NBLK // 3) as i:
                for j in range(3):
                    project(i, j)
            project(0, NBLK)

        @block.scalar
        def _(act):
            w.split_hi(act, 0, 3, 0)
            nrm.squares(act)
            for k in range(KC):
                act.wait_ge(h_scaled, k + 1)
                act.copy(h_hi[:, k, :], out[:, k % 2, :]).then_inc(h_hi_done, 1)
            act.wait_ge(h_ready, KC)

            def unit(i, n, b):
                act.wait_ge(unit_done, i * 9 + (3 * n + b + 1))
                return bank[b][:, 0:TH]

            with act.Fori(0, KC) as i:
                for j in range(2):
                    w.split_hi(act, i, 3, j + 1)
                    if j == 0:
                        act.wait_ge(y_ready, i + 1)
                    for b in range(NB):
                        src = unit(i, j, b)
                        act.copy(conv[:, 1 + j, third(b)], src).then_inc(bank_free[b], 1)
                w.split_hi(act, i, 3, 3)
            act.wait_ge(y_ready, KC + 1)

            with act.Fori(0, H) as i:
                def silu(j):
                    act.wait_ge(conv_done, i * 3 + (j + 1 + 3))
                    act.wait_ge(stored[j], i * 16 + (16 + (16 * KC if j == 0 else 0)))
                    act.activation(out[:, j, 0:PT], conv[:, j, 0:PT], ACT.Silu)
                    act.activation(out[:, j, PT:T].rearrange("p (s l) -> p s l", l=LS),
                                   conv[:, j, GP + PT:GL].rearrange("p (s l) -> p s l", l=GP + LS)[:, :, 0:LS],
                                   ACT.Silu).then_inc(silu_done, 1)

                for j in range(3):
                    n = 24 + j
                    w.split_hi(act, i, 3, n + 1)
                    act.wait_ge(conv_done, i * 3 + (j + 1))
                    for b in range(NB):
                        src = unit(i, n, b)
                        if b < 2:
                            act.copy(pre[:, j, GP + b * TH:GP + (b + 1) * TH], src).then_inc(bank_free[b], 1)
                        else:
                            act.copy(pre[:, j, GP + 2 * TH:GP + PT], src[:, 0:PT - 2 * TH])
                            act.copy(pre[:, j, GP + PT:GL].rearrange("p (s l) -> p s l", l=GP + LS)[:, :, GP:],
                                     src[:, PT - 2 * TH:TH].rearrange("p (s l) -> p s l", l=LS)).then_inc(bank_free[b], 1)
                    if j:
                        silu(j - 1)
                silu(2)

            with act.Fori(0, KC) as i:
                for j in range(3):
                    n = 48 + j
                    w.split_hi(act, i, 3, n + 1)
                    if j:
                        act.wait_ge(stored[j], i * 16 + 16 * (1 + KC))
                    for b in range(NB):
                        src = unit(i, n, b)
                        if j == 0:
                            act.wait_ge(z_ready, i * 3 + (b + 1))
                            act.activation(conv[:, 0, third(b)], src, ACT.Sigmoid).then_inc(zsig_done, 1)
                        else:
                            act.activation(out[:, j, third(b)], src, ACT.Sigmoid).then_inc(bank_free[b], 1)
            for b in range(NB):
                src = unit(0, NBLK, b)
                act.copy(ab_rows[:, third(b)], src[0:2 * H, :]).then_inc(bank_free[b], 1)

        @block.vector
        def _(dve):
            dve.memset(pre[:, :, 0:GP], 0.0).then_inc(pads_zero, 1)
            dve.sem_inc(conv_done, 3)
            dve.sem_inc(silu_done, 3)
            dve.sem_inc(z_ready, 3)
            dve.sem_inc(y_ready, 1)
            nrm.factors(dve)
            for k in range(KC):
                if k >= 2:
                    dve.wait_ge(h_ready, k - 1)
                dve.scalar_tensor_tensor(out[:, k % 2, :], x[:, k, :], gains[:, 1, k:k + 1], nrm.rstd[:, :],
                                         ALU.mult, ALU.mult).then_inc(h_scaled, 1)
                dve.wait_ge(h_hi_done, k + 1)
                dve.tensor_tensor(h_lo[:, k, :], out[:, k % 2, :], h_hi[:, k, :].bitcast(F32),
                                  ALU.subtract).then_inc(h_ready, 1)
            dve.wait_ge(pads_zero, 1)

            cx = pre[:, 0, GP - SPD:GP - SPD + SL]
            cx_sample = cx[:, SPD + PT:SL].rearrange("p (s l) -> p s l", l=SPD + LS)
            with dve.Fori(0, KC) as i:
                ch = Chain(vec, 0, i, 6)
                dve.tensor_copy(cx_sample[:, :, 0:SPD],
                                sc_hist[:, bass.ds(i, 1), :].rearrange("p o (s t) -> p (o s) t", t=SPD))
                ch.link(dve, dve.tensor_copy(sc_w[:, :], sc_taps[:, bass.ds(i, 1), :].rearrange("p o t -> p (o t)")))
                for b in range(NB):
                    dve.wait_ge(unit_done, i * 9 + (6 + b + 1))
                    dve.wait_ge(bank_free[b], i * 3 + 3)
                    if b < 2:
                        dve.tensor_tensor(cx[:, SPD + b * TH:SPD + (b + 1) * TH], bank[b][:, 0:TH],
                                          conv[:, 2, third(b)], ALU.mult).then_inc(bank_free[b], 1)
                    else:
                        dve.tensor_tensor(cx[:, SPD + 2 * TH:SPD + PT], bank[b][:, 0:PT - 2 * TH],
                                          conv[:, 2, 2 * TH:PT], ALU.mult)
                        dve.tensor_tensor(cx_sample[:, :, SPD:], bank[b][:, PT - 2 * TH:TH].rearrange("p (s l) -> p s l", l=LS),
                                          conv[:, 2, PT:T].rearrange("p (s l) -> p s l", l=LS),
                                          ALU.mult).then_inc(bank_free[b], 1)
                dve.wait_ge(bank_free[2], i * 3 + 4)
                W = SL - SPD
                ch.link(dve, dve.tensor_scalar(conv[:, 0, 0:W], cx[:, 0:W], sc_w[:, 0:1], None, ALU.mult))
                for t in range(1, SC_T):
                    ch.link(dve, dve.scalar_tensor_tensor(conv[:, 0, 0:W], cx[:, t:t + W], sc_w[:, t:t + 1],
                                                          conv[:, 0, 0:W], ALU.mult, ALU.add))
                dve.tensor_copy(sc_tail[:, bass.ds(i, 1), 0:SPD].rearrange("p o t -> p (o t)"), cx[:, PT:PT + SPD])
                ch.link(dve, dve.tensor_copy(sc_tail[:, bass.ds(i, 1), SPD:].rearrange("p o (s t) -> p (o s) t", t=SPD),
                                             cx_sample[:, :, LS:]))
                dve.wait_ge(stored[0], i * 16 + 16)
                ch.link(dve, dve.tensor_tensor(out[:, 0, 0:PT], conv[:, 0, 0:PT], conv[:, 1, 0:PT], ALU.mult))
                dve.tensor_tensor(out[:, 0, PT:T].rearrange("p (s l) -> p s l", l=LS),
                                  conv[:, 0, SPD + PT:SL].rearrange("p (s l) -> p s l", l=SPD + LS)[:, :, 0:LS],
                                  conv[:, 1, PT:T].rearrange("p (s l) -> p s l", l=LS), ALU.mult).then_inc(y_ready, 1)
                ch.end()
            base = ch.per * KC

            with dve.Fori(0, H) as i:
                ch = Chain(vec, base, i, 1 + 3 * GC_T)
                ch.link(dve, dve.tensor_copy(gc_w[:, :, :], gc_taps.rearrange("p (j h) t -> p j h t", h=H)[:, :, bass.ds(i, 1), :]
                                             .rearrange("p j o t -> p j (o t)")))
                for j in range(3):
                    row = pre[:, j, :]
                    row_sample = pre[:, j, GP + PT:GL].rearrange("p (s l) -> p s l", l=GP + LS)
                    dve.wait_ge(conv_done, i * 3 + (j + 3))
                    dve.tensor_copy(row_sample[:, :, 0:GP],
                                    gc_hist[:, bass.ds(i + j * H, 1), :].rearrange("p o (s t) -> p (o s) t", t=GP)).then_inc(pads_zero, 1)
                    dve.wait_ge(pads_zero, i * 3 + (j + 2))
                    dve.wait_ge(bank_free[2], i * 3 + (24 + j + 2))
                    dve.wait_ge(silu_done, i * 3 + (j + 1))
                    W = GL - GP
                    ch.link(dve, dve.tensor_scalar(conv[:, j, 0:W], row[:, 0:W], gc_w[:, j, 0:1], None, ALU.mult))
                    for t in range(1, GC_T):
                        ch.link(dve, dve.scalar_tensor_tensor(conv[:, j, 0:W], row[:, t:t + W], gc_w[:, j, t:t + 1],
                                                              conv[:, j, 0:W], ALU.mult, ALU.add))
                    tail = gc_tail[:, bass.ds(i + j * H, 1), :]
                    dve.tensor_copy(tail[:, :, 0:GP].rearrange("p o t -> p (o t)"), row[:, PT:PT + GP])
                    dve.tensor_copy(tail[:, :, GP:].rearrange("p o (s t) -> p (o s) t", t=GP),
                                    row_sample[:, :, LS:]).then_inc(conv_done, 1)
                ch.end()

            with dve.Fori(0, KC) as i:
                for b in range(NB):
                    dve.wait_ge(zsig_done, i * 3 + (b + 1))
                    if b == 0:
                        dve.wait_ge(stored[0], i * 16 + 16 * (1 + 2 * KC))
                    dve.tensor_tensor(out[:, 0, third(b)], bank[b][:, 0:TH], conv[:, 0, third(b)],
                                      ALU.mult).then_inc(z_ready, 1)
                    dve.wait_ge(z_ready, i * 3 + (b + 1 + 3))
                    dve.sem_inc(bank_free[b], 1)


class Units:

    def __init__(self, s, label, order, banks):
        self.order = order
        self.banks = banks
        self.at = {name: k for k, (name, _) in enumerate(order)}
        self.per = len(order)
        self.bank_per = [sum(b == k for _, b in order) for k in range(len(banks))]
        self.use = {name: sum(b == bank for _, b in order[:k]) for k, (name, bank) in enumerate(order)}
        self.done = s.sem(f"{label}_done")
        self.free = [s.sem(f"{label}_bank{k}_free") for k in range(len(banks))]

    def ps(self, name):
        return self.banks[self.order[self.at[name]][1]]

    def sem(self, name):
        return self.free[self.order[self.at[name]][1]]

    def wait_bank(self, pe, h, name):
        b = self.order[self.at[name]][1]
        pe.wait_ge(self.free[b], h * self.bank_per[b] + (self.use[name] + 1))

    def wait_done(self, eng, h, name):
        eng.wait_ge(self.done, h * self.per + (self.at[name] + 1))

    def wait_read(self, eng, h, name):
        b = self.order[self.at[name]][1]
        eng.wait_ge(self.free[b], h * self.bank_per[b] + (self.use[name] + 2))


CONST_COLS = {}
_at = 0
for _name, _width in (("upto", P), ("upto_tail", TAIL), ("after", P), ("after_tail", TAIL), ("level", LEVELS * P),
                      ("segment", NSEG)):
    CONST_COLS[_name] = (_at, _width)
    _at += _width
CONST_W = _at


def delta_constants():
    t = np.zeros((P, CONST_W), np.float32)
    m, i = np.arange(P)[:, None], np.arange(P)[None, :]
    seg = np.where(np.arange(TAIL) < PT_TAIL, 0, 1 + (np.arange(TAIL) - PT_TAIL) // LS)
    same = seg[:, None] == seg[None, :]
    mt, it = m[:TAIL], i[:, :TAIL]

    def put(name, a):
        t[:a.shape[0], CONST_COLS[name][0]:CONST_COLS[name][0] + a.shape[1]] = a

    put("upto", m <= i)
    put("upto_tail", (mt <= it) & same)
    put("after", m > i)
    put("after_tail", (mt > it) & same)
    put("level", np.concatenate([(m >> (k + 1) == i >> (k + 1)) & (m >> k & 1 == 0) & (i >> k & 1 == 1)
                                 for k in range(LEVELS)], 1))
    put("segment", seg[:, None] == np.arange(NSEG)[None, :])
    return t


GROUPS_OF_TILES = ((0, 4), (4, 4), (8, 1))


def delta_rule(nc, ones, ident, eps_col, consts_in, head_params, g_norm, ab_rows, state_in, scratch, prompt_state,
               sample_state):
    with ExitStack() as ctx:
        s = Scope(nc, ctx, "dr")
        con = s.sb("con", [P, CONST_W])
        hp = s.sb("head_params", [2 * H, 2])
        gn = s.sb("g_norm", [P, 1])

        def const(name, n=P):
            a, width = CONST_COLS[name]
            return con[0:n, a:a + width]

        level = const("level").rearrange("p (k i) -> p k i", i=P)
        per_token = s.sb("per_token", [P, 4, NT + 1, H])
        na = s.sb("neg_rate", [2 * H, 1])
        tok = [s.sb(f"tok{p}", [P, 4, NT + 1]) for p in range(2)]
        q = s.sb("q", [P, T])
        k_t = [s.sb(f"k{p}", [P, T]) for p in range(2)]
        v = [s.sb(f"v{p}", [P, T]) for p in range(2)]
        z = s.sb("z", [P, T])
        sq = s.sb("sq", [P, 2, T])
        lu = s.sb("lu", [P, T])
        dec = s.sb("dec", [P, T])
        bdec = s.sb("bdec", [P, T])
        raw = [buf[0:2 * H, :] for buf in (sq[:, 0, :], sq[:, 1, :], lu, dec)]
        bmat = s.sb("bmat", [P, T])
        bk = s.sb("bk", [P, 2, T])
        w_inv = s.sb("w_inv", [P, T])
        y_lev = s.sb("y_lev", [P, T])
        x_inv = [s.sb(f"x_inv{p}", [P, T]) for p in range(2)]
        eg = [s.sb(f"eg{p}", [P, T]) for p in range(2)]
        qd = [s.sb(f"qd{p}", [P, T]) for p in range(2)]
        aqk = [s.sb(f"aqk{p}", [P, T]) for p in range(2)]
        kdec = [s.sb(f"kdec{p}", [P, (NT + 1), P]) for p in range(2)]
        v_tok = [s.sb(f"v_tok{p}", [P, NT, P]) for p in range(2)]
        st = [s.sb(f"st{p}", [P, NSEG, P]) for p in range(2)]
        st_out = s.sb("st_out", [P, NSEG, P])
        resid = s.sb("resid", [P, P])
        resid_t = s.sb("resid_t", [P, TAIL])
        nu = s.sb("nu", [P, P])
        nu_seg = s.sb("nu_seg", [TAIL, NSEG, P])
        o = s.sb("o", [P, T])
        o_sq = s.sb("o_sq", [P, T])

        a_names = ([f"sq{b}" for b in range(3)] + [f"sk{b}" for b in range(3)] + [f"dec{g}" for g in range(3)]
                   + [f"eg{g}" for g in range(3)] + [f"kk{g}" for g in range(3)] + [f"qk{g}" for g in range(3)]
                   + [f"kt{g}" for g in range(3)] + [f"vt{g}" for g in range(2)] + [f"T0{g}" for g in range(3)])
        for k in range(1, LEVELS):
            gs = range(3 if k < TAIL_LEVELS else 2)
            a_names += [f"Y{k}{g}" for g in gs]
            for g in gs:
                a_names += [f"X{k}{g}"] + ([f"T{k}{g}"] if k < LEVELS - 1 else [])
        A = Units(s, "a", [(n, k % 5) for k, n in enumerate(a_names)], [s.ps(f"a_bank{k}", [P, 512]) for k in range(5)])
        b_order = []
        for t in range(NT):
            b_order += [(f"ks{t}", 0), (f"nu{t}", 0), (f"ds{t}", 0), (f"o{t}", 1 + t % 2)]
        b_order += [("ks8", 0), ("r8", 0), ("nu8", 0), ("o8", 1), ("ds8_0", 0), ("ds8_1", 2), ("ds8_2", 0),
                    ("on0", 1), ("on1", 2), ("on2", 0)]
        B = Units(s, "b", b_order, [s.ps(f"b_bank{k}", [P, 512]) for k in range(3)])

        cons_loaded, prep = s.sem("cons_loaded"), s.sem("prep")
        prep_act, prep_pe = s.sem("prep_act"), s.sem("prep_pe")
        qk_loaded, v_loaded, z_loaded, st_loaded = s.sem("qk_loaded"), s.sem("v_loaded"), s.sem("z_loaded"), s.sem("st_loaded")
        a_inputs_used, b_inputs_used = s.sem("a_inputs_used"), s.sem("b_inputs_used")
        sq_ready, lu_ready, rooted = s.sem("sq_ready"), s.sem("lu_ready"), s.sem("rooted")
        qk_ready, dec_masked, bdec_ready, qd_ready = s.sem("qk_ready"), s.sem("dec_masked"), s.sem("bdec_ready"), s.sem("qd_ready")
        bk_ready, tok_ready, b_ready = s.sem("bk_ready"), s.sem("tok_ready"), s.sem("b_ready")
        st_zeroed, nu_seg_ready, st_scaled = s.sem("st_zeroed"), s.sem("nu_seg_ready"), s.sem("st_scaled")
        o_sq_ready, o_rooted, y_ready = s.sem("o_sq_ready"), s.sem("o_rooted"), s.sem("y_ready")
        y_stored, st_stored = s.sem("y_stored"), s.sem("st_stored")
        vec, vec_b = s.sem("vec"), s.sem("vec_b")
        block = s.block()

        def tile(t):
            return slice(t * P, min(t * P + P, T))

        def rows(t):
            return P if t < NT else TAIL

        def span(buf, g):
            t0, n = GROUPS_OF_TILES[g]
            return buf[0:rows(t0), t0 * P:min((t0 + n) * P, T)]

        def full(buf):
            return buf[:, 0:NT * P].rearrange("p (t i) -> p t i", i=P)

        def tail(buf):
            return buf[0:TAIL, NT * P:T]

        def psum(units, name, g):
            t0, n = GROUPS_OF_TILES[g]
            return units.ps(name)[0:rows(t0), 0:(n * P if t0 < NT else TAIL)]

        def over_tiles(a, n=NT):
            return a.unsqueeze(1).broadcast_to([P, n, P])

        def per_row(a, width=P):
            return a.unsqueeze(2).broadcast_to([a.shape[0], a.shape[1], width])

        @block.sync
        def _(sp):
            sp.dma_start(con[:, :], consts_in).then_inc(cons_loaded, 16)
            sp.dma_start(hp[:, :], head_params).then_inc(cons_loaded, 16)
            sp.dma_start(gn[:, :], g_norm).then_inc(cons_loaded, 16)

            def head(i, par, last=False):
                h = i * 2 + par
                for j, buf in ((0, q), (1, k_t[par]), (2, v[par])):
                    if j == 0:
                        sp.wait_ge(a_inputs_used, h + 1)
                    sp.dma_start(buf[:, :], scratch["qkv"][j][bass.ds(h, 1)].rearrange("c p t -> p (c t)")) \
                        .then_inc(v_loaded if j == 2 else qk_loaded, 16)
                sp.wait_ge(b_inputs_used, h + 1)
                sp.dma_start(z[:, :], scratch["z"][bass.ds(h, 1)].rearrange("c p t -> p (c t)")).then_inc(z_loaded, 16)
                sp.dma_start(st[par][:, 1:NSEG, :], state_in[0][:, bass.ds(h, 1)].rearrange("s o k v -> k (s o) v")).then_inc(st_loaded, 16)

            def store(i, par):
                h = i * 2 + par
                sp.wait_ge(y_ready, h + 1)
                sp.dma_start(scratch["y_b"][bass.ds(h, 1)].rearrange("c p t -> p (c t)"), o[:, :]).then_inc(y_stored, 16)
                sp.dma_start(prompt_state[0, 0, bass.ds(h, 1)].rearrange("o k v -> k (o v)"), st_out[:, 0, :]).then_inc(st_stored, 16)
                sp.dma_start(sample_state[0][:, bass.ds(h, 1)].rearrange("s o k v -> k (s o) v"), st_out[:, 1:NSEG, :]).then_inc(st_stored, 16)

            sp.sem_inc(y_stored, 16)
            sp.sem_inc(st_stored, 32)
            with sp.Fori(0, H // 2) as i:
                for par in range(2):
                    head(i, par)
                    store(i, par)
            sp.wait_ge(y_stored, 16 * (1 + H))
            sp.wait_ge(st_stored, 32 * (1 + H))

        def heads(eng, stage_a, stage_b):
            with eng.Fori(0, H // 2) as i:
                for par in range(2):
                    stage_a(i, par, i * 2 + par)
                    stage_b(i, par, i * 2 + par)

        @block.gpsimd
        def _(pool):
            def stage_a(i, par, h):
                pool.wait_ge(qk_loaded, h * 32 + 32)
                pool.wait_ge(rooted, h * 6 + 6)
                pool.tensor_tensor(sq[:, 0, :], q[:, :], q[:, :], ALU.mult).then_inc(sq_ready, 1)
                pool.tensor_tensor(sq[:, 1, :], k_t[par][:, :], k_t[par][:, :], ALU.mult).then_inc(sq_ready, 1)
                pool.wait_ge(tok_ready, h + 1)
                pool.tensor_tensor(full(lu), over_tiles(const("upto")), per_row(tok[par][:, 0, 0:NT]), ALU.mult)
                pool.tensor_tensor(tail(lu), const("upto_tail", TAIL), tok[par][0:TAIL, 0, NT:NT + 1].broadcast_to([TAIL, TAIL]),
                                   ALU.mult).then_inc(lu_ready, 1)
                for g in range(3):
                    A.wait_read(pool, h, f"dec{g}")
                pool.tensor_tensor(full(dec), full(dec), over_tiles(const("upto")), ALU.mult)
                pool.tensor_tensor(tail(dec), tail(dec), const("upto_tail", TAIL), ALU.mult).then_inc(dec_masked, 1)
                pool.wait_ge(dec_masked, h + 1)
                pool.tensor_tensor(full(bdec), full(dec), per_row(tok[par][:, 1, 0:NT]), ALU.mult)
                pool.tensor_tensor(tail(bdec), tail(dec), tok[par][0:TAIL, 1, NT:NT + 1].broadcast_to([TAIL, TAIL]),
                                   ALU.mult).then_inc(bdec_ready, 1)
                for g in range(3):
                    A.wait_read(pool, h, f"eg{g}")
                pool.wait_ge(qk_ready, h + 1)
                pool.tensor_tensor(qd[par][:, :], q[:, :], eg[par][:, :], ALU.mult).then_inc(qd_ready, 1)
                for g in range(3):
                    A.wait_read(pool, h, f"kk{g}")
                for k in range(LEVELS):
                    if k == 2:
                        A.wait_read(pool, h, "T02")
                    elif k > 2:
                        A.wait_done(pool, h, f"Y{k - 2}{2 if k - 2 < TAIL_LEVELS else 1}")
                    if k < TAIL_LEVELS:
                        pool.tensor_tensor(tail(bk[:, k % 2, :]), tail(bmat), level[0:TAIL, k, 0:TAIL], ALU.mult)
                    pool.tensor_tensor(full(bk[:, k % 2, :]), full(bmat), over_tiles(level[:, k, :]), ALU.mult).then_inc(bk_ready, 1)

            def stage_b(i, par, h):
                B.wait_read(pool, h, "o7")
                B.wait_read(pool, h, "o8")
                pool.tensor_tensor(o_sq[:, :], o[:, :], o[:, :], ALU.mult).then_inc(o_sq_ready, 1)

            heads(pool, stage_a, stage_b)

        @block.tensor
        def _(pe):
            ps = A.banks
            pe.wait_ge(prep, 1)
            for t in range(NT + 1):
                for r in range(2):
                    mm = pe.transpose(ps[0][0:rows(t), (2 * t + r) * 2 * H:(2 * t + r + 1) * 2 * H],
                                      raw[1 + r][:, tile(t)], ident[0:2 * H, 0:2 * H])
            mm.then_inc(prep_pe, 1)
            pe.wait_ge(prep, 2)
            pe.wait_ge(cons_loaded, 48)
            for r, name in ((1, "upto"), (2, "after")):
                pe.matmul(ps[r][:, 0:NT * H], const(name), per_token[:, 0, 0:NT, :].rearrange("p t h -> p (t h)"),
                          start=True, stop=True)
                mm = pe.matmul(ps[r][0:TAIL, NT * H:(NT + 1) * H], const(name + "_tail", TAIL),
                               per_token[0:TAIL, 0, NT, :], start=True, stop=True)
            mm.then_inc(prep_pe, 1)
            pe.wait_ge(prep_act, 5)
            for f in [*A.free, *B.free]:
                pe.sem_inc(f, 1)

            def stage_a(i, par, h):
                kn, xi = k_t[par], x_inv[par]

                def norm_sums(which, r):
                    pe.wait_ge(sq_ready, h * 2 + (r + 1))
                    for b in range(NB):
                        A.wait_bank(pe, h, f"{which}{b}")
                        pe.matmul(A.ps(f"{which}{b}")[:, 0:TH], ones, sq[:, r, third(b)], start=True,
                                  stop=True).then_inc(A.done, 1)

                norm_sums("sq", 0)
                norm_sums("sk", 1)
                pe.wait_ge(lu_ready, h + 1)
                for name, full_w, tail_w in (("dec", const("after"), const("after_tail", TAIL)), ("eg", ones, ones[0:TAIL, :])):
                    for g in range(3):
                        A.wait_bank(pe, h, f"{name}{g}")
                        n = P if g < 2 or name == "eg" else TAIL
                        cols = span(lu, g).shape[1]
                        pe.matmul(A.ps(f"{name}{g}")[0:n, 0:cols], full_w if g < 2 else tail_w, span(lu, g),
                                  start=True, stop=True).then_inc(A.done, 1)
                pe.wait_ge(qk_ready, h + 1)

                def per_tile(name, g, product):
                    A.wait_bank(pe, h, f"{name}{g}")
                    t0, n = GROUPS_OF_TILES[g]
                    for t in range(t0, t0 + n):
                        r = rows(t)
                        mm = product(A.ps(f"{name}{g}")[0:r, (t - t0) * P:(t - t0) * P + r], t)
                    mm.then_inc(A.done, 1)

                for g in range(3):
                    per_tile("kk", g, lambda out, t: pe.matmul(out, kn[:, tile(t)], kn[:, tile(t)], start=True, stop=True))
                for g in range(3):
                    per_tile("qk", g, lambda out, t: pe.matmul(out, kn[:, tile(t)], q[:, tile(t)], start=True, stop=True))
                for name, src, gs in (("kt", kn, 3), ("vt", v[par], 2)):
                    if name == "vt":
                        pe.wait_ge(v_loaded, h * 16 + 16)
                    for g in range(gs):
                        A.wait_bank(pe, h, f"{name}{g}")
                        t0, n = GROUPS_OF_TILES[g]
                        for t in range(t0, t0 + n):
                            mm = pe.transpose(A.ps(f"{name}{g}")[0:rows(t), (t - t0) * P:(t - t0 + 1) * P],
                                              src[:, tile(t)], ident[:, :])
                        mm.then_inc(A.done, 1)
                pe.wait_ge(bk_ready, h * LEVELS + 1)
                b0 = bk[:, 0, :]
                for g in range(3):
                    per_tile("T0", g, lambda out, t: pe.transpose(out, b0[0:rows(t), tile(t)], ident[0:rows(t), 0:rows(t)]))
                for k in range(1, LEVELS):
                    gs = range(3 if k < TAIL_LEVELS else 2)
                    pe.wait_ge(bk_ready, h * LEVELS + (k + 1))
                    cur = bk[:, k % 2, :]
                    for g in gs:
                        A.wait_read(pe, h, f"T{k - 1}{g}")
                        per_tile(f"Y{k}", g, lambda out, t: pe.matmul(out, cur[0:rows(t), tile(t)], w_inv[0:rows(t), tile(t)],
                                                                     start=True, stop=True))
                    for g in gs:
                        A.wait_read(pe, h, f"Y{k}{g}")
                        per_tile(f"X{k}", g, lambda out, t: pe.matmul(out, y_lev[0:rows(t), tile(t)], xi[0:rows(t), tile(t)],
                                                                     start=True, stop=True))
                        if k < LEVELS - 1:
                            per_tile(f"T{k}", g, lambda out, t: pe.matmul(out, xi[0:rows(t), tile(t)], y_lev[0:rows(t), tile(t)],
                                                                         start=True, stop=True))

            def stage_b(i, par, h):
                kn, xi, state, qdp, aq, kd = k_t[par], x_inv[par], st[par], qd[par], aqk[par], kdec[par]
                pe.wait_ge(st_zeroed, h + 1)
                pe.wait_ge(qd_ready, h + 1)
                A.wait_read(pe, h, f"X{LEVELS - 1}0")
                A.wait_read(pe, h, f"X{LEVELS - 1}1")
                for t in range(NT):
                    if t:
                        B.wait_read(pe, h, f"ds{t - 1}")
                    B.wait_bank(pe, h, f"ks{t}")
                    pe.matmul(B.ps(f"ks{t}")[:, 0:P], kn[:, tile(t)], state[:, 0, :], start=True, stop=True).then_inc(B.done, 1)
                    B.wait_bank(pe, h, f"o{t}")
                    pe.matmul(B.ps(f"o{t}")[:, 0:P], state[:, 0, :], qdp[:, tile(t)], start=True, stop=False)
                    B.wait_read(pe, h, f"ks{t}")
                    pe.matmul(B.ps(f"nu{t}")[:, P:2 * P], xi[:, tile(t)], resid[:, :], start=True, stop=True).then_inc(B.done, 1)
                    B.wait_read(pe, h, f"nu{t}")
                    pe.matmul(B.ps(f"ds{t}")[:, 2 * P:3 * P], kd[:, t, :], nu[:, :], start=True, stop=True).then_inc(B.done, 1)
                    pe.matmul(B.ps(f"o{t}")[:, 0:P], nu[:, :], aq[:, tile(t)], start=False, stop=True).then_inc(B.done, 1)
                pe.wait_ge(st_loaded, h * 16 + 16)
                B.wait_read(pe, h, f"ds{NT - 1}")
                seqs = [(0, 0, PT_TAIL)] + [(1 + r, PT_TAIL + r * LS, LS) for r in range(NS)]
                B.wait_bank(pe, h, "ks8")
                for r, c, n in seqs:
                    mm = pe.matmul(B.ps("ks8")[:, c:c + n], state[:, r, :], kn[:, NT * P + c:NT * P + c + n], start=True, stop=True)
                mm.then_inc(B.done, 1)
                B.wait_bank(pe, h, "o8")
                for r, c, n in seqs:
                    pe.matmul(B.ps("o8")[:, c:c + n], state[:, r, :], qdp[:, NT * P + c:NT * P + c + n], start=(r == 0), stop=False,
                              skip_group_check=True)
                B.wait_read(pe, h, "ks8")
                pe.transpose(B.ps("r8")[0:TAIL, P:2 * P], resid_t[:, :], ident[:, :]).then_inc(B.done, 1)
                B.wait_read(pe, h, "r8")
                pe.matmul(B.ps("nu8")[0:TAIL, 2 * P:3 * P], xi[0:TAIL, tile(NT)], resid[0:TAIL, :], start=True, stop=True).then_inc(B.done, 1)
                B.wait_read(pe, h, "nu8")
                pe.matmul(B.ps("o8")[:, 0:TAIL], nu[0:TAIL, :], aq[0:TAIL, tile(NT)], start=False, stop=True,
                          skip_group_check=True).then_inc(B.done, 1)
                pe.wait_ge(nu_seg_ready, h + 1)
                for u in range(3):
                    B.wait_bank(pe, h, f"ds8_{u}")
                    pe.matmul(B.ps(f"ds8_{u}")[:, 0:3 * P], kd[0:TAIL, NT, :], nu_seg[:, 3 * u:3 * u + 3, :].rearrange("p a b -> p (a b)"),
                              start=True, stop=True).then_inc(B.done, 1)
                pe.wait_ge(o_sq_ready, h + 1)
                for b in range(NB):
                    B.wait_bank(pe, h, f"on{b}")
                    pe.matmul(B.ps(f"on{b}")[:, 0:TH], ones, o_sq[:, third(b)], start=True, stop=True).then_inc(B.done, 1)

            heads(pe, stage_a, stage_b)

        @block.scalar
        def _(act):
            act.wait_ge(cons_loaded, 48)
            act.activation(na[:, :], hp[:, 1:2], ACT.Exp).then_inc(prep_act, 1)
            act.activation(raw[2], ab_rows[:, :], ACT.Exp, scale=-1.0).then_inc(prep_act, 1)
            act.wait_ge(vec, 2)
            act.activation(raw[3], raw[3], ACT.Exp, scale=-1.0).then_inc(prep_act, 1)
            act.wait_ge(prep_act, 3)
            act.activation(raw[3], raw[3], ACT.Ln, bias=ones[0:2 * H, 0:1]).then_inc(prep_act, 1)
            act.wait_ge(prep_pe, 2)
            for r in (1, 2):
                act.activation(per_token[:, 1 + r, 0:NT, :], A.banks[r][:, 0:NT * H].rearrange("p (t h) -> p t h", h=H), ACT.Exp)
                ins = act.activation(per_token[0:TAIL, 1 + r, NT, :], A.banks[r][0:TAIL, NT * H:(NT + 1) * H], ACT.Exp)
            ins.then_inc(prep_act, 1)

            def stage_a(i, par, h):
                for r, which in enumerate(("sq", "sk")):
                    A.wait_done(act, h, f"{which}2")
                    for b in range(NB):
                        act.activation(sq[:, r, third(b)], A.ps(f"{which}{b}")[:, 0:TH], ACT.Sqrt,
                                       bias=eps_col).then_inc(A.sem(f"{which}{b}"), 1)
                for g in range(3):
                    A.wait_done(act, h, f"dec{g}")
                    act.activation(span(dec, g), psum(A, f"dec{g}", g), ACT.Exp).then_inc(A.sem(f"dec{g}"), 1)
                for g in range(3):
                    A.wait_done(act, h, f"eg{g}")
                    t0, n = GROUPS_OF_TILES[g]
                    c = slice(t0 * P, min((t0 + n) * P, T))
                    act.activation(eg[par][:, c], A.ps(f"eg{g}")[:, 0:c.stop - c.start], ACT.Exp).then_inc(A.sem(f"eg{g}"), 1)
                for g in range(2):
                    A.wait_done(act, h, f"vt{g}")
                    act.copy(v_tok[par][:, 4 * g:4 * g + 4, :], A.ps(f"vt{g}").rearrange("p (t d) -> p t d", d=P)) \
                        .then_inc(A.sem(f"vt{g}"), 1)
                for k in range(1, LEVELS):
                    for g in range(3 if k < TAIL_LEVELS else 2):
                        A.wait_done(act, h, f"Y{k}{g}")
                        act.copy(span(y_lev, g), psum(A, f"Y{k}{g}", g)).then_inc(A.sem(f"Y{k}{g}"), 1)

            def stage_b(i, par, h):
                act.wait_ge(y_stored, h * 16 + 16)
                for t in range(NT):
                    B.wait_done(act, h, f"o{t}")
                    act.copy(o[:, tile(t)], B.ps(f"o{t}")[:, 0:P]).then_inc(B.sem(f"o{t}"), 1)
                B.wait_done(act, h, "r8")
                act.copy(resid[0:TAIL, :], B.ps("r8")[0:TAIL, P:2 * P]).then_inc(B.sem("r8"), 1)
                B.wait_done(act, h, "o8")
                act.copy(o[:, tile(NT)], B.ps("o8")[:, 0:TAIL]).then_inc(B.sem("o8"), 1)
                B.wait_done(act, h, "on2")
                for b in range(NB):
                    act.activation(o_sq[:, third(b)], B.ps(f"on{b}")[:, 0:TH], ACT.Sqrt, bias=eps_col,
                                   scale=1.0 / P).then_inc(B.sem(f"on{b}"), 1)

            heads(act, stage_a, stage_b)

        @block.vector
        def _(dve):
            ch = Chain(vec)
            dve.sem_inc(a_inputs_used, 1)
            dve.sem_inc(b_inputs_used, 1)
            dve.wait_ge(cons_loaded, 48)
            ch.link(dve, dve.tensor_scalar(raw[0], ab_rows[:, :], hp[:, 0:1], None, ALU.add))
            ch.link(dve, dve.scalar_tensor_tensor(raw[3], raw[0], -1.0, raw[0], ALU.mult, ALU.max))
            ch.link(dve, dve.memset(per_token[:, :, :, :], 0.0))
            dve.wait_ge(prep_act, 1)
            ch.link(dve, dve.tensor_scalar(na[:, :], na[:, :], -1.0, None, ALU.mult))
            dve.wait_ge(prep_act, 4)
            ch.link(dve, dve.scalar_tensor_tensor(raw[1], raw[0], 0.0, raw[3], ALU.max, ALU.add))
            ch.link(dve, dve.tensor_scalar(raw[1], raw[1], na[:, 0:1], None, ALU.mult))
            ch.link(dve, dve.tensor_scalar(raw[2], raw[2], 1.0, None, ALU.add))
            dve.reciprocal(raw[2], raw[2]).then_inc(prep, 1)
            dve.wait_ge(prep_pe, 1)
            tr = A.banks[0][:, 0:(NT + 1) * 4 * H].rearrange("p (t r h) -> p t r h", r=2, h=2 * H)
            for r in range(2):
                cols = slice(r * H, (r + 1) * H)
                dve.tensor_copy(per_token[:, r, 0:NT, :], tr[:, 0:NT, r, cols])
                ins = dve.tensor_copy(per_token[0:TAIL, r, NT, :], tr[0:TAIL, NT, r, cols])
            ins.then_inc(prep, 1)
            dve.wait_ge(prep_act, 5)
            ch.link(dve, dve.tensor_scalar(per_token[:, 2, :, :], per_token[:, 2, :, :], -1.0, None, ALU.mult))
            base = ch.end()
            dve.sem_inc(rooted, 6)

            def per_head(h):
                return [per_token[:, r, :, bass.ds(h, 1)].rearrange("p t o -> p (t o)") for r in range(4)]

            PER_A, PER_B = 4, 5

            def stage_a(i, par, h):
                ca = Chain(vec, base + PER_A * par, i, 2 * PER_A)
                for r, src in enumerate(per_head(h)):
                    ins = dve.tensor_copy(tok[par][:, r, :], src)
                ins.then_inc(tok_ready, 1)
                dve.wait_ge(tok_ready, h + 1)
                for r, which in enumerate(("sq", "sk")):
                    for b in range(NB):
                        A.wait_read(dve, h, f"{which}{b}")
                    ca.link(dve, dve.reciprocal(sq[:, r, :], sq[:, r, :]))
                ca.link(dve, dve.scalar_tensor_tensor(q[:, :], q[:, :], float(P) ** -0.5, sq[:, 0, :], ALU.mult, ALU.mult))
                dve.tensor_tensor(k_t[par][:, :], k_t[par][:, :], sq[:, 1, :], ALU.mult).then_inc(qk_ready, 1)
                dve.wait_ge(qk_ready, h + 1)
                dve.sem_inc(rooted, 6)
                dve.wait_ge(bdec_ready, h + 1)
                for g in range(3):
                    A.wait_done(dve, h, f"kk{g}")
                    dve.tensor_tensor(span(bmat, g), psum(A, f"kk{g}", g), span(bdec, g), ALU.mult).then_inc(A.sem(f"kk{g}"), 1)
                for g in range(3):
                    A.wait_done(dve, h, f"qk{g}")
                    dve.tensor_tensor(span(aqk[par], g), psum(A, f"qk{g}", g), span(dec, g), ALU.mult).then_inc(A.sem(f"qk{g}"), 1)
                for g in range(3):
                    t0, n = GROUPS_OF_TILES[g]
                    r = rows(t0)
                    A.wait_done(dve, h, f"kt{g}")
                    dve.tensor_tensor(kdec[par][0:r, t0:t0 + n, :], A.ps(f"kt{g}")[0:r, 0:n * P].rearrange("p (t d) -> p t d", d=P),
                                      per_row(tok[par][0:r, 3, t0:t0 + n]), ALU.mult).then_inc(A.sem(f"kt{g}"), 1)
                dve.wait_ge(bk_ready, h * LEVELS + 1)
                b0 = bk[:, 0, :]
                dve.tensor_tensor(full(x_inv[par]), over_tiles(ident[:, :]), full(b0), ALU.subtract)
                ca.link(dve, dve.tensor_tensor(tail(x_inv[par]), ident[0:TAIL, 0:TAIL], tail(b0), ALU.subtract))
                for g in range(3):
                    t0, n = GROUPS_OF_TILES[g]
                    eye = over_tiles(ident[:, :], n) if g < 2 else ident[0:TAIL, 0:TAIL]
                    split = (lambda a: a.rearrange("p (t i) -> p t i", i=P)) if g < 2 else (lambda a: a)
                    A.wait_done(dve, h, f"T0{g}")
                    dve.tensor_tensor(split(span(w_inv, g)), eye, split(psum(A, f"T0{g}", g)), ALU.subtract).then_inc(A.sem(f"T0{g}"), 1)
                for k in range(1, LEVELS):
                    for g in range(3 if k < TAIL_LEVELS else 2):
                        A.wait_done(dve, h, f"T{k}{g}" if k < LEVELS - 1 else f"X{k}{g}")
                        dve.tensor_tensor(span(x_inv[par], g), span(x_inv[par], g), psum(A, f"X{k}{g}", g),
                                          ALU.subtract).then_inc(A.sem(f"X{k}{g}"), 1)
                        if k < LEVELS - 1:
                            dve.tensor_tensor(span(w_inv, g), span(w_inv, g), psum(A, f"T{k}{g}", g),
                                              ALU.subtract).then_inc(A.sem(f"T{k}{g}"), 1)
                dve.wait_ge(qd_ready, h + 1)
                dve.sem_inc(a_inputs_used, 1)
                assert ca.n == PER_A, ca.n

            def stage_b(i, par, h):
                cb = Chain(vec_b, PER_B * par, i, 2 * PER_B)
                tk, state = tok[par], st[par]
                dve.memset(state[:, 0, :], 0.0).then_inc(st_zeroed, 1)
                for t in range(NT):
                    B.wait_done(dve, h, f"ks{t}")
                    if t == 0:
                        A.wait_read(dve, h, "vt1")
                    dve.scalar_tensor_tensor(resid[:, :], B.ps(f"ks{t}")[:, 0:P], tk[:, 2, t:t + 1], v_tok[par][:, t, :],
                                             ALU.mult, ALU.add).then_inc(B.sem(f"ks{t}"), 1)
                    B.wait_done(dve, h, f"nu{t}")
                    dve.tensor_scalar(nu[:, :], B.ps(f"nu{t}")[:, P:2 * P], tk[:, 1, t:t + 1], None, ALU.mult).then_inc(B.sem(f"nu{t}"), 1)
                    B.wait_done(dve, h, f"ds{t}")
                    dve.scalar_tensor_tensor(state[:, 0, :], state[:, 0, :], eg[par][:, t * P + P - 1:t * P + P],
                                             B.ps(f"ds{t}")[:, 2 * P:3 * P], ALU.mult, ALU.add).then_inc(B.sem(f"ds{t}"), 1)
                B.wait_done(dve, h, "ks8")
                cb.link(dve, dve.tensor_tensor(resid_t[:, :], B.ps("ks8")[:, 0:TAIL], eg[par][:, NT * P:T], ALU.mult))
                dve.tensor_tensor(resid_t[:, :], v[par][:, NT * P:T], resid_t[:, :], ALU.subtract).then_inc(B.sem("ks8"), 1)
                B.wait_done(dve, h, "nu8")
                dve.tensor_scalar(nu[0:TAIL, :], B.ps("nu8")[0:TAIL, 2 * P:3 * P], tk[0:TAIL, 1, NT:NT + 1], None, ALU.mult) \
                    .then_inc(B.sem("nu8"), 1)
                B.wait_read(dve, h, "nu8")
                dve.tensor_tensor(nu_seg[:, :, :], nu[0:TAIL, :].unsqueeze(1).broadcast_to([TAIL, NSEG, P]),
                                  per_row(const("segment", TAIL)), ALU.mult).then_inc(nu_seg_ready, 1)
                dve.wait_ge(st_stored, h * 32 + 32)
                last = eg[par][:, NT * P + PT_TAIL - 1:T:LS]
                cb.link(dve, dve.tensor_tensor(st_out[:, :, :], state[:, :, :], per_row(last), ALU.mult))
                for u in range(3):
                    B.wait_done(dve, h, f"ds8_{u}")
                    dve.tensor_tensor(st_out[:, 3 * u:3 * u + 3, :], st_out[:, 3 * u:3 * u + 3, :],
                                      B.ps(f"ds8_{u}")[:, 0:3 * P].rearrange("p (a b) -> p a b", b=P), ALU.add).then_inc(B.sem(f"ds8_{u}"), 1)
                for b in range(NB):
                    B.wait_read(dve, h, f"on{b}")
                cb.link(dve, dve.reciprocal(o_sq[:, :], o_sq[:, :]))
                cb.link(dve, dve.scalar_tensor_tensor(o[:, :], o[:, :], gn[:, 0:1], o_sq[:, :], ALU.mult, ALU.mult))
                dve.wait_ge(z_loaded, h * 16 + 16)
                cb.link(dve, dve.tensor_tensor(o[:, :], o[:, :], z[:, :], ALU.mult))
                dve.sem_inc(y_ready, 1)
                dve.sem_inc(b_inputs_used, 1)
                assert cb.n == PER_B, cb.n

            heads(dve, stage_a, stage_b)


def merge_outputs(nc, x, ident, w_a, w_b, w_o, scratch, sc_tail, gc_tail, prompt_sconv, sample_sconv, prompt_gconv,
                  sample_gconv):
    with ExitStack() as ctx:
        s = Scope(nc, ctx, "mrg")
        y_hi = s.sb("y_hi", [P, KC, T], F32R)
        y_lo = s.sb("y_lo", [P, KC, T], F32R)
        merged = s.sb("merged", [P, KC, T])
        w = WeightStream(s, 2)
        y_raw = s.sb("y_raw", [P, 2, T])
        sig = s.sb("sig", [P, 2, T])
        t_rows = s.sb("tail_rows", [(1 + NS) * (GC_T - 1), 2, 4 * P])
        bank = [s.ps(f"bank{k}", [P, 512]) for k in range(8)]
        bank_free = [s.sem(f"bank_free{k}") for k in range(6)]
        unit_done = s.sem("unit_done")
        y_loaded = [s.sem(f"y_loaded{k}") for k in range(2)]
        sig_loaded = [s.sem(f"sig_loaded{k}") for k in range(2)]
        y_hi_done, y_ready, sig_used, merged_done = s.sem("y_hi_done"), s.sem("y_ready"), s.sem("sig_used"), s.sem("merged_done")
        t_turned, t_copied = s.sem("t_turned"), s.sem("t_copied")
        t_stored = [s.sem(f"t_stored{k}") for k in range(2)]
        block = s.block()
        weights = (w_a, w_b, w_o)
        jobs = [("gc", c) for c in range(0, 3 * H, 4)] + [("sc", c) for c in range(0, KC, 4)]

        @block.sync
        def _(sp):
            def loads(r, i):
                for j in range(2):
                    w.load(sp, i, 2, KC * r + j, weights[r][:, bass.ds(i * (2 * P) + j * P, P)].rearrange("(k p) n -> p k n", p=P))

            def load_y(r, c):
                if r or c >= 2:
                    sp.wait_ge(y_ready, KC * r + c - 1)
                sp.dma_start(y_raw[:, c % 2, :], scratch["y_a" if r == 0 else "y_b"][c]).then_inc(y_loaded[c % 2], 16)

            load_y(0, 0)
            load_y(0, 1)
            loads(0, 0)
            for c in range(2, KC):
                load_y(0, c)
            for r in range(3):
                def gates(i):
                    for j in range(2):
                        sp.wait_ge(sig_used, i * 2 + (KC * r + j + 1))
                        sp.dma_start(sig[:, j, :], scratch["sig_a" if r == 0 else "sig_b"][bass.ds(i * 2 + j, 1)]
                                     .rearrange("c p t -> p (c t)")).then_inc(sig_loaded[j], 16)
                with sp.Fori(0, KC // 2 - 1) as i:
                    if r < 2:
                        gates(i)
                    for j in range(2):
                        w.load(sp, i, 2, KC * r + 2 + j,
                               weights[r][:, bass.ds(i * (2 * P) + (2 + j) * P, P)].rearrange("(k p) n -> p k n", p=P))
                if r < 2:
                    gates(KC // 2 - 1)
                    if r == 0:
                        for c in range(2):
                            load_y(1, c)
                    loads(r + 1, 0)
                    if r == 0:
                        for c in range(2, KC):
                            load_y(1, c)

        @block.gpsimd
        def _(pool):
            w.credit_raw(pool)
            with pool.Fori(0, 3 * KC // 2) as i:
                for j in range(2):
                    w.split_lo(pool, i, 2, j)

        @block.tensor
        def _(pe):
            w.credit_split(pe)
            for k in range(6):
                pe.sem_inc(bank_free[k], 1)
            for n, (which, c) in enumerate(jobs):
                src = gc_tail if which == "gc" else sc_tail
                if n >= 2:
                    pe.wait_ge(t_copied, n - 1)
                for k in range(4):
                    mm = pe.transpose(bank[6 + n % 2][0:src.shape[2], k * P:(k + 1) * P], src[:, c + k, :], ident[:, :])
                mm.then_inc(t_turned, 1)
            for r in range(3):
                pe.wait_ge(y_ready, KC * (r + 1))
                with pe.Fori(0, KC // 2) as i:
                    for j in range(2):
                        n = KC * r + j
                        pe.wait_ge(w.lo_done, i * 2 + (n + 1))
                        for b in range(NB):
                            pe.wait_ge(bank_free[3 * j + b], i + (KC // 2 * r + 1))
                            for k in range(KC):
                                mm = three_passes(pe, bank[3 * j + b][:, 0:TH], w.hi[:, j, k, :], w.lo[:, j, k, :],
                                                  y_hi[:, k, third(b)], y_lo[:, k, third(b)], k == 0, k == KC - 1)
                            mm.then_inc(unit_done, 1)
                            if b == 1:
                                pe.wait_ge(unit_done, i * 6 + (3 * n + 1))
                                pe.sem_inc(w.split_free, 1)

        @block.scalar
        def _(act):
            w.split_hi(act, 0, 2, 0)
            for n, (which, c) in enumerate(jobs):
                act.wait_ge(t_turned, n + 1)
                if n >= 2:
                    act.wait_ge(t_stored[n % 2], 32 * (n // 2))
                rows = (gc_tail if which == "gc" else sc_tail).shape[2]
                act.copy(t_rows[0:rows, n % 2, :], bank[6 + n % 2][0:rows, :]).then_inc(t_copied, 1)
                act.wait_ge(t_copied, n + 1)
                g = (GC_T if which == "gc" else SC_T) - 1
                p_out, s_out = (prompt_gconv, sample_gconv) if which == "gc" else (prompt_sconv, sample_sconv)
                act.dma_start(p_out[0, 0][:, c * P:(c + 4) * P], t_rows[0:g, n % 2, :]).then_inc(t_stored[n % 2], 16)
                act.dma_start(s_out[0][:, :, c * P:(c + 4) * P].rearrange("s t c -> (s t) c"),
                              t_rows[g:(1 + NS) * g, n % 2, :]).then_inc(t_stored[n % 2], 16)
            for r in range(3):
                for c in range(KC):
                    if r and c == 0:
                        act.wait_ge(unit_done, 3 * KC * r)
                    if r < 2:
                        act.wait_ge(y_loaded[c % 2], 16 * (KC // 2 * r + c // 2 + 1))
                    else:
                        act.wait_ge(merged_done, 2 * NB * KC)
                    act.copy(y_hi[:, c, :], y_raw[:, c % 2, :] if r < 2 else merged[:, c, :]).then_inc(y_hi_done, 1)
                with act.Fori(0, KC // 2 - (r == 2)) as i:
                    for j in range(2):
                        w.split_hi(act, i, 2, KC * r + j + 1)
            w.split_hi(act, 0, 2, 3 * KC - 1)
            for k in range(2):
                act.wait_ge(t_stored[k], 16 * len(jobs))

        @block.vector
        def _(dve):
            dve.sem_inc(sig_used, 2)
            for r in range(3):
                for c in range(KC):
                    dve.wait_ge(y_hi_done, KC * r + c + 1)
                    dve.tensor_tensor(y_lo[:, c, :], y_raw[:, c % 2, :] if r < 2 else merged[:, c, :],
                                      y_hi[:, c, :].bitcast(F32), ALU.subtract).then_inc(y_ready, 1)
                with dve.Fori(0, KC // 2) as i:
                    for j in range(2):
                        if r < 2:
                            dve.wait_ge(sig_loaded[j], i * 16 + 16 * (KC // 2 * r + 1))
                        for b in range(NB):
                            dve.wait_ge(unit_done, i * 6 + (3 * (KC * r + j) + b + 1))
                            ps = bank[3 * j + b][:, 0:TH]
                            m = merged[:, bass.ds(i * 2 + j, 1), third(b)].rearrange("p o t -> p (o t)")
                            xc = x[:, bass.ds(i * 2 + j, 1), third(b)].rearrange("p o t -> p (o t)")
                            g = sig[:, j, third(b)]
                            if r == 0:
                                dve.tensor_tensor(m, ps, g, ALU.mult).then_inc(bank_free[3 * j + b], 1)
                                dve.wait_ge(bank_free[3 * j + b], i + 2)
                                dve.sem_inc(merged_done, 1)
                            elif r == 1:
                                dve.tensor_tensor(g, ps, g, ALU.mult).then_inc(bank_free[3 * j + b], 1)
                                dve.wait_ge(bank_free[3 * j + b], i + (KC // 2 + 2))
                                dve.tensor_tensor(m, m, g, ALU.add).then_inc(merged_done, 1)
                            else:
                                dve.tensor_tensor(xc, ps, xc, ALU.add).then_inc(bank_free[3 * j + b], 1)
                        if r < 2:
                            dve.wait_ge(merged_done, i * 6 + (3 * (KC * r + j) + NB))
                            dve.sem_inc(sig_used, 1)


def build(nc, c, out):
    scratch = {}
    for name, shape in (("y_a", (KC, P, T)), ("y_b", (H, P, T)), ("qkv", (3, H, P, T)), ("z", (H, P, T)),
                        ("sig_a", (KC, P, T)), ("sig_b", (KC, P, T))):
        scratch[name] = nc.dram_tensor(f"scratch_{name}", shape, F32, kind="Internal").ap()
    with ExitStack() as ctx:
        s = Scope(nc, ctx, "g")
        x = s.sb("x", [P, KC, T])
        ident = s.sb("ident", [P, P])
        ones = s.sb("ones", [P, P])
        gains = s.sb("gains", [P, 4, KC])
        taps = s.sb("taps", [P, KC * SC_T + 3 * H * GC_T])
        eps = s.sb("eps", [P, 1])
        sc_hist = s.sb("sc_hist", [P, KC, NS * (SC_T - 1)])
        gc_hist = s.sb("gc_hist", [P, 3 * H, NS * (GC_T - 1)])
        sc_tail = s.sb("sc_tail", [P, KC, NSEG * (SC_T - 1)])
        gc_tail = s.sb("gc_tail", [P, 3 * H, NSEG * (GC_T - 1)])
        ab_rows = s.sb("ab_rows", [2 * H, T])
        transpose_inputs(nc, c, x, ident, ones, eps, gains, taps, sc_hist, gc_hist)
        eps_col = eps[:, 0:1]
        ffn(nc, "ffn1", x, gains, 0, ones[:, :], eps_col, c["ffn1_w_gate"][0], c["ffn1_w_up"][0], c["ffn1_w_down"][0])
        input_projections(nc, x, gains, ones[:, :], eps_col, c["w_in"][0],
                          taps[:, 0:KC * SC_T].rearrange("p (c t) -> p c t", t=SC_T),
                          taps[:, KC * SC_T:].rearrange("p (c t) -> p c t", t=GC_T),
                          sc_hist, gc_hist, sc_tail, gc_tail, ab_rows, scratch)
        delta_rule(nc, ones[:, :], ident, eps_col, c["delta_consts"], c["head_params"], c["g_norm"], ab_rows,
                   c["state_gdn"], scratch, out["prompt_gdn"], out["sample_gdn"])
        merge_outputs(nc, x, ident, c["w_a_out"][0], c["w_b_out"][0], c["w_o"][0], scratch, sc_tail, gc_tail,
                      out["prompt_sconv"], out["sample_sconv"], out["prompt_gdn_conv"], out["sample_gdn_conv"])
        ffn(nc, "ffn2", x, gains, 2, ones[:, :], eps_col, c["ffn2_w_gate"][0], c["ffn2_w_up"][0], c["ffn2_w_down"][0])
        final_output(nc, x, gains, 3, ones[:, :], eps_col, ident, out["y_prompt"], out["y_sample"])


OUTPUTS = {
    "y_prompt": (1, SEQ, D), "y_sample": (NS, LS, D), "prompt_sconv": (1, 1, SC_T - 1, D),
    "prompt_gdn_conv": (1, 1, GC_T - 1, QKV), "prompt_gdn": (1, 1, H, P, P), "sample_sconv": (1, NS, SC_T - 1, D),
    "sample_gdn_conv": (1, NS, GC_T - 1, QKV), "sample_gdn": (1, NS, H, P, P),
}


def laid_out(inputs):
    a = {name: np.ascontiguousarray(v) for name, v in inputs.items()}

    def features_first(v):
        v = v.reshape(-1, v.shape[-1] // P, P).transpose(2, 1, 0)
        return v

    gains = [features_first(a.pop(n)).reshape(P, KC) for n in ("norm_ffn1", "norm_mix", "norm_ffn2", "norm_final")]
    taps = [features_first(a.pop(n)).reshape(P, -1) for n in ("sconv_w", "gdn_conv_w")]
    a["gains"] = np.concatenate(gains, 1)
    a["taps"] = np.concatenate(taps, 1)
    empty = np.zeros((1, H), np.float32)
    a["head_params"] = np.concatenate([np.stack([a.pop("gdn_dt_bias")[0], a.pop("gdn_a_log")[0]], 1),
                                       np.concatenate([empty, empty]).T], 0)
    a["g_norm"] = a.pop("gdn_norm").reshape(P, 1)
    a["delta_consts"] = delta_constants()
    a["identity"] = np.eye(P, dtype=np.float32)
    return a


def kernel(**inputs):
    from concourse import bacc
    from concourse.bass_utils import run_bass_kernel_spmd

    nc = bacc.Bacc("TRN2", target_bir_lowering=False, num_devices=1)
    arrays, args = {}, {}
    for name, a in laid_out(inputs).items():
        arrays[f"in_{name}"] = np.ascontiguousarray(a)
        args[name] = nc.dram_tensor(f"in_{name}", a.shape, F32, kind="ExternalInput").ap()
    outs = {n: nc.dram_tensor(f"out_{n}", shape, F32, kind="ExternalOutput").ap() for n, shape in OUTPUTS.items()}
    build(nc, args, outs)
    r = run_bass_kernel_spmd(nc, [arrays], core_ids=[0])
    return tuple(r.results[0][f"out_{n}"] for n in OUTPUTS)
```

```python
from contextlib import ExitStack

import numpy as np
import concourse.bass as bass
from concourse import mybir

F32 = mybir.dt.float32
F32R = mybir.dt.float32r
ALU = mybir.AluOpType
ACT = mybir.ActivationFunctionType

P = 128
D = 1024
KC = D // P
FF = 2816
N_META = 16
SEQ = 1024
NS = 8
LS = 8
H = 8
PT = N_META + SEQ
T = PT + NS * LS
TH = T // 3
NB = 3
EPS = 1e-6
SC_T = 3
GC_T = 4
QKV = 3 * H * P
COL_B, COL_C, COL_X = 0, D, 2 * D
COL_QKV = 3 * D
COL_AB = COL_QKV + QKV
COL_Z = COL_AB + 2 * H
COL_GA = COL_Z + D
COL_GB = COL_GA + D
NT = T // P
TAIL = T - NT * P
NSEG = 1 + NS
PT_TAIL = PT - NT * P
LEVELS = 7
TAIL_LEVELS = 4


class Chain:

    def __init__(self, sem, base=0, turn=0, per=0):
        self.sem, self.base, self.turn, self.per, self.n = sem, base, turn, per, 0

    def link(self, eng, ins):
        ins.then_inc(self.sem, 1)
        self.n += 1
        eng.wait_ge(self.sem, self.turn * self.per + (self.base + self.n))

    def end(self):
        assert self.per in (0, self.n), (self.per, self.n)
        return self.base + self.n


class Scope:

    def __init__(self, nc, ctx, phase):
        self.nc, self.ctx, self.phase, self.sems = nc, ctx, phase, []

    def sb(self, name, shape, dt=F32):
        return self.ctx.enter_context(self.nc.sbuf_tensor(f"{self.phase}_{name}", shape, dt))

    def ps(self, name, shape):
        return self.ctx.enter_context(self.nc.psum_tensor(f"{self.phase}_{name}", shape, F32))

    def sem(self, name):
        handle = self.ctx.enter_context(self.nc.semaphore(f"{self.phase}_{name}"))
        self.sems.append(handle.num)
        return handle

    def block(self):
        self.ctx.callback(self.clear)
        return self.ctx.enter_context(self.nc.Block())

    def clear(self):
        numbers = sorted(self.sems)
        while numbers:
            first = last = numbers.pop(0)
            while numbers and numbers[0] == last + 1:
                last = numbers.pop(0)
            self.nc.gpsimd.sem_clear(range(first, last + 1))
        self.nc.all_engine_barrier()


def third(b):
    return slice(b * TH, (b + 1) * TH)


class WeightStream:

    def __init__(self, s, slots):
        self.slots = slots
        self.raw = s.sb("w_raw", [P, slots, KC, P])
        self.hi = s.sb("w_hi", [P, slots, KC, P], F32R)
        self.lo = s.sb("w_lo", [P, slots, KC, P], F32R)
        self.raw_loaded = [s.sem(f"w_raw_loaded{k}") for k in range(slots)]
        self.raw_free = s.sem("w_raw_free")
        self.hi_done = s.sem("w_hi_done")
        self.lo_done = s.sem("w_lo_done")
        self.split_free = s.sem("w_split_free")

    def load(self, sp, i, per, j, src, shape=None):
        sp.wait_ge(self.raw_free, i * per + (j + 1))
        k = j % self.slots
        dst = self.raw[:, k, :, :]
        if shape is not None:
            dst = dst.rearrange("p k n -> p (k n)").rearrange("p (a b) -> p a b", a=shape)
        sp.dma_start(dst, src).then_inc(self.raw_loaded[k], 16)

    def split_hi(self, act, i, per, j):
        k = j % self.slots
        act.wait_ge(self.raw_loaded[k], i * (16 * per // self.slots) + 16 * (j // self.slots + 1))
        act.wait_ge(self.split_free, i * per + (j + 1))
        act.activation(self.hi[:, k, :, :], self.raw[:, k, :, :], ACT.Copy).then_inc(self.hi_done, 1)

    def split_lo(self, pool, i, per, j):
        k = j % self.slots
        pool.wait_ge(self.hi_done, i * per + (j + 1))
        pool.tensor_tensor(self.lo[:, k, :, :], self.raw[:, k, :, :], self.hi[:, k, :, :].bitcast(F32),
                           ALU.subtract).then_inc(self.lo_done, 1)
        pool.wait_ge(self.lo_done, i * per + (j + 1))
        pool.sem_inc(self.raw_free, 1)

    def credit_raw(self, pool):
        pool.sem_inc(self.raw_free, self.slots)

    def credit_split(self, pe):
        pe.sem_inc(self.split_free, self.slots - 1)


def three_passes(pe, out, w_hi, w_lo, x_hi, x_lo, first, last):
    pe.matmul(out, w_hi, x_hi, start=first, stop=False)
    pe.matmul(out, w_hi, x_lo, start=False, stop=False)
    return pe.matmul(out, w_lo, x_hi, start=False, stop=last)


def transpose_inputs(nc, c, x, rstd, ident, ones, eps, gains, taps, sc_hist, gc_hist):
    x_prompt, x_sample, meta = c["x_prompt"], c["x_sample"], c["meta_tokens"]
    state_sconv, state_gdn_conv = c["state_sconv"], c["state_gdn_conv"]
    with ExitStack() as ctx:
        s = Scope(nc, ctx, "tr")
        NJ = 9
        rows = s.sb("rows", [P, 3, D])
        hist = s.sb("hist", [P, QKV + D])
        sq = s.sb("sq", [P, 2, KC, P])
        ps = [s.ps(f"ps{k}", [P, 4, P]) for k in range(4)]
        sums = [s.ps(f"sums{k}", [P, 4, P]) for k in range(3)]
        rows_loaded = [s.sem(f"rows_loaded{k}") for k in range(3)]
        ident_loaded, hist_loaded, tables_loaded = s.sem("ident_loaded"), s.sem("hist_loaded"), s.sem("tables_loaded")
        turned = s.sem("turned")
        vec_out, act_out = s.sem("vec_out"), s.sem("act_out")
        squared, summed, logged = s.sem("squared"), s.sem("summed"), s.sem("logged")
        consts_set = s.sem("consts_set")
        NHIST = (QKV + D) // P
        tail_rows = N_META + NS * LS
        block = s.block()

        @block.sync
        def _(sp):
            sp.dma_start(ident[:], c["identity"]).then_inc(ident_loaded, 16)
            for j in range(NJ):
                if j >= 3:
                    sp.wait_ge(turned, 2 * (j - 2))
                if j < 8:
                    sp.dma_start(rows[:, j % 3, :], x_prompt[0, j * P:(j + 1) * P, :]).then_inc(rows_loaded[j % 3], 16)
                else:
                    sp.dma_start(rows[0:N_META, j % 3, :], meta).then_inc(rows_loaded[j % 3], 16)
                    sp.dma_start(rows[N_META:tail_rows, j % 3, :],
                                 x_sample.rearrange("b t d -> (b t) d")).then_inc(rows_loaded[j % 3], 16)
            sp.dma_start(hist[0:NS * (GC_T - 1), 0:QKV],
                         state_gdn_conv[0].rearrange("s t c -> (s t) c")).then_inc(hist_loaded, 16)
            sp.dma_start(hist[0:NS * (SC_T - 1), QKV:QKV + D],
                         state_sconv[0].rearrange("s t c -> (s t) c")).then_inc(hist_loaded, 16)
            sp.dma_start(gains[:, :, :], c["gains"].rearrange("p (a k) -> p a k", a=4)).then_inc(tables_loaded, 16)
            sp.dma_start(taps[:, :], c["taps"]).then_inc(tables_loaded, 16)
            sp.wait_ge(tables_loaded, 32)

        @block.tensor
        def _(pe):
            def tile_sums(j):
                n = P if j < 8 else tail_rows
                pe.wait_ge(consts_set, 2)
                pe.wait_ge(squared, j + 1)
                for k in range(KC):
                    mm = pe.matmul(sums[j // 4][:, j % 4, 0:n], ones[:, :], sq[:, j % 2, k, 0:n], start=(k == 0), stop=(k == KC - 1))
                mm.then_inc(summed, 1)

            pe.wait_ge(ident_loaded, 16)
            for j in range(NJ):
                n = P if j < 8 else tail_rows
                pe.wait_ge(rows_loaded[j % 3], 16 * (j // 3 + 1) + (16 if j == 8 else 0))
                for hf in range(2):
                    q = 2 * j + hf
                    if q >= 4:
                        pe.wait_ge(vec_out if hf == 0 else act_out, (q - 4) // 2 + 1)
                    for c in range(4):
                        k = 4 * hf + c
                        mm = pe.transpose(ps[q % 4][:, c, 0:n], rows[0:n, j % 3, k * P:(k + 1) * P], ident[0:n, 0:n])
                    mm.then_inc(turned, 1)
                if j:
                    tile_sums(j - 1)
            tile_sums(NJ - 1)
            pe.wait_ge(hist_loaded, 32)
            for g in range(NHIST // 4):
                q = 2 * NJ + g
                pe.wait_ge(vec_out if q % 2 == 0 else act_out, (q - 4) // 2 + 1)
                n = NS * (GC_T - 1) if g < 6 else NS * (SC_T - 1)
                for c in range(4):
                    k = 4 * g + c
                    mm = pe.transpose(ps[q % 4][:, c, 0:n], hist[0:n, k * P:(k + 1) * P], ident[0:n, 0:n])
                mm.then_inc(turned, 1)

        def copies(eng, odd, done):
            copy = eng.copy if odd else eng.tensor_copy
            for q in range(odd, 2 * NJ + NHIST // 4, 2):
                eng.wait_ge(turned, q + 1)
                b = ps[q % 4]
                if q < 2 * NJ:
                    j, k = q // 2, 4 * (q % 2)
                    if j < 8:
                        copy(x[:, k:k + 4, N_META + j * P:N_META + (j + 1) * P], b[:, :, :]).then_inc(done, 1)
                    else:
                        copy(x[:, k:k + 4, 0:N_META], b[:, :, 0:N_META])
                        copy(x[:, k:k + 4, PT:T], b[:, :, N_META:tail_rows]).then_inc(done, 1)
                elif q < 2 * NJ + 6:
                    g = q - 2 * NJ
                    copy(gc_hist[:, 4 * g:4 * g + 4, :], b[:, :, 0:NS * (GC_T - 1)]).then_inc(done, 1)
                else:
                    g = q - 2 * NJ - 6
                    copy(sc_hist[:, 4 * g:4 * g + 4, :], b[:, :, 0:NS * (SC_T - 1)]).then_inc(done, 1)

        @block.vector
        def _(dve):
            dve.memset(ones[:, :], 1.0).then_inc(consts_set, 1)
            dve.memset(eps[:, :], EPS).then_inc(consts_set, 1)
            copies(dve, 0, vec_out)

        @block.gpsimd
        def _(pool):
            for j in range(NJ):
                pool.wait_ge(vec_out, j + 1)
                pool.wait_ge(act_out, j + 1)
                if j >= 2:
                    pool.wait_ge(summed, j - 1)
                if j < 8:
                    cols = x[:, :, N_META + j * P:N_META + (j + 1) * P]
                    pool.tensor_tensor(sq[:, j % 2, :, :], cols, cols, ALU.mult).then_inc(squared, 1)
                else:
                    pool.tensor_tensor(sq[:, j % 2, :, 0:N_META], x[:, :, 0:N_META], x[:, :, 0:N_META], ALU.mult)
                    pool.tensor_tensor(sq[:, j % 2, :, N_META:tail_rows], x[:, :, PT:T], x[:, :, PT:T],
                                       ALU.mult).then_inc(squared, 1)

        @block.scalar
        def _(act):
            copies(act, 1, act_out)
            act.wait_ge(consts_set, 2)
            act.wait_ge(summed, NJ)
            log = {"func": ACT.Ln, "bias": eps[:, 0:1], "scale": 1.0 / D}
            for g in range(2):
                at = N_META + 4 * P * g
                act.activation(rstd[:, at:at + 4 * P], sums[g][:, :, :].rearrange("p a b -> p (a b)"), **log)
            act.activation(rstd[:, 0:N_META], sums[2][:, 0, 0:N_META], **log)
            act.activation(rstd[:, PT:T], sums[2][:, 0, N_META:tail_rows], **log).then_inc(logged, 1)
            act.wait_ge(logged, 1)
            act.activation(rstd[:, :], rstd[:, :], ACT.Exp, scale=-0.5)


class NextNorm:

    def __init__(self, s, rstd, ones, eps_col, sq):
        self.rstd, self.ones, self.eps_col, self.sq = rstd, ones, eps_col, sq
        self.squared = s.sem("nrm_squared")
        self.added = s.sem("nrm_added")
        self.summed = s.sem("nrm_summed")
        self.logged = s.sem("nrm_logged")
        self.factor = s.sem("nrm_factor")

    def clear(self, pool):
        pool.memset(self.rstd[:, :], 0.0).then_inc(self.added, NB)

    def square(self, act, x_part, i, per, n):
        act.wait_ge(self.added, i * per + (n + 1))
        act.activation(self.sq[:, third(n % NB)], x_part, ACT.Square).then_inc(self.squared, 1)

    def add(self, pool, i, per, n):
        pool.wait_ge(self.squared, i * per + (n + 1))
        pool.wait_ge(self.added, i * per + (n + 1))
        part = third(n % NB)
        pool.tensor_tensor(self.rstd[:, part], self.rstd[:, part], self.sq[:, part], ALU.add).then_inc(self.added, 1)

    def sum(self, pe, out, b):
        pe.wait_ge(self.added, NB * KC + b + 1)
        pe.matmul(out, self.ones, self.rstd[:, third(b)], start=True, stop=True).then_inc(self.summed, 1)

    def factors(self, act, ps):
        for b in range(NB):
            act.wait_ge(self.summed, b + 1)
            act.activation(self.rstd[:, third(b)], ps(b), ACT.Ln, bias=self.eps_col, scale=1.0 / D).then_inc(self.logged, 1)
        for b in range(NB):
            act.wait_ge(self.logged, b + 1)
            act.activation(self.rstd[:, third(b)], self.rstd[:, third(b)], ACT.Exp, scale=-0.5).then_inc(self.factor, 1)


def ffn(nc, name, x, rstd, gains, g_at, ones, eps_col, w_gate, w_up, w_down):
    GROUPS = FF // (2 * P)
    TURNS = (GROUPS - 1) // 2
    PER = 6
    with ExitStack() as ctx:
        s = Scope(nc, ctx, name)
        h_hi = s.sb("h_hi", [P, KC, T], F32R)
        h_lo = s.sb("h_lo", [P, KC, T], F32R)
        mid_hi = s.sb("mid_hi", [P, 2, 2, T], F32R)
        mid_lo = s.sb("mid_lo", [P, 2, 2, T], F32R)
        w = WeightStream(s, 3)
        hid = s.sb("hid", [P, 2, T])
        bank = [s.ps(f"bank{k}", [P, 512]) for k in range(6)]
        nrm = NextNorm(s, rstd, ones, eps_col, hid[:, 0, :])
        bank_free = [s.sem(f"bank_free{k}") for k in range(6)]
        h_scaled, h_hi_done, h_ready = s.sem("h_scaled"), s.sem("h_hi_done"), s.sem("h_ready")
        gu_done, down_done = s.sem("gu_done"), s.sem("down_done")
        mid_hi_done, mid_ready, x_final = s.sem("mid_hi_done"), s.sem("mid_ready"), s.sem("x_final")
        block = s.block()
        TURN = 12

        def first_block(par):
            return 0 if par == 0 else 4 + PER * (par - 1)

        def gu_use(par, a):
            return a if par == 0 else 6 * par - 4 + a

        @block.sync
        def _(sp):
            def gate_up(i, par):
                for a in range(2):
                    for q, src in enumerate((w_gate, w_up)):
                        w.load(sp, i, TURN, first_block(par) + 2 * a + q,
                               src[:, bass.ds(i * (4 * P) + (2 * par + a) * P, P)].rearrange("(k p) n -> p k n", p=P))

            def down(i, par, j0):
                for a in range(2):
                    w.load(sp, i, TURN, j0 + a,
                           w_down[bass.ds(i * (4 * P) + (2 * par + a) * P, P), :].rearrange("p (k n) -> p k n", n=P))

            gate_up(0, 0)
            with sp.Fori(0, TURNS) as i:
                for par in (1, 2):
                    gate_up(i, par)
                    down(i, par - 1, first_block(par) + 4)
            down(TURNS, 0, 4)

        @block.gpsimd
        def _(pool):
            w.credit_raw(pool)
            for j in range(4):
                w.split_lo(pool, 0, TURN, j)
            with pool.Fori(0, TURNS) as i:
                for j in range(4, 4 + TURN):
                    w.split_lo(pool, i, TURN, j)
            for j in (4, 5):
                w.split_lo(pool, TURNS, TURN, j)
            pool.wait_ge(h_ready, KC)
            nrm.clear(pool)
            for n in range(NB * KC):
                nrm.add(pool, 0, 0, n)

        @block.tensor
        def _(pe):
            w.credit_split(pe)
            for k in range(6):
                pe.sem_inc(bank_free[k], 1)

            pe.wait_ge(w.lo_done, 2)
            for k6 in range(6):
                pe.wait_ge(bank_free[k6], 1)
            for k in range(KC):
                pe.wait_ge(h_ready, k + 1)
                for k6 in range(6):
                    q, b = divmod(k6, NB)
                    mm = three_passes(pe, bank[k6][:, 0:TH], w.hi[:, q, k, :], w.lo[:, q, k, :],
                                      h_hi[:, k, third(b)], h_lo[:, k, third(b)], k == 0, k == KC - 1)
                    if k == KC - 1:
                        mm.then_inc(gu_done, 1)
            pe.wait_ge(gu_done, 4)
            pe.sem_inc(w.split_free, 1)

            def gate_up(i, par):
                for j in range(2 if par == 0 else 0, 4):
                    a, q = divmod(j, 2)
                    n = first_block(par) + j
                    pe.wait_ge(w.lo_done, i * TURN + (n + 1))
                    for b in range(NB):
                        k6 = 3 * q + b
                        pe.wait_ge(bank_free[k6], i * TURN + (gu_use(par, a) + 1))
                        for k in range(KC):
                            mm = three_passes(pe, bank[k6][:, 0:TH], w.hi[:, n % 3, k, :], w.lo[:, n % 3, k, :],
                                              h_hi[:, k, third(b)], h_lo[:, k, third(b)], k == 0, k == KC - 1)
                        mm.then_inc(gu_done, 1)
                        if b == 1:
                            pe.wait_ge(gu_done, i * 24 + (12 * par + 3 * j + 1))
                            pe.sem_inc(w.split_free, 1 if j else 2)

            def down(i, par, n, use, after):
                m = par % 2
                pe.wait_ge(w.lo_done, i * TURN + (n + 2))
                pe.wait_ge(mid_ready, i * 12 + (6 * par + 6))
                for c in range(KC):
                    for b in range(NB):
                        k6 = 3 * (c % 2) + b
                        pe.wait_ge(bank_free[k6], i * TURN + (use + c // 2 + 1))
                        for a in range(2):
                            mm = three_passes(pe, bank[k6][:, 0:TH], w.hi[:, (n + a) % 3, c, :],
                                              w.lo[:, (n + a) % 3, c, :], mid_hi[:, m, a, third(b)],
                                              mid_lo[:, m, a, third(b)], a == 0, a == 1)
                        mm.then_inc(down_done, 1)
                        if after and c == 0 and b == 0:
                            pe.wait_ge(gu_done, i * 24 + 12 * (par + 2))
                            pe.sem_inc(w.split_free, 1)

            gate_up(0, 0)
            with pe.Fori(0, TURNS) as i:
                gate_up(i, 1)
                down(i, 0, first_block(1) + 4, 4, True)
                gate_up(i, 2)
                down(i, 1, first_block(2) + 4, 10, True)
            pe.wait_ge(down_done, 24 * 2 * TURNS)
            pe.sem_inc(w.split_free, 2)
            down(TURNS, 0, 4, 2, False)
            for b in range(NB):
                pe.wait_ge(bank_free[b], TURNS * TURN + 2 + KC // 2 + 1)
                nrm.sum(pe, bank[b][:, 0:TH], b)

        @block.scalar
        def _(act):
            w.split_hi(act, 0, TURN, 0)
            w.split_hi(act, 0, TURN, 1)
            for k in range(KC):
                act.wait_ge(h_scaled, k + 1)
                act.copy(h_hi[:, k, :], hid[:, k % 2, :]).then_inc(h_hi_done, 1)

            def gate_up(i, par):
                n = first_block(par)
                for a in range(2):
                    if par or a:
                        w.split_hi(act, i, TURN, n + 2 * a + 1)
                    for b in range(NB):
                        act.wait_ge(gu_done, i * 24 + (12 * par + 6 * a + b + 1))
                        if par == 0:
                            act.wait_ge(h_ready, KC)
                        else:
                            act.wait_ge(mid_ready, i * 12 + (6 * (par - 1) + 3 * a + b + 1))
                        act.activation(hid[:, a, third(b)], bank[b][:, 0:TH], ACT.Silu).then_inc(bank_free[b], 1)
                    w.split_hi(act, i, TURN, n + 2 * a + 2)
                    for b in range(NB):
                        act.wait_ge(bank_free[3 + b], i * TURN + (gu_use(par, a) + 2))
                        act.copy(mid_hi[:, par % 2, a, third(b)], hid[:, a, third(b)]).then_inc(mid_hi_done, 1)

            gate_up(0, 0)
            with act.Fori(0, TURNS) as i:
                for par in (1, 2):
                    gate_up(i, par)
                    w.split_hi(act, i, TURN, first_block(par) + 5)
                    w.split_hi(act, i, TURN, first_block(par) + 6)
            w.split_hi(act, TURNS, TURN, 5)
            act.wait_ge(mid_ready, TURNS * 12 + 6)
            for n in range(NB * KC):
                c, b = divmod(n, NB)
                act.wait_ge(x_final, n + 1)
                nrm.square(act, x[:, c, third(b)], 0, 0, n)
            nrm.factors(act, lambda b: bank[b][:, 0:TH])

        @block.vector
        def _(dve):
            for k in range(KC):
                if k >= 2:
                    dve.wait_ge(h_ready, k - 1)
                dve.scalar_tensor_tensor(hid[:, k % 2, :], x[:, k, :], gains[:, g_at, k:k + 1], rstd[:, :],
                                         ALU.mult, ALU.mult).then_inc(h_scaled, 1)
                dve.wait_ge(h_hi_done, k + 1)
                dve.tensor_tensor(h_lo[:, k, :], hid[:, k % 2, :], h_hi[:, k, :].bitcast(F32),
                                  ALU.subtract).then_inc(h_ready, 1)

            def gate_up(i, par):
                for a in range(2):
                    for b in range(NB):
                        dve.wait_ge(gu_done, i * 24 + (12 * par + 6 * a + 3 + b + 1))
                        dve.wait_ge(bank_free[b], i * TURN + (gu_use(par, a) + 2))
                        dve.tensor_tensor(hid[:, a, third(b)], bank[3 + b][:, 0:TH], hid[:, a, third(b)],
                                          ALU.mult).then_inc(bank_free[3 + b], 1)
                        dve.wait_ge(mid_hi_done, i * 12 + (6 * par + 3 * a + b + 1))
                        dve.tensor_tensor(mid_lo[:, par % 2, a, third(b)], hid[:, a, third(b)],
                                          mid_hi[:, par % 2, a, third(b)].bitcast(F32),
                                          ALU.subtract).then_inc(mid_ready, 1)

            def down(i, par, last=False):
                for c in range(KC):
                    for b in range(NB):
                        k6 = 3 * (c % 2) + b
                        dve.wait_ge(down_done, i * 48 + (24 * par + 3 * c + b + 1))
                        ins = dve.scalar_tensor_tensor(x[:, c, third(b)], bank[k6][:, 0:TH], 0.5, x[:, c, third(b)],
                                                       ALU.mult, ALU.add)
                        if last:
                            ins.then_inc(x_final, 1)
                            dve.wait_ge(x_final, NB * c + b + 1)
                            dve.sem_inc(bank_free[k6], 1)
                        else:
                            ins.then_inc(bank_free[k6], 1)

            gate_up(0, 0)
            with dve.Fori(0, TURNS) as i:
                gate_up(i, 1)
                down(i, 0)
                gate_up(i, 2)
                down(i, 1)
            down(TURNS, 0, last=True)


def final_output(nc, x, rstd, gains, g_at, ident, y_prompt, y_sample):
    with ExitStack() as ctx:
        s = Scope(nc, ctx, "fin")
        y = s.sb("y", [P, KC, T])
        rows = s.sb("rows", [P, 3, D])
        bank = [s.ps(f"bank{k}", [P, 512]) for k in range(6)]
        scaled, turned = s.sem("scaled"), s.sem("turned")
        vec_out, act_out, stored = s.sem("vec_out"), s.sem("act_out"), [s.sem(f"stored{k}") for k in range(3)]
        block = s.block()
        NJ = 9

        @block.tensor
        def _(pe):
            for q in range(2 * NJ):
                j, k = q // 2, 4 * (q % 2)
                n = P if j < 8 else NS * LS
                if q < 2:
                    pe.wait_ge(scaled, 4 * (q + 1))
                if q >= 6:
                    pe.wait_ge(vec_out if q % 2 == 0 else act_out, (q - 6) // 2 + 1)
                for c in range(4):
                    mm = pe.transpose(bank[q % 6][0:n, c * P:(c + 1) * P],
                                      y[:, k + c, N_META + j * P:N_META + j * P + n], ident[:, :])
                mm.then_inc(turned, 1)

        def copies(eng, odd, done):
            copy = eng.copy if odd else eng.tensor_copy
            for q in range(odd, 2 * NJ, 2):
                j = q // 2
                n = P if j < 8 else NS * LS
                eng.wait_ge(turned, q + 1)
                if j >= 3:
                    eng.wait_ge(stored[j % 3], 16 * (j // 3))
                copy(rows[0:n, j % 3, 512 * odd:512 * odd + 512], bank[q % 6][0:n, :]).then_inc(done, 1)

        @block.scalar
        def _(act):
            copies(act, 1, act_out)

        @block.vector
        def _(dve):
            for k in range(KC):
                dve.scalar_tensor_tensor(y[:, k, :], x[:, k, :], gains[:, g_at, k:k + 1], rstd[:, :],
                                         ALU.mult, ALU.mult).then_inc(scaled, 1)
            copies(dve, 0, vec_out)

        @block.sync
        def _(sp):
            for j in range(NJ):
                sp.wait_ge(vec_out, j + 1)
                sp.wait_ge(act_out, j + 1)
                if j < 8:
                    sp.dma_start(y_prompt[0, j * P:(j + 1) * P, :], rows[:, j % 3, :]).then_inc(stored[j % 3], 16)
                else:
                    sp.dma_start(y_sample.rearrange("b t d -> (b t) d"),
                                 rows[0:NS * LS, j % 3, :]).then_inc(stored[j % 3], 16)
            for k in range(3):
                sp.wait_ge(stored[k], 16 * (NJ // 3))


def input_projections(nc, x, rstd, gains, w_in, sc_taps, gc_taps, sc_hist, gc_hist, sc_tail, gc_tail,
                      ab_rows, scratch):
    GP, SPD = GC_T - 1, SC_T - 1
    GL = GP + PT + NS * (GP + LS)
    SL = SPD + PT + NS * (SPD + LS)
    with ExitStack() as ctx:
        s = Scope(nc, ctx, "inp")
        h_hi = s.sb("h_hi", [P, KC, T], F32R)
        h_lo = s.sb("h_lo", [P, KC, T], F32R)
        w = WeightStream(s, 3)
        pre = s.sb("pre", [P, 3, GL])
        conv = s.sb("conv", [P, 3, GL])
        out = s.sb("out", [P, 3, T])
        sc_w = s.sb("sc_w", [P, SC_T])
        gc_w = s.sb("gc_w", [P, 3, GC_T])
        bank = [s.ps(f"bank{k}", [P, 512]) for k in range(3)]
        bank_free = [s.sem(f"bank_free{k}") for k in range(3)]
        unit_done = s.sem("unit_done")
        h_scaled, h_hi_done, h_ready = s.sem("h_scaled"), s.sem("h_hi_done"), s.sem("h_ready")
        stored = [s.sem(f"stored{k}") for k in range(3)]
        y_ready, conv_done, silu_done = s.sem("y_ready"), s.sem("conv_done"), s.sem("silu_done")
        zsig_done, z_ready, pads_zero = s.sem("zsig_done"), s.sem("z_ready"), s.sem("pads_zero")
        vec = s.sem("vec")
        block = s.block()
        NBLK = 72
        cols = lambda n0, i: w_in[:, bass.ds(n0 + i * P, P)].rearrange("(k p) n -> p k n", p=P)

        @block.sync
        def _(sp):
            for k in range(3):
                sp.sem_inc(stored[k], 16)

            def loads(loop, i, ahead):
                starts = ((COL_B, COL_C, COL_X), (COL_QKV, COL_QKV + D, COL_QKV + 2 * D), (COL_Z, COL_GA, COL_GB))
                for j in range(3):
                    w.load(sp, i, 3, 24 * loop + 3 * ahead + j, cols(starts[loop][j] + ahead * P, i))

            def store_y(i):
                sp.wait_ge(y_ready, i + 2)
                sp.dma_start(scratch["y_a"][bass.ds(i, 1)].rearrange("c p t -> p (c t)"), out[:, 0, :]).then_inc(stored[0], 16)

            def store_qkv(i):
                for j in range(3):
                    sp.wait_ge(silu_done, i * 3 + (j + 1 + 3))
                    sp.dma_start(scratch["qkv"][j][bass.ds(i, 1)].rearrange("c p t -> p (c t)"), out[:, j, :]).then_inc(stored[j], 16)

            def store_gates(i):
                sp.wait_ge(z_ready, i * 3 + 6)
                sp.dma_start(scratch["z"][bass.ds(i, 1)].rearrange("c p t -> p (c t)"), out[:, 0, :]).then_inc(stored[0], 16)
                for j, name in ((1, "sig_a"), (2, "sig_b")):
                    sp.wait_ge(bank_free[2], i * 3 + (48 + j + 2))
                    sp.dma_start(scratch[name][bass.ds(i, 1)].rearrange("c p t -> p (c t)"), out[:, j, :]).then_inc(stored[j], 16)

            loads(0, 0, 0)
            for loop, store in enumerate((store_y, store_qkv, store_gates)):
                with sp.Fori(0, KC - 1) as i:
                    loads(loop, i, 1)
                    store(i)
                if loop < 2:
                    loads(loop + 1, 0, 0)
                else:
                    w.load(sp, 0, 3, NBLK, cols(COL_AB, 0))
                store(KC - 1)
            for k in range(3):
                sp.wait_ge(stored[k], 16 * (1 + (3 if k == 0 else 2) * KC))

        @block.gpsimd
        def _(pool):
            w.credit_raw(pool)
            with pool.Fori(0, NBLK // 3) as i:
                for j in range(3):
                    w.split_lo(pool, i, 3, j)
            w.split_lo(pool, 0, 3, NBLK)

        @block.tensor
        def _(pe):
            w.credit_split(pe)
            for b in range(NB):
                pe.sem_inc(bank_free[b], 1)

            def project(i, j):
                pe.wait_ge(w.lo_done, i * 3 + (j + 1))
                for b in range(NB):
                    pe.wait_ge(bank_free[b], i * 3 + (j + 1))
                    for k in range(KC):
                        mm = three_passes(pe, bank[b][:, 0:TH], w.hi[:, j % 3, k, :], w.lo[:, j % 3, k, :],
                                          h_hi[:, k, third(b)], h_lo[:, k, third(b)], k == 0, k == KC - 1)
                    mm.then_inc(unit_done, 1)
                    if b == 1:
                        pe.wait_ge(unit_done, i * 9 + (3 * j + 1))
                        pe.sem_inc(w.split_free, 1)

            pe.wait_ge(w.lo_done, 1)
            for b in range(NB):
                pe.wait_ge(bank_free[b], 1)
            for k in range(KC):
                pe.wait_ge(h_ready, k + 1)
                for b in range(NB):
                    mm = three_passes(pe, bank[b][:, 0:TH], w.hi[:, 0, k, :], w.lo[:, 0, k, :],
                                      h_hi[:, k, third(b)], h_lo[:, k, third(b)], k == 0, k == KC - 1)
                    if k == KC - 1:
                        mm.then_inc(unit_done, 1)
            with pe.Fori(0, NBLK // 3) as i:
                for j in range(3):
                    project(i, j + 1)

        @block.scalar
        def _(act):
            w.split_hi(act, 0, 3, 0)
            for k in range(KC):
                act.wait_ge(h_scaled, k + 1)
                act.copy(h_hi[:, k, :], out[:, k % 2, :]).then_inc(h_hi_done, 1)
            act.wait_ge(h_ready, KC)

            def unit(i, n, b):
                act.wait_ge(unit_done, i * 9 + (3 * n + b + 1))
                return bank[b][:, 0:TH]

            with act.Fori(0, KC) as i:
                for j in range(2):
                    w.split_hi(act, i, 3, j + 1)
                    if j == 0:
                        act.wait_ge(y_ready, i + 1)
                    for b in range(NB):
                        src = unit(i, j, b)
                        act.copy(conv[:, 1 + j, third(b)], src).then_inc(bank_free[b], 1)
                w.split_hi(act, i, 3, 3)
            act.wait_ge(y_ready, KC + 1)

            with act.Fori(0, H) as i:
                def silu(j):
                    act.wait_ge(conv_done, i * 3 + (j + 1 + 3))
                    act.wait_ge(stored[j], i * 16 + (16 + (16 * KC if j == 0 else 0)))
                    act.activation(out[:, j, 0:PT], conv[:, j, 0:PT], ACT.Silu)
                    act.activation(out[:, j, PT:T].rearrange("p (s l) -> p s l", l=LS),
                                   conv[:, j, GP + PT:GL].rearrange("p (s l) -> p s l", l=GP + LS)[:, :, 0:LS],
                                   ACT.Silu).then_inc(silu_done, 1)

                for j in range(3):
                    n = 24 + j
                    w.split_hi(act, i, 3, n + 1)
                    act.wait_ge(conv_done, i * 3 + (j + 1))
                    for b in range(NB):
                        src = unit(i, n, b)
                        if b < 2:
                            act.copy(pre[:, j, GP + b * TH:GP + (b + 1) * TH], src).then_inc(bank_free[b], 1)
                        else:
                            act.copy(pre[:, j, GP + 2 * TH:GP + PT], src[:, 0:PT - 2 * TH])
                            act.copy(pre[:, j, GP + PT:GL].rearrange("p (s l) -> p s l", l=GP + LS)[:, :, GP:],
                                     src[:, PT - 2 * TH:TH].rearrange("p (s l) -> p s l", l=LS)).then_inc(bank_free[b], 1)
                    if j:
                        silu(j - 1)
                silu(2)

            with act.Fori(0, KC) as i:
                for j in range(3):
                    n = 48 + j
                    w.split_hi(act, i, 3, n + 1)
                    if j:
                        act.wait_ge(stored[j], i * 16 + 16 * (1 + KC))
                    for b in range(NB):
                        src = unit(i, n, b)
                        if j == 0:
                            act.wait_ge(z_ready, i * 3 + (b + 1))
                            act.activation(conv[:, 0, third(b)], src, ACT.Sigmoid).then_inc(zsig_done, 1)
                        else:
                            act.activation(out[:, j, third(b)], src, ACT.Sigmoid).then_inc(bank_free[b], 1)
            for b in range(NB):
                src = unit(0, NBLK, b)
                act.copy(ab_rows[:, third(b)], src[0:2 * H, :]).then_inc(bank_free[b], 1)

        @block.vector
        def _(dve):
            dve.memset(pre[:, :, 0:GP], 0.0).then_inc(pads_zero, 1)
            dve.sem_inc(conv_done, 3)
            dve.sem_inc(silu_done, 3)
            dve.sem_inc(z_ready, 3)
            dve.sem_inc(y_ready, 1)
            for k in range(KC):
                if k >= 2:
                    dve.wait_ge(h_ready, k - 1)
                dve.scalar_tensor_tensor(out[:, k % 2, :], x[:, k, :], gains[:, 1, k:k + 1], rstd[:, :],
                                         ALU.mult, ALU.mult).then_inc(h_scaled, 1)
                dve.wait_ge(h_hi_done, k + 1)
                dve.tensor_tensor(h_lo[:, k, :], out[:, k % 2, :], h_hi[:, k, :].bitcast(F32),
                                  ALU.subtract).then_inc(h_ready, 1)
            dve.wait_ge(pads_zero, 1)

            cx = pre[:, 0, GP - SPD:GP - SPD + SL]
            cx_sample = cx[:, SPD + PT:SL].rearrange("p (s l) -> p s l", l=SPD + LS)
            with dve.Fori(0, KC) as i:
                ch = Chain(vec, 0, i, 6)
                dve.tensor_copy(cx_sample[:, :, 0:SPD],
                                sc_hist[:, bass.ds(i, 1), :].rearrange("p o (s t) -> p (o s) t", t=SPD))
                ch.link(dve, dve.tensor_copy(sc_w[:, :], sc_taps[:, bass.ds(i, 1), :].rearrange("p o t -> p (o t)")))
                for b in range(NB):
                    dve.wait_ge(unit_done, i * 9 + (6 + b + 1))
                    dve.wait_ge(bank_free[b], i * 3 + 3)
                    if b < 2:
                        dve.tensor_tensor(cx[:, SPD + b * TH:SPD + (b + 1) * TH], bank[b][:, 0:TH],
                                          conv[:, 2, third(b)], ALU.mult).then_inc(bank_free[b], 1)
                    else:
                        dve.tensor_tensor(cx[:, SPD + 2 * TH:SPD + PT], bank[b][:, 0:PT - 2 * TH],
                                          conv[:, 2, 2 * TH:PT], ALU.mult)
                        dve.tensor_tensor(cx_sample[:, :, SPD:], bank[b][:, PT - 2 * TH:TH].rearrange("p (s l) -> p s l", l=LS),
                                          conv[:, 2, PT:T].rearrange("p (s l) -> p s l", l=LS),
                                          ALU.mult).then_inc(bank_free[b], 1)
                dve.wait_ge(bank_free[2], i * 3 + 4)
                W = SL - SPD
                ch.link(dve, dve.tensor_scalar(conv[:, 0, 0:W], cx[:, 0:W], sc_w[:, 0:1], None, ALU.mult))
                for t in range(1, SC_T):
                    ch.link(dve, dve.scalar_tensor_tensor(conv[:, 0, 0:W], cx[:, t:t + W], sc_w[:, t:t + 1],
                                                          conv[:, 0, 0:W], ALU.mult, ALU.add))
                dve.tensor_copy(sc_tail[:, bass.ds(i, 1), 0:SPD].rearrange("p o t -> p (o t)"), cx[:, PT:PT + SPD])
                ch.link(dve, dve.tensor_copy(sc_tail[:, bass.ds(i, 1), SPD:].rearrange("p o (s t) -> p (o s) t", t=SPD),
                                             cx_sample[:, :, LS:]))
                dve.wait_ge(stored[0], i * 16 + 16)
                ch.link(dve, dve.tensor_tensor(out[:, 0, 0:PT], conv[:, 0, 0:PT], conv[:, 1, 0:PT], ALU.mult))
                dve.tensor_tensor(out[:, 0, PT:T].rearrange("p (s l) -> p s l", l=LS),
                                  conv[:, 0, SPD + PT:SL].rearrange("p (s l) -> p s l", l=SPD + LS)[:, :, 0:LS],
                                  conv[:, 1, PT:T].rearrange("p (s l) -> p s l", l=LS), ALU.mult).then_inc(y_ready, 1)
                ch.end()
            base = ch.per * KC

            with dve.Fori(0, H) as i:
                ch = Chain(vec, base, i, 1 + 3 * GC_T)
                ch.link(dve, dve.tensor_copy(gc_w[:, :, :], gc_taps.rearrange("p (j h) t -> p j h t", h=H)[:, :, bass.ds(i, 1), :]
                                             .rearrange("p j o t -> p j (o t)")))
                for j in range(3):
                    row = pre[:, j, :]
                    row_sample = pre[:, j, GP + PT:GL].rearrange("p (s l) -> p s l", l=GP + LS)
                    dve.wait_ge(conv_done, i * 3 + (j + 3))
                    dve.tensor_copy(row_sample[:, :, 0:GP],
                                    gc_hist[:, bass.ds(i + j * H, 1), :].rearrange("p o (s t) -> p (o s) t", t=GP)).then_inc(pads_zero, 1)
                    dve.wait_ge(pads_zero, i * 3 + (j + 2))
                    dve.wait_ge(bank_free[2], i * 3 + (24 + j + 2))
                    dve.wait_ge(silu_done, i * 3 + (j + 1))
                    W = GL - GP
                    ch.link(dve, dve.tensor_scalar(conv[:, j, 0:W], row[:, 0:W], gc_w[:, j, 0:1], None, ALU.mult))
                    for t in range(1, GC_T):
                        ch.link(dve, dve.scalar_tensor_tensor(conv[:, j, 0:W], row[:, t:t + W], gc_w[:, j, t:t + 1],
                                                              conv[:, j, 0:W], ALU.mult, ALU.add))
                    tail = gc_tail[:, bass.ds(i + j * H, 1), :]
                    dve.tensor_copy(tail[:, :, 0:GP].rearrange("p o t -> p (o t)"), row[:, PT:PT + GP])
                    dve.tensor_copy(tail[:, :, GP:].rearrange("p o (s t) -> p (o s) t", t=GP),
                                    row_sample[:, :, LS:]).then_inc(conv_done, 1)
                ch.end()

            with dve.Fori(0, KC) as i:
                for b in range(NB):
                    dve.wait_ge(zsig_done, i * 3 + (b + 1))
                    if b == 0:
                        dve.wait_ge(stored[0], i * 16 + 16 * (1 + 2 * KC))
                    dve.tensor_tensor(out[:, 0, third(b)], bank[b][:, 0:TH], conv[:, 0, third(b)],
                                      ALU.mult).then_inc(z_ready, 1)
                    dve.wait_ge(z_ready, i * 3 + (b + 1 + 3))
                    dve.sem_inc(bank_free[b], 1)


class Units:

    def __init__(self, s, label, order, banks):
        self.order = order
        self.banks = banks
        self.at = {name: k for k, (name, _) in enumerate(order)}
        self.per = len(order)
        self.bank_per = [sum(b == k for _, b in order) for k in range(len(banks))]
        self.use = {name: sum(b == bank for _, b in order[:k]) for k, (name, bank) in enumerate(order)}
        self.done = s.sem(f"{label}_done")
        self.free = [s.sem(f"{label}_bank{k}_free") for k in range(len(banks))]

    def ps(self, name):
        return self.banks[self.order[self.at[name]][1]]

    def sem(self, name):
        return self.free[self.order[self.at[name]][1]]

    def wait_bank(self, pe, h, name):
        b = self.order[self.at[name]][1]
        pe.wait_ge(self.free[b], h * self.bank_per[b] + (self.use[name] + 1))

    def wait_done(self, eng, h, name):
        eng.wait_ge(self.done, h * self.per + (self.at[name] + 1))

    def wait_read(self, eng, h, name):
        b = self.order[self.at[name]][1]
        eng.wait_ge(self.free[b], h * self.bank_per[b] + (self.use[name] + 2))


CONST_COLS = {}
_at = 0
for _name, _width in (("upto", P), ("upto_tail", TAIL), ("after", P), ("after_tail", TAIL), ("level", LEVELS * P),
                      ("segment", NSEG)):
    CONST_COLS[_name] = (_at, _width)
    _at += _width
CONST_W = _at


def delta_constants():
    t = np.zeros((P, CONST_W), np.float32)
    m, i = np.arange(P)[:, None], np.arange(P)[None, :]
    seg = np.where(np.arange(TAIL) < PT_TAIL, 0, 1 + (np.arange(TAIL) - PT_TAIL) // LS)
    same = seg[:, None] == seg[None, :]
    mt, it = m[:TAIL], i[:, :TAIL]

    def put(name, a):
        t[:a.shape[0], CONST_COLS[name][0]:CONST_COLS[name][0] + a.shape[1]] = a

    put("upto", m <= i)
    put("upto_tail", (mt <= it) & same)
    put("after", m > i)
    put("after_tail", (mt > it) & same)
    put("level", np.concatenate([(m >> (k + 1) == i >> (k + 1)) & (m >> k & 1 == 0) & (i >> k & 1 == 1)
                                 for k in range(LEVELS)], 1))
    put("segment", seg[:, None] == np.arange(NSEG)[None, :])
    return t


GROUPS_OF_TILES = ((0, 4), (4, 4), (8, 1))


def delta_rule(nc, ones, ident, eps_col, consts_in, head_params, g_norm, ab_rows, state_in, scratch, prompt_state,
               sample_state):
    with ExitStack() as ctx:
        s = Scope(nc, ctx, "dr")
        con = s.sb("con", [P, CONST_W])
        hp = s.sb("head_params", [2 * H, 2])
        gn = s.sb("g_norm", [P, 1])

        def const(name, n=P):
            a, width = CONST_COLS[name]
            return con[0:n, a:a + width]

        level = const("level").rearrange("p (k i) -> p k i", i=P)
        per_token = s.sb("per_token", [P, 4, NT + 1, H])
        na = s.sb("neg_rate", [2 * H, 1])
        tok = [s.sb(f"tok{p}", [P, 4, NT + 1]) for p in range(2)]
        q = s.sb("q", [P, T])
        k_raw = s.sb("k_raw", [P, T])
        v = s.sb("v", [P, T])
        k_t = [s.sb(f"k{p}", [P, T]) for p in range(2)]
        v_tail = [s.sb(f"v_tail{p}", [P, TAIL]) for p in range(2)]
        z = s.sb("z", [P, T])
        sq = s.sb("sq", [P, 2, T])
        lu = s.sb("lu", [P, T])
        dec = s.sb("dec", [P, T])
        bdec = s.sb("bdec", [P, T])
        raw = [buf[0:2 * H, :] for buf in (sq[:, 0, :], sq[:, 1, :], lu, dec)]
        bmat = s.sb("bmat", [P, T])
        bk = s.sb("bk", [P, 2, T])
        w_inv = s.sb("w_inv", [P, T])
        y_lev = s.sb("y_lev", [P, T])
        x_inv = [s.sb(f"x_inv{p}", [P, T]) for p in range(2)]
        eg = [s.sb(f"eg{p}", [P, T]) for p in range(2)]
        qd = [s.sb(f"qd{p}", [P, T]) for p in range(2)]
        aqk = [s.sb(f"aqk{p}", [P, T]) for p in range(2)]
        kdec = [s.sb(f"kdec{p}", [P, (NT + 1), P]) for p in range(2)]
        v_tok = [s.sb(f"v_tok{p}", [P, NT, P]) for p in range(2)]
        state = s.sb("state", [P, NSEG, P])
        st_out = s.sb("st_out", [P, NSEG, P])
        resid = s.sb("resid", [P, P])
        resid_t = s.sb("resid_t", [P, TAIL])
        nu = s.sb("nu", [P, P])
        nu_seg = s.sb("nu_seg", [TAIL, NSEG, P])
        o = [s.sb(f"o{p}", [P, T]) for p in range(2)]
        o_sq = s.sb("o_sq", [P, T])

        level_steps = []
        a_names = [f"{name}{g}" for name in ("dec", "eg", "sq", "sk", "kk", "qk", "kt") for g in range(3)]
        a_names += ["vt0", "vt1", "T00", "T01", "T02"]
        for k in range(1, LEVELS):
            gs = range(3 if k < TAIL_LEVELS else 2)
            level_steps += [("Y", k, g) for g in gs] + [("X", k, g) for g in gs]
            a_names += [f"Y{k}{g}" for g in gs]
            for g in gs:
                a_names += [f"X{k}{g}"] + ([f"T{k}{g}"] if k < LEVELS - 1 else [])
        A = Units(s, "a", [(n, k % 5) for k, n in enumerate(a_names)], [s.ps(f"a_bank{k}", [P, 512]) for k in range(5)])
        a_steps = [(("pre", 0, 0), 4), (("decay", 0, 0), 6), (("norm", 0, 0), 7), (("scale", 0, 0), 5), (("kk", 0, 0), 4),
                   (("qk", 0, 0), 3), (("kt", 0, 0), 4), (("zero", 0, 0), 4)]
        a_steps += [(step, 1 if step[0] == "Y" else 2) for step in level_steps]
        b_steps = [((name, t, 0), 2) for t in range(NT) for name in ("ks", "nu", "ds")]
        b_steps += [((f"tail{k}", 0, 0), 4) for k in range(1, 5)] + [(("out1", 0, 0), 6), (("out2", 0, 0), 6)]
        A_STEPS, B_STEPS = [step for step, _ in a_steps], [step for step, _ in b_steps]

        def starts(stage, steps):
            whole = sum(share for _, share in steps)
            return [(sum(share for _, share in steps[:k]) / whole, stage, step) for k, (step, _) in enumerate(steps)]

        TURN = sorted(starts("a", a_steps) + starts("b", b_steps))
        b_order = []
        for t in range(NT):
            b_order += [(f"ks{t}", 0), (f"nu{t}", 0), (f"ds{t}", 0), (f"o{t}", 1 + t % 2)]
        b_order += [("ks8", 0), ("r8", 0), ("nu8", 0), ("o8", 1), ("ds8_0", 0), ("ds8_1", 2), ("ds8_2", 0),
                    ("on0", 1), ("on1", 2), ("on2", 0)]
        B = Units(s, "b", b_order, [s.ps(f"b_bank{k}", [P, 512]) for k in range(3)])

        cons_loaded, prep = s.sem("cons_loaded"), s.sem("prep")
        prep_act, prep_pe, vec = s.sem("prep_act"), s.sem("prep_pe"), s.sem("vec")
        qk_loaded, v_loaded, z_loaded, st_loaded = s.sem("qk_loaded"), s.sem("v_loaded"), s.sem("z_loaded"), s.sem("st_loaded")
        a_inputs_used, b_inputs_used = s.sem("a_inputs_used"), s.sem("b_inputs_used")
        lu_ready, sq_ready, sq_used, factor = s.sem("lu_ready"), s.sem("sq_ready"), s.sem("sq_used"), s.sem("factor")
        qk_ready, dec_masked, bdec_ready, qd_ready = s.sem("qk_ready"), s.sem("dec_masked"), s.sem("bdec_ready"), s.sem("qd_ready")
        bk_ready, tok_ready, v_tail_ready, x_started = s.sem("bk_ready"), s.sem("tok_ready"), s.sem("v_tail_ready"), s.sem("x_started")
        st_zeroed, r_scaled, nu_seg_ready, st_scaled = s.sem("st_zeroed"), s.sem("r_scaled"), s.sem("nu_seg_ready"), s.sem("st_scaled")
        o_sq_ready, o_rooted, o_scaled, y_ready = s.sem("o_sq_ready"), s.sem("o_rooted"), s.sem("o_scaled"), s.sem("y_ready")
        y_stored, st_stored = s.sem("y_stored"), s.sem("st_stored")
        block = s.block()

        def tile(t):
            return slice(t * P, min(t * P + P, T))

        def rows(t):
            return P if t < NT else TAIL

        def span(buf, g):
            t0, n = GROUPS_OF_TILES[g]
            return buf[0:rows(t0), t0 * P:min((t0 + n) * P, T)]

        def full(buf):
            return buf[:, 0:NT * P].rearrange("p (t i) -> p t i", i=P)

        def tail(buf):
            return buf[0:TAIL, NT * P:T]

        def psum(units, name, g):
            t0, n = GROUPS_OF_TILES[g]
            return units.ps(name)[0:rows(t0), 0:(n * P if t0 < NT else TAIL)]

        def over_tiles(a, n=NT):
            return a.unsqueeze(1).broadcast_to([P, n, P])

        def per_row(a, width=P):
            return a.unsqueeze(2).broadcast_to([a.shape[0], a.shape[1], width])

        @block.sync
        def _(sp):
            sp.dma_start(con[:, :], consts_in).then_inc(cons_loaded, 16)
            sp.dma_start(hp[:, :], head_params).then_inc(cons_loaded, 16)
            sp.dma_start(gn[:, :], g_norm).then_inc(cons_loaded, 16)

            def load_a(h):
                sp.wait_ge(a_inputs_used, h + 1)
                for j, buf in ((0, q), (1, k_raw), (2, v)):
                    sp.dma_start(buf[:, :], scratch["qkv"][j][bass.ds(h, 1)].rearrange("c p t -> p (c t)")) \
                        .then_inc(v_loaded if j == 2 else qk_loaded, 16)

            def load_b(h):
                sp.wait_ge(b_inputs_used, h + 1)
                sp.dma_start(z[:, :], scratch["z"][bass.ds(h, 1)].rearrange("c p t -> p (c t)")).then_inc(z_loaded, 16)
                sp.dma_start(state[:, 1:NSEG, :], state_in[0][:, bass.ds(h, 1)].rearrange("s o k v -> k (s o) v")).then_inc(st_loaded, 16)

            def store(h, p):
                sp.wait_ge(y_ready, h + 1)
                sp.dma_start(scratch["y_b"][bass.ds(h, 1)].rearrange("c p t -> p (c t)"), o[p][:, :]).then_inc(y_stored, 16)
                sp.dma_start(prompt_state[0, 0, bass.ds(h, 1)].rearrange("o k v -> k (o v)"), st_out[:, 0, :]).then_inc(st_stored, 16)
                sp.dma_start(sample_state[0][:, bass.ds(h, 1)].rearrange("s o k v -> k (s o) v"), st_out[:, 1:NSEG, :]).then_inc(st_stored, 16)

            sp.sem_inc(y_stored, 32)
            sp.sem_inc(st_stored, 32)
            load_a(0)
            load_b(0)
            load_a(1)
            with sp.Fori(0, H // 2 - 1) as i:
                for p in range(2):
                    h = i * 2 + p
                    load_a(h + 2)
                    store(h, p)
                    load_b(h + 1)
            store(H - 2, 0)
            load_b(H - 1)
            store(H - 1, 1)
            sp.wait_ge(y_stored, 16 * (2 + H))
            sp.wait_ge(st_stored, 32 * (1 + H))

        def heads(eng, stage_a, stage_b):
            def turn(h_a, p_a, h_b, p_b):
                for _, stage, step in TURN:
                    if stage == "a":
                        stage_a(step, h_a, p_a)
                    else:
                        stage_b(step, h_b, p_b)

            for step in A_STEPS:
                stage_a(step, 0, 0)
            with eng.Fori(0, H // 2 - 1) as i:
                turn(i * 2 + 1, 1, i * 2, 0)
                turn(i * 2 + 2, 0, i * 2 + 1, 1)
            turn(H - 1, 1, H - 2, 0)
            for step in B_STEPS:
                stage_b(step, H - 1, 1)

        @block.gpsimd
        def _(pool):
            def stage_a(step, h, p):
                name, k, g = step
                if name == "pre":
                    pool.wait_ge(tok_ready, h + 1)
                    pool.tensor_tensor(full(lu), over_tiles(const("upto")), per_row(tok[p][:, 0, 0:NT]), ALU.mult)
                    pool.tensor_tensor(tail(lu), const("upto_tail", TAIL), tok[p][0:TAIL, 0, NT:NT + 1].broadcast_to([TAIL, TAIL]),
                                       ALU.mult).then_inc(lu_ready, 1)
                    pool.wait_ge(qk_loaded, h * 32 + 32)
                    pool.wait_ge(sq_used, h + 1)
                    pool.tensor_tensor(sq[:, 0, :], q[:, :], q[:, :], ALU.mult).then_inc(sq_ready, 1)
                    pool.tensor_tensor(sq[:, 1, :], k_raw[:, :], k_raw[:, :], ALU.mult).then_inc(sq_ready, 1)
                elif name == "decay":
                    A.wait_read(pool, h, "dec2")
                    pool.tensor_tensor(full(dec), full(dec), over_tiles(const("upto")), ALU.mult)
                    pool.tensor_tensor(tail(dec), tail(dec), const("upto_tail", TAIL), ALU.mult).then_inc(dec_masked, 1)
                    pool.wait_ge(dec_masked, h + 1)
                    pool.tensor_tensor(full(bdec), full(dec), per_row(tok[p][:, 1, 0:NT]), ALU.mult)
                    pool.tensor_tensor(tail(bdec), tail(dec), tok[p][0:TAIL, 1, NT:NT + 1].broadcast_to([TAIL, TAIL]),
                                       ALU.mult).then_inc(bdec_ready, 1)
                elif name == "kt":
                    A.wait_read(pool, h, "eg2")
                    pool.wait_ge(qk_ready, h + 1)
                    pool.tensor_tensor(qd[p][:, :], q[:, :], eg[p][:, :], ALU.mult).then_inc(qd_ready, 1)
                elif name == "kk":
                    for gg in range(3):
                        A.wait_read(pool, h, f"kk{gg}")
                    mask_level(0)
                elif name == "qk":
                    mask_level(1)
                elif name == "Y" and g == 0 and k + 1 < LEVELS:
                    if k == 1:
                        A.wait_read(pool, h, "T02")
                    else:
                        A.wait_done(pool, h, f"Y{k - 1}{2 if k - 1 < TAIL_LEVELS else 1}")
                    mask_level(k + 1)

            def mask_level(k):
                if k < TAIL_LEVELS:
                    pool.tensor_tensor(tail(bk[:, k % 2, :]), tail(bmat), level[0:TAIL, k, 0:TAIL], ALU.mult)
                pool.tensor_tensor(full(bk[:, k % 2, :]), full(bmat), over_tiles(level[:, k, :]), ALU.mult).then_inc(bk_ready, 1)

            def stage_b(step, h, p):
                if step[0] == "out1":
                    B.wait_read(pool, h, "o7")
                    B.wait_read(pool, h, "o8")
                    pool.wait_ge(b_inputs_used, h + 1)
                    pool.tensor_tensor(o_sq[:, :], o[p][:, :], o[p][:, :], ALU.mult).then_inc(o_sq_ready, 1)

            heads(pool, stage_a, stage_b)

        @block.tensor
        def _(pe):
            ps = A.banks
            pe.wait_ge(prep, 1)
            for t in range(NT + 1):
                for r in range(2):
                    mm = pe.transpose(ps[0][0:rows(t), (2 * t + r) * 2 * H:(2 * t + r + 1) * 2 * H],
                                      raw[1 + r][:, tile(t)], ident[0:2 * H, 0:2 * H])
            mm.then_inc(prep_pe, 1)
            pe.wait_ge(prep, 2)
            pe.wait_ge(cons_loaded, 48)
            for r, name in ((1, "upto"), (2, "after")):
                pe.matmul(ps[r][:, 0:NT * H], const(name), per_token[:, 0, 0:NT, :].rearrange("p t h -> p (t h)"),
                          start=True, stop=True)
                mm = pe.matmul(ps[r][0:TAIL, NT * H:(NT + 1) * H], const(name + "_tail", TAIL),
                               per_token[0:TAIL, 0, NT, :], start=True, stop=True)
            mm.then_inc(prep_pe, 1)
            pe.wait_ge(prep_act, 5)
            for f in [*A.free, *B.free]:
                pe.sem_inc(f, 1)

            def per_tile(h, name, g, product):
                A.wait_bank(pe, h, f"{name}{g}")
                t0, n = GROUPS_OF_TILES[g]
                for t in range(t0, t0 + n):
                    r = rows(t)
                    mm = product(A.ps(f"{name}{g}")[0:r, (t - t0) * P:(t - t0) * P + r], t)
                mm.then_inc(A.done, 1)

            def turned(h, name, g, src):
                A.wait_bank(pe, h, f"{name}{g}")
                t0, n = GROUPS_OF_TILES[g]
                for t in range(t0, t0 + n):
                    mm = pe.transpose(A.ps(f"{name}{g}")[0:rows(t), (t - t0) * P:(t - t0 + 1) * P], src[:, tile(t)], ident[:, :])
                mm.then_inc(A.done, 1)

            def stage_a(step, h, p):
                name, k, g = step
                kn, xi = k_t[p], x_inv[p]
                if name == "decay":
                    pe.wait_ge(lu_ready, h + 1)
                    for unit, full_w, tail_w in (("dec", const("after"), const("after_tail", TAIL)), ("eg", ones, ones[0:TAIL, :])):
                        for gg in range(3):
                            A.wait_bank(pe, h, f"{unit}{gg}")
                            n = P if gg < 2 or unit == "eg" else TAIL
                            cols = span(lu, gg).shape[1]
                            pe.matmul(A.ps(f"{unit}{gg}")[0:n, 0:cols], full_w if gg < 2 else tail_w, span(lu, gg),
                                      start=True, stop=True).then_inc(A.done, 1)
                elif name == "norm":
                    for r, unit in enumerate(("sq", "sk")):
                        pe.wait_ge(sq_ready, h * 2 + (r + 1))
                        for b in range(NB):
                            A.wait_bank(pe, h, f"{unit}{b}")
                            pe.matmul(A.ps(f"{unit}{b}")[:, 0:TH], ones, sq[:, r, third(b)], start=True,
                                      stop=True).then_inc(A.done, 1)
                elif name == "kk":
                    pe.wait_ge(qk_ready, h + 1)
                    for gg in range(3):
                        per_tile(h, "kk", gg, lambda out, t: pe.matmul(out, kn[:, tile(t)], kn[:, tile(t)], start=True, stop=True))
                elif name == "qk":
                    for gg in range(3):
                        per_tile(h, "qk", gg, lambda out, t: pe.matmul(out, kn[:, tile(t)], q[:, tile(t)], start=True, stop=True))
                elif name == "kt":
                    for gg in range(3):
                        turned(h, "kt", gg, kn)
                    pe.wait_ge(v_loaded, h * 16 + 16)
                    for gg in range(2):
                        turned(h, "vt", gg, v)
                elif name == "zero":
                    pe.wait_ge(bk_ready, h * LEVELS + 1)
                    b0 = bk[:, 0, :]
                    for gg in range(3):
                        per_tile(h, "T0", gg, lambda out, t: pe.transpose(out, b0[0:rows(t), tile(t)], ident[0:rows(t), 0:rows(t)]))
                elif name == "Y":
                    if g == 0:
                        pe.wait_ge(bk_ready, h * LEVELS + (k + 1))
                    cur = bk[:, k % 2, :]
                    A.wait_read(pe, h, f"T{k - 1}{g}")
                    per_tile(h, f"Y{k}", g, lambda out, t: pe.matmul(out, cur[0:rows(t), tile(t)], w_inv[0:rows(t), tile(t)],
                                                                     start=True, stop=True))
                elif name == "X":
                    A.wait_read(pe, h, f"Y{k}{g}")
                    per_tile(h, f"X{k}", g, lambda out, t: pe.matmul(out, y_lev[0:rows(t), tile(t)], xi[0:rows(t), tile(t)],
                                                                     start=True, stop=True))
                    if k < LEVELS - 1:
                        per_tile(h, f"T{k}", g, lambda out, t: pe.matmul(out, xi[0:rows(t), tile(t)], y_lev[0:rows(t), tile(t)],
                                                                         start=True, stop=True))

            seqs = [(0, 0, PT_TAIL)] + [(1 + r, PT_TAIL + r * LS, LS) for r in range(NS)]

            def stage_b(step, h, p):
                name, t, _ = step
                kn, xi, qdp, aq, kd = k_t[p], x_inv[p], qd[p], aqk[p], kdec[p]
                if name == "ks":
                    if t == 0:
                        pe.wait_ge(st_zeroed, h + 1)
                        pe.wait_ge(qd_ready, h + 1)
                        A.wait_read(pe, h, f"X{LEVELS - 1}0")
                        A.wait_read(pe, h, f"X{LEVELS - 1}1")
                    else:
                        B.wait_read(pe, h, f"ds{t - 1}")
                    B.wait_bank(pe, h, f"ks{t}")
                    pe.matmul(B.ps(f"ks{t}")[:, 0:P], kn[:, tile(t)], state[:, 0, :], start=True, stop=True).then_inc(B.done, 1)
                    B.wait_bank(pe, h, f"o{t}")
                    pe.matmul(B.ps(f"o{t}")[:, 0:P], state[:, 0, :], qdp[:, tile(t)], start=True, stop=False)
                elif name == "nu":
                    B.wait_read(pe, h, f"ks{t}")
                    pe.matmul(B.ps(f"nu{t}")[:, P:2 * P], xi[:, tile(t)], resid[:, :], start=True, stop=True).then_inc(B.done, 1)
                elif name == "ds":
                    B.wait_read(pe, h, f"nu{t}")
                    pe.matmul(B.ps(f"ds{t}")[:, 2 * P:3 * P], kd[:, t, :], nu[:, :], start=True, stop=True).then_inc(B.done, 1)
                    pe.matmul(B.ps(f"o{t}")[:, 0:P], nu[:, :], aq[:, tile(t)], start=False, stop=True).then_inc(B.done, 1)
                elif name == "tail1":
                    pe.wait_ge(st_loaded, h * 16 + 16)
                    B.wait_read(pe, h, f"ds{NT - 1}")
                    B.wait_bank(pe, h, "ks8")
                    for r, c, n in seqs:
                        mm = pe.matmul(B.ps("ks8")[:, c:c + n], state[:, r, :], kn[:, NT * P + c:NT * P + c + n], start=True, stop=True)
                    mm.then_inc(B.done, 1)
                    B.wait_bank(pe, h, "o8")
                    for r, c, n in seqs:
                        pe.matmul(B.ps("o8")[:, c:c + n], state[:, r, :], qdp[:, NT * P + c:NT * P + c + n], start=(r == 0),
                                  stop=False, skip_group_check=True)
                elif name == "tail2":
                    B.wait_read(pe, h, "ks8")
                    pe.transpose(B.ps("r8")[0:TAIL, P:2 * P], resid_t[:, :], ident[:, :]).then_inc(B.done, 1)
                elif name == "tail3":
                    B.wait_read(pe, h, "r8")
                    pe.matmul(B.ps("nu8")[0:TAIL, 2 * P:3 * P], xi[0:TAIL, tile(NT)], resid[0:TAIL, :], start=True, stop=True).then_inc(B.done, 1)
                elif name == "tail4":
                    B.wait_read(pe, h, "nu8")
                    pe.matmul(B.ps("o8")[:, 0:TAIL], nu[0:TAIL, :], aq[0:TAIL, tile(NT)], start=False, stop=True,
                              skip_group_check=True).then_inc(B.done, 1)
                    pe.wait_ge(nu_seg_ready, h + 1)
                    for u in range(3):
                        B.wait_bank(pe, h, f"ds8_{u}")
                        pe.matmul(B.ps(f"ds8_{u}")[:, 0:3 * P], kd[0:TAIL, NT, :],
                                  nu_seg[:, 3 * u:3 * u + 3, :].rearrange("p a b -> p (a b)"), start=True, stop=True).then_inc(B.done, 1)
                elif name == "out2":
                    pe.wait_ge(o_sq_ready, h + 1)
                    for b in range(NB):
                        B.wait_bank(pe, h, f"on{b}")
                        pe.matmul(B.ps(f"on{b}")[:, 0:TH], ones, o_sq[:, third(b)], start=True, stop=True).then_inc(B.done, 1)

            heads(pe, stage_a, stage_b)

        @block.scalar
        def _(act):
            act.wait_ge(cons_loaded, 48)
            act.activation(na[:, :], hp[:, 1:2], ACT.Exp).then_inc(prep_act, 1)
            act.activation(raw[2], ab_rows[:, :], ACT.Exp, scale=-1.0).then_inc(prep_act, 1)
            act.wait_ge(vec, 2)
            act.activation(raw[3], raw[3], ACT.Exp, scale=-1.0).then_inc(prep_act, 1)
            act.wait_ge(prep_act, 3)
            act.activation(raw[3], raw[3], ACT.Ln, bias=ones[0:2 * H, 0:1]).then_inc(prep_act, 1)
            act.wait_ge(prep_pe, 2)
            for r in (1, 2):
                act.activation(per_token[:, 1 + r, 0:NT, :], A.banks[r][:, 0:NT * H].rearrange("p (t h) -> p t h", h=H), ACT.Exp)
                ins = act.activation(per_token[0:TAIL, 1 + r, NT, :], A.banks[r][0:TAIL, NT * H:(NT + 1) * H], ACT.Exp)
            ins.then_inc(prep_act, 1)

            def stage_a(step, h, p):
                name, k, g = step
                if name == "decay":
                    for gg in range(3):
                        A.wait_done(act, h, f"dec{gg}")
                        act.activation(span(dec, gg), psum(A, f"dec{gg}", gg), ACT.Exp).then_inc(A.sem(f"dec{gg}"), 1)
                    for gg in range(3):
                        A.wait_done(act, h, f"eg{gg}")
                        t0, n = GROUPS_OF_TILES[gg]
                        c = slice(t0 * P, min((t0 + n) * P, T))
                        act.activation(eg[p][:, c], A.ps(f"eg{gg}")[:, 0:c.stop - c.start], ACT.Exp).then_inc(A.sem(f"eg{gg}"), 1)
                elif name == "norm":
                    for r, unit in enumerate(("sq", "sk")):
                        A.wait_done(act, h, f"{unit}2")
                        for b in range(NB):
                            act.activation(sq[:, r, third(b)], A.ps(f"{unit}{b}")[:, 0:TH], ACT.Ln,
                                           bias=eps_col).then_inc(A.sem(f"{unit}{b}"), 1)
                        for b in range(NB):
                            A.wait_read(act, h, f"{unit}{b}")
                        act.activation(sq[:, r, :], sq[:, r, :], ACT.Exp, scale=-0.5).then_inc(factor, 1)
                elif name == "kt":
                    for gg in range(2):
                        A.wait_done(act, h, f"vt{gg}")
                        act.copy(v_tok[p][:, 4 * gg:4 * gg + 4, :], A.ps(f"vt{gg}").rearrange("p (t d) -> p t d", d=P)) \
                            .then_inc(A.sem(f"vt{gg}"), 1)
                elif name == "Y":
                    A.wait_done(act, h, f"Y{k}{g}")
                    act.copy(span(y_lev, g), psum(A, f"Y{k}{g}", g)).then_inc(A.sem(f"Y{k}{g}"), 1)

            def stage_b(step, h, p):
                name, t, _ = step
                if name == "ds":
                    if t == 0:
                        act.wait_ge(y_stored, h * 16 + 16)
                    B.wait_done(act, h, f"o{t}")
                    act.copy(o[p][:, tile(t)], B.ps(f"o{t}")[:, 0:P]).then_inc(B.sem(f"o{t}"), 1)
                elif name == "tail2":
                    B.wait_done(act, h, "r8")
                    act.copy(resid[0:TAIL, :], B.ps("r8")[0:TAIL, P:2 * P]).then_inc(B.sem("r8"), 1)
                elif name == "tail4":
                    B.wait_done(act, h, "o8")
                    act.copy(o[p][:, tile(NT)], B.ps("o8")[:, 0:TAIL]).then_inc(B.sem("o8"), 1)
                elif name == "out2":
                    B.wait_done(act, h, "on2")
                    for b in range(NB):
                        act.activation(o_sq[:, third(b)], B.ps(f"on{b}")[:, 0:TH], ACT.Ln, bias=eps_col,
                                       scale=1.0 / P).then_inc(B.sem(f"on{b}"), 1)
                    for b in range(NB):
                        B.wait_read(act, h, f"on{b}")
                    act.activation(o_sq[:, :], o_sq[:, :], ACT.Exp, scale=-0.5).then_inc(o_rooted, 1)

            heads(act, stage_a, stage_b)

        @block.vector
        def _(dve):
            ch = Chain(vec)
            dve.sem_inc(a_inputs_used, 1)
            dve.sem_inc(b_inputs_used, 1)
            dve.wait_ge(cons_loaded, 48)
            ch.link(dve, dve.tensor_scalar(raw[0], ab_rows[:, :], hp[:, 0:1], None, ALU.add))
            ch.link(dve, dve.scalar_tensor_tensor(raw[3], raw[0], -1.0, raw[0], ALU.mult, ALU.max))
            ch.link(dve, dve.memset(per_token[:, :, :, :], 0.0))
            dve.wait_ge(prep_act, 1)
            ch.link(dve, dve.tensor_scalar(na[:, :], na[:, :], -1.0, None, ALU.mult))
            dve.wait_ge(prep_act, 4)
            ch.link(dve, dve.scalar_tensor_tensor(raw[1], raw[0], 0.0, raw[3], ALU.max, ALU.add))
            ch.link(dve, dve.tensor_scalar(raw[1], raw[1], na[:, 0:1], None, ALU.mult))
            ch.link(dve, dve.tensor_scalar(raw[2], raw[2], 1.0, None, ALU.add))
            dve.reciprocal(raw[2], raw[2]).then_inc(prep, 1)
            dve.wait_ge(prep_pe, 1)
            tr = A.banks[0][:, 0:(NT + 1) * 4 * H].rearrange("p (t r h) -> p t r h", r=2, h=2 * H)
            for r in range(2):
                cols = slice(r * H, (r + 1) * H)
                dve.tensor_copy(per_token[:, r, 0:NT, :], tr[:, 0:NT, r, cols])
                ins = dve.tensor_copy(per_token[0:TAIL, r, NT, :], tr[0:TAIL, NT, r, cols])
            ins.then_inc(prep, 1)
            dve.wait_ge(prep_act, 5)
            ch.link(dve, dve.tensor_scalar(per_token[:, 2, :, :], per_token[:, 2, :, :], -1.0, None, ALU.mult))
            dve.sem_inc(sq_used, 1)

            def per_head(h):
                return [per_token[:, r, :, bass.ds(h, 1)].rearrange("p t o -> p (t o)") for r in range(4)]

            def stage_a(step, h, p):
                name, k, g = step
                if name == "pre":
                    for r, row in enumerate(per_head(h)):
                        ins = dve.tensor_copy(tok[p][:, r, :], row)
                    ins.then_inc(tok_ready, 1)
                    dve.wait_ge(tok_ready, h + 1)
                elif name == "scale":
                    dve.wait_ge(factor, h * 2 + 1)
                    dve.scalar_tensor_tensor(q[:, :], q[:, :], float(P) ** -0.5, sq[:, 0, :], ALU.mult, ALU.mult)
                    dve.wait_ge(factor, h * 2 + 2)
                    dve.tensor_tensor(k_t[p][:, :], k_raw[:, :], sq[:, 1, :], ALU.mult).then_inc(qk_ready, 1)
                    dve.wait_ge(qk_ready, h + 1)
                    dve.sem_inc(sq_used, 1)
                elif name == "kk":
                    dve.wait_ge(bdec_ready, h + 1)
                    for gg in range(3):
                        A.wait_done(dve, h, f"kk{gg}")
                        dve.tensor_tensor(span(bmat, gg), psum(A, f"kk{gg}", gg), span(bdec, gg), ALU.mult).then_inc(A.sem(f"kk{gg}"), 1)
                elif name == "qk":
                    for gg in range(3):
                        A.wait_done(dve, h, f"qk{gg}")
                        dve.tensor_tensor(span(aqk[p], gg), psum(A, f"qk{gg}", gg), span(dec, gg), ALU.mult).then_inc(A.sem(f"qk{gg}"), 1)
                elif name == "kt":
                    for gg in range(3):
                        t0, n = GROUPS_OF_TILES[gg]
                        r = rows(t0)
                        A.wait_done(dve, h, f"kt{gg}")
                        dve.tensor_tensor(kdec[p][0:r, t0:t0 + n, :], A.ps(f"kt{gg}")[0:r, 0:n * P].rearrange("p (t d) -> p t d", d=P),
                                          per_row(tok[p][0:r, 3, t0:t0 + n]), ALU.mult).then_inc(A.sem(f"kt{gg}"), 1)
                    dve.wait_ge(v_loaded, h * 16 + 16)
                    dve.tensor_copy(v_tail[p][:, :], v[:, NT * P:T]).then_inc(v_tail_ready, 1)
                    dve.wait_ge(qd_ready, h + 1)
                    A.wait_done(dve, h, "vt1")
                    dve.wait_ge(v_tail_ready, h + 1)
                    dve.sem_inc(a_inputs_used, 1)
                elif name == "zero":
                    dve.wait_ge(bk_ready, h * LEVELS + 1)
                    b0 = bk[:, 0, :]
                    dve.tensor_tensor(full(x_inv[p]), over_tiles(ident[:, :]), full(b0), ALU.subtract)
                    dve.tensor_tensor(tail(x_inv[p]), ident[0:TAIL, 0:TAIL], tail(b0), ALU.subtract).then_inc(x_started, 1)
                    for gg in range(3):
                        t0, n = GROUPS_OF_TILES[gg]
                        eye = over_tiles(ident[:, :], n) if gg < 2 else ident[0:TAIL, 0:TAIL]
                        split = (lambda a: a.rearrange("p (t i) -> p t i", i=P)) if gg < 2 else (lambda a: a)
                        A.wait_done(dve, h, f"T0{gg}")
                        dve.tensor_tensor(split(span(w_inv, gg)), eye, split(psum(A, f"T0{gg}", gg)), ALU.subtract).then_inc(A.sem(f"T0{gg}"), 1)
                    dve.wait_ge(x_started, h + 1)
                elif name == "X":
                    A.wait_done(dve, h, f"T{k}{g}" if k < LEVELS - 1 else f"X{k}{g}")
                    dve.tensor_tensor(span(x_inv[p], g), span(x_inv[p], g), psum(A, f"X{k}{g}", g),
                                      ALU.subtract).then_inc(A.sem(f"X{k}{g}"), 1)
                    if k < LEVELS - 1:
                        dve.tensor_tensor(span(w_inv, g), span(w_inv, g), psum(A, f"T{k}{g}", g),
                                          ALU.subtract).then_inc(A.sem(f"T{k}{g}"), 1)

            def stage_b(step, h, p):
                name, t, _ = step
                tk = tok[p]
                if name == "ks":
                    if t == 0:
                        dve.memset(state[:, 0, :], 0.0).then_inc(st_zeroed, 1)
                        A.wait_read(dve, h, "vt0")
                        A.wait_read(dve, h, "vt1")
                    B.wait_done(dve, h, f"ks{t}")
                    dve.scalar_tensor_tensor(resid[:, :], B.ps(f"ks{t}")[:, 0:P], tk[:, 2, t:t + 1], v_tok[p][:, t, :],
                                             ALU.mult, ALU.add).then_inc(B.sem(f"ks{t}"), 1)
                elif name == "nu":
                    B.wait_done(dve, h, f"nu{t}")
                    dve.tensor_scalar(nu[:, :], B.ps(f"nu{t}")[:, P:2 * P], tk[:, 1, t:t + 1], None, ALU.mult).then_inc(B.sem(f"nu{t}"), 1)
                elif name == "ds":
                    B.wait_done(dve, h, f"ds{t}")
                    dve.scalar_tensor_tensor(state[:, 0, :], state[:, 0, :], eg[p][:, t * P + P - 1:t * P + P],
                                             B.ps(f"ds{t}")[:, 2 * P:3 * P], ALU.mult, ALU.add).then_inc(B.sem(f"ds{t}"), 1)
                elif name == "tail1":
                    B.wait_done(dve, h, "ks8")
                    dve.tensor_tensor(resid_t[:, :], B.ps("ks8")[:, 0:TAIL], eg[p][:, NT * P:T], ALU.mult).then_inc(r_scaled, 1)
                    dve.wait_ge(r_scaled, h + 1)
                    dve.tensor_tensor(resid_t[:, :], v_tail[p][:, :], resid_t[:, :], ALU.subtract).then_inc(B.sem("ks8"), 1)
                elif name == "tail3":
                    B.wait_done(dve, h, "nu8")
                    dve.tensor_scalar(nu[0:TAIL, :], B.ps("nu8")[0:TAIL, 2 * P:3 * P], tk[0:TAIL, 1, NT:NT + 1], None, ALU.mult) \
                        .then_inc(B.sem("nu8"), 1)
                    B.wait_read(dve, h, "nu8")
                    dve.tensor_tensor(nu_seg[:, :, :], nu[0:TAIL, :].unsqueeze(1).broadcast_to([TAIL, NSEG, P]),
                                      per_row(const("segment", TAIL)), ALU.mult).then_inc(nu_seg_ready, 1)
                elif name == "tail4":
                    dve.wait_ge(st_stored, h * 32 + 32)
                    last = eg[p][:, NT * P + PT_TAIL - 1:T:LS]
                    dve.tensor_tensor(st_out[:, :, :], state[:, :, :], per_row(last), ALU.mult).then_inc(st_scaled, 1)
                    dve.wait_ge(st_scaled, h + 1)
                    for u in range(3):
                        B.wait_done(dve, h, f"ds8_{u}")
                        dve.tensor_tensor(st_out[:, 3 * u:3 * u + 3, :], st_out[:, 3 * u:3 * u + 3, :],
                                          B.ps(f"ds8_{u}")[:, 0:3 * P].rearrange("p (a b) -> p a b", b=P), ALU.add).then_inc(B.sem(f"ds8_{u}"), 1)
                elif name == "out2":
                    dve.wait_ge(o_rooted, h + 1)
                    dve.scalar_tensor_tensor(o[p][:, :], o[p][:, :], gn[:, 0:1], o_sq[:, :], ALU.mult, ALU.mult).then_inc(o_scaled, 1)
                    dve.wait_ge(o_scaled, h + 1)
                    dve.wait_ge(z_loaded, h * 16 + 16)
                    dve.tensor_tensor(o[p][:, :], o[p][:, :], z[:, :], ALU.mult).then_inc(y_ready, 1)
                    dve.wait_ge(y_ready, h + 1)
                    dve.sem_inc(b_inputs_used, 1)

            heads(dve, stage_a, stage_b)


def merge_outputs(nc, x, rstd, ones, eps_col, ident, w_a, w_b, w_o, scratch, sc_tail, gc_tail, prompt_sconv, sample_sconv, prompt_gconv,
                  sample_gconv):
    with ExitStack() as ctx:
        s = Scope(nc, ctx, "mrg")
        y_hi = s.sb("y_hi", [P, KC, T], F32R)
        y_lo = s.sb("y_lo", [P, KC, T], F32R)
        merged = s.sb("merged", [P, KC, T])
        w = WeightStream(s, 2)
        y_raw = s.sb("y_raw", [P, 2, T])
        sig = s.sb("sig", [P, 2, T])
        t_rows = s.sb("tail_rows", [(1 + NS) * (GC_T - 1), 2, 4 * P])
        bank = [s.ps(f"bank{k}", [P, 512]) for k in range(8)]
        nrm = NextNorm(s, rstd, ones, eps_col, y_raw[:, 0, :])
        x_final = s.sem("x_final")
        bank_free = [s.sem(f"bank_free{k}") for k in range(6)]
        unit_done = s.sem("unit_done")
        y_loaded = [s.sem(f"y_loaded{k}") for k in range(2)]
        sig_loaded = [s.sem(f"sig_loaded{k}") for k in range(2)]
        y_hi_done, y_ready, sig_used, merged_done = s.sem("y_hi_done"), s.sem("y_ready"), s.sem("sig_used"), s.sem("merged_done")
        t_turned, t_copied = s.sem("t_turned"), s.sem("t_copied")
        t_stored = [s.sem(f"t_stored{k}") for k in range(2)]
        block = s.block()
        weights = (w_a, w_b, w_o)
        jobs = [("gc", c) for c in range(0, 3 * H, 4)] + [("sc", c) for c in range(0, KC, 4)]

        @block.sync
        def _(sp):
            def loads(r, i):
                for j in range(2):
                    w.load(sp, i, 2, KC * r + j, weights[r][:, bass.ds(i * (2 * P) + j * P, P)].rearrange("(k p) n -> p k n", p=P))

            def load_y(r, c):
                if r or c >= 2:
                    sp.wait_ge(y_ready, KC * r + c - 1)
                sp.dma_start(y_raw[:, c % 2, :], scratch["y_a" if r == 0 else "y_b"][c]).then_inc(y_loaded[c % 2], 16)

            load_y(0, 0)
            load_y(0, 1)
            loads(0, 0)
            for c in range(2, KC):
                load_y(0, c)
            for r in range(3):
                def gates(i):
                    for j in range(2):
                        sp.wait_ge(sig_used, i * 2 + (KC * r + j + 1))
                        sp.dma_start(sig[:, j, :], scratch["sig_a" if r == 0 else "sig_b"][bass.ds(i * 2 + j, 1)]
                                     .rearrange("c p t -> p (c t)")).then_inc(sig_loaded[j], 16)
                with sp.Fori(0, KC // 2 - 1) as i:
                    if r < 2:
                        gates(i)
                    for j in range(2):
                        w.load(sp, i, 2, KC * r + 2 + j,
                               weights[r][:, bass.ds(i * (2 * P) + (2 + j) * P, P)].rearrange("(k p) n -> p k n", p=P))
                if r < 2:
                    gates(KC // 2 - 1)
                    if r == 0:
                        for c in range(2):
                            load_y(1, c)
                    loads(r + 1, 0)
                    if r == 0:
                        for c in range(2, KC):
                            load_y(1, c)

        @block.gpsimd
        def _(pool):
            w.credit_raw(pool)
            nrm.clear(pool)
            with pool.Fori(0, KC) as i:
                for j in range(2):
                    w.split_lo(pool, i, 2, j)
            for j in range(2):
                w.split_lo(pool, 0, 2, 2 * KC + j)
            with pool.Fori(0, KC // 2 - 1) as i:
                for j in range(2):
                    w.split_lo(pool, i, 2, 2 * KC + 2 + j)
                    for b in range(NB):
                        nrm.add(pool, i, 2 * NB, NB * j + b)
            for n in range(NB * (KC - 2), NB * KC):
                nrm.add(pool, 0, 0, n)

        @block.tensor
        def _(pe):
            w.credit_split(pe)
            for k in range(6):
                pe.sem_inc(bank_free[k], 1)
            for n, (which, c) in enumerate(jobs):
                src = gc_tail if which == "gc" else sc_tail
                if n >= 2:
                    pe.wait_ge(t_copied, n - 1)
                for k in range(4):
                    mm = pe.transpose(bank[6 + n % 2][0:src.shape[2], k * P:(k + 1) * P], src[:, c + k, :], ident[:, :])
                mm.then_inc(t_turned, 1)
            for r in range(3):
                pe.wait_ge(y_ready, KC * (r + 1))
                with pe.Fori(0, KC // 2) as i:
                    for j in range(2):
                        n = KC * r + j
                        pe.wait_ge(w.lo_done, i * 2 + (n + 1))
                        for b in range(NB):
                            pe.wait_ge(bank_free[3 * j + b], i + (KC // 2 * r + 1))
                            for k in range(KC):
                                mm = three_passes(pe, bank[3 * j + b][:, 0:TH], w.hi[:, j, k, :], w.lo[:, j, k, :],
                                                  y_hi[:, k, third(b)], y_lo[:, k, third(b)], k == 0, k == KC - 1)
                            mm.then_inc(unit_done, 1)
                            if b == 1:
                                pe.wait_ge(unit_done, i * 6 + (3 * n + 1))
                                pe.sem_inc(w.split_free, 1)
            for b in range(NB):
                pe.wait_ge(bank_free[b], 3 * KC // 2 + 1)
                nrm.sum(pe, bank[b][:, 0:TH], b)

        @block.scalar
        def _(act):
            w.split_hi(act, 0, 2, 0)
            for n, (which, c) in enumerate(jobs):
                act.wait_ge(t_turned, n + 1)
                if n >= 2:
                    act.wait_ge(t_stored[n % 2], 32 * (n // 2))
                rows = (gc_tail if which == "gc" else sc_tail).shape[2]
                act.copy(t_rows[0:rows, n % 2, :], bank[6 + n % 2][0:rows, :]).then_inc(t_copied, 1)
                act.wait_ge(t_copied, n + 1)
                g = (GC_T if which == "gc" else SC_T) - 1
                p_out, s_out = (prompt_gconv, sample_gconv) if which == "gc" else (prompt_sconv, sample_sconv)
                act.dma_start(p_out[0, 0][:, c * P:(c + 4) * P], t_rows[0:g, n % 2, :]).then_inc(t_stored[n % 2], 16)
                act.dma_start(s_out[0][:, :, c * P:(c + 4) * P].rearrange("s t c -> (s t) c"),
                              t_rows[g:(1 + NS) * g, n % 2, :]).then_inc(t_stored[n % 2], 16)
            for r in range(3):
                for c in range(KC):
                    if r and c == 0:
                        act.wait_ge(unit_done, 3 * KC * r)
                    if r < 2:
                        act.wait_ge(y_loaded[c % 2], 16 * (KC // 2 * r + c // 2 + 1))
                    else:
                        act.wait_ge(merged_done, 2 * NB * KC)
                    act.copy(y_hi[:, c, :], y_raw[:, c % 2, :] if r < 2 else merged[:, c, :]).then_inc(y_hi_done, 1)
                if r < 2:
                    with act.Fori(0, KC // 2) as i:
                        for j in range(2):
                            w.split_hi(act, i, 2, KC * r + j + 1)

            def squares(i, j):
                for b in range(NB):
                    act.wait_ge(x_final, i * 6 + (NB * j + b + 1))
                    nrm.square(act, x[:, bass.ds(i * 2 + j, 1), third(b)].rearrange("p o t -> p (o t)"), i, 6, NB * j + b)

            w.split_hi(act, 0, 2, 2 * KC + 1)
            with act.Fori(0, KC // 2 - 1) as i:
                for j in range(2):
                    w.split_hi(act, i, 2, 2 * KC + 2 + j)
                    squares(i, j)
            for j in range(2):
                squares(KC // 2 - 1, j)
            nrm.factors(act, lambda b: bank[b][:, 0:TH])
            for k in range(2):
                act.wait_ge(t_stored[k], 16 * len(jobs))

        @block.vector
        def _(dve):
            dve.sem_inc(sig_used, 2)
            for r in range(3):
                for c in range(KC):
                    dve.wait_ge(y_hi_done, KC * r + c + 1)
                    dve.tensor_tensor(y_lo[:, c, :], y_raw[:, c % 2, :] if r < 2 else merged[:, c, :],
                                      y_hi[:, c, :].bitcast(F32), ALU.subtract).then_inc(y_ready, 1)
                with dve.Fori(0, KC // 2) as i:
                    for j in range(2):
                        if r < 2:
                            dve.wait_ge(sig_loaded[j], i * 16 + 16 * (KC // 2 * r + 1))
                        for b in range(NB):
                            dve.wait_ge(unit_done, i * 6 + (3 * (KC * r + j) + b + 1))
                            ps = bank[3 * j + b][:, 0:TH]
                            m = merged[:, bass.ds(i * 2 + j, 1), third(b)].rearrange("p o t -> p (o t)")
                            xc = x[:, bass.ds(i * 2 + j, 1), third(b)].rearrange("p o t -> p (o t)")
                            g = sig[:, j, third(b)]
                            if r == 0:
                                dve.tensor_tensor(m, ps, g, ALU.mult).then_inc(bank_free[3 * j + b], 1)
                                dve.wait_ge(bank_free[3 * j + b], i + 2)
                                dve.sem_inc(merged_done, 1)
                            elif r == 1:
                                dve.tensor_tensor(g, ps, g, ALU.mult).then_inc(bank_free[3 * j + b], 1)
                                dve.wait_ge(bank_free[3 * j + b], i + (KC // 2 + 2))
                                dve.tensor_tensor(m, m, g, ALU.add).then_inc(merged_done, 1)
                            else:
                                dve.tensor_tensor(xc, ps, xc, ALU.add).then_inc(x_final, 1)
                                dve.wait_ge(x_final, i * 6 + (NB * j + b + 1))
                                dve.sem_inc(bank_free[3 * j + b], 1)
                        if r < 2:
                            dve.wait_ge(merged_done, i * 6 + (3 * (KC * r + j) + NB))
                            dve.sem_inc(sig_used, 1)


def build(nc, c, out):
    scratch = {}
    for name, shape in (("y_a", (KC, P, T)), ("y_b", (H, P, T)), ("qkv", (3, H, P, T)), ("z", (H, P, T)),
                        ("sig_a", (KC, P, T)), ("sig_b", (KC, P, T))):
        scratch[name] = nc.dram_tensor(f"scratch_{name}", shape, F32, kind="Internal").ap()
    with ExitStack() as ctx:
        s = Scope(nc, ctx, "g")
        x = s.sb("x", [P, KC, T])
        ident = s.sb("ident", [P, P])
        ones = s.sb("ones", [P, P])
        gains = s.sb("gains", [P, 4, KC])
        taps = s.sb("taps", [P, KC * SC_T + 3 * H * GC_T])
        eps = s.sb("eps", [P, 1])
        sc_hist = s.sb("sc_hist", [P, KC, NS * (SC_T - 1)])
        gc_hist = s.sb("gc_hist", [P, 3 * H, NS * (GC_T - 1)])
        sc_tail = s.sb("sc_tail", [P, KC, NSEG * (SC_T - 1)])
        gc_tail = s.sb("gc_tail", [P, 3 * H, NSEG * (GC_T - 1)])
        ab_rows = s.sb("ab_rows", [2 * H, T])
        eps_col = eps[:, 0:1]
        with nc.sbuf_tensor("rstd_1", [P, T], F32) as rstd:
            transpose_inputs(nc, c, x, rstd, ident, ones, eps, gains, taps, sc_hist, gc_hist)
            ffn(nc, "ffn1", x, rstd, gains, 0, ones[:, :], eps_col, c["ffn1_w_gate"][0], c["ffn1_w_up"][0], c["ffn1_w_down"][0])
            input_projections(nc, x, rstd, gains, c["w_in"][0],
                              taps[:, 0:KC * SC_T].rearrange("p (c t) -> p c t", t=SC_T),
                              taps[:, KC * SC_T:].rearrange("p (c t) -> p c t", t=GC_T),
                              sc_hist, gc_hist, sc_tail, gc_tail, ab_rows, scratch)
        delta_rule(nc, ones[:, :], ident, eps_col, c["delta_consts"], c["head_params"], c["g_norm"], ab_rows,
                   c["state_gdn"], scratch, out["prompt_gdn"], out["sample_gdn"])
        with nc.sbuf_tensor("rstd_2", [P, T], F32) as rstd:
            merge_outputs(nc, x, rstd, ones[:, :], eps_col, ident, c["w_a_out"][0], c["w_b_out"][0], c["w_o"][0], scratch,
                          sc_tail, gc_tail, out["prompt_sconv"], out["sample_sconv"], out["prompt_gdn_conv"],
                          out["sample_gdn_conv"])
            ffn(nc, "ffn2", x, rstd, gains, 2, ones[:, :], eps_col, c["ffn2_w_gate"][0], c["ffn2_w_up"][0], c["ffn2_w_down"][0])
            final_output(nc, x, rstd, gains, 3, ident, out["y_prompt"], out["y_sample"])


OUTPUTS = {
    "y_prompt": (1, SEQ, D), "y_sample": (NS, LS, D), "prompt_sconv": (1, 1, SC_T - 1, D),
    "prompt_gdn_conv": (1, 1, GC_T - 1, QKV), "prompt_gdn": (1, 1, H, P, P), "sample_sconv": (1, NS, SC_T - 1, D),
    "sample_gdn_conv": (1, NS, GC_T - 1, QKV), "sample_gdn": (1, NS, H, P, P),
}


def laid_out(inputs):
    a = {name: np.ascontiguousarray(v) for name, v in inputs.items()}

    def features_first(v):
        v = v.reshape(-1, v.shape[-1] // P, P).transpose(2, 1, 0)
        return v

    gains = [features_first(a.pop(n)).reshape(P, KC) for n in ("norm_ffn1", "norm_mix", "norm_ffn2", "norm_final")]
    taps = [features_first(a.pop(n)).reshape(P, -1) for n in ("sconv_w", "gdn_conv_w")]
    a["gains"] = np.concatenate(gains, 1)
    a["taps"] = np.concatenate(taps, 1)
    empty = np.zeros((1, H), np.float32)
    a["head_params"] = np.concatenate([np.stack([a.pop("gdn_dt_bias")[0], a.pop("gdn_a_log")[0]], 1),
                                       np.concatenate([empty, empty]).T], 0)
    a["g_norm"] = a.pop("gdn_norm").reshape(P, 1)
    a["delta_consts"] = delta_constants()
    a["identity"] = np.eye(P, dtype=np.float32)
    return a


def kernel(**inputs):
    from concourse import bacc
    from concourse.bass_utils import run_bass_kernel_spmd

    nc = bacc.Bacc("TRN2", target_bir_lowering=False, num_devices=1)
    arrays, args = {}, {}
    for name, a in laid_out(inputs).items():
        arrays[f"in_{name}"] = np.ascontiguousarray(a)
        args[name] = nc.dram_tensor(f"in_{name}", a.shape, F32, kind="ExternalInput").ap()
    outs = {n: nc.dram_tensor(f"out_{n}", shape, F32, kind="ExternalOutput").ap() for n, shape in OUTPUTS.items()}
    build(nc, args, outs)
    r = run_bass_kernel_spmd(nc, [arrays], core_ids=[0])
    return tuple(r.results[0][f"out_{n}"] for n in OUTPUTS)
```

```python
from contextlib import ExitStack

import numpy as np
import concourse.bass as bass
from concourse import mybir

F32 = mybir.dt.float32
F32R = mybir.dt.float32r
ALU = mybir.AluOpType
ACT = mybir.ActivationFunctionType

P = 128
D = 1024
KC = D // P
FF = 2816
N_META = 16
SEQ = 1024
NS = 8
LS = 8
H = 8
PT = N_META + SEQ
T = PT + NS * LS
TH = T // 3
NB = 3
EPS = 1e-6
SC_T = 3
GC_T = 4
QKV = 3 * H * P
COL_B, COL_C, COL_X = 0, D, 2 * D
COL_QKV = 3 * D
COL_AB = COL_QKV + QKV
COL_Z = COL_AB + 2 * H
COL_GA = COL_Z + D
COL_GB = COL_GA + D
NT = T // P
TAIL = T - NT * P
NSEG = 1 + NS
PT_TAIL = PT - NT * P
LEVELS = 7
TAIL_LEVELS = 4


class Chain:

    def __init__(self, sem, base=0, turn=0, per=0):
        self.sem, self.base, self.turn, self.per, self.n = sem, base, turn, per, 0

    def link(self, eng, ins):
        ins.then_inc(self.sem, 1)
        self.n += 1
        eng.wait_ge(self.sem, self.turn * self.per + (self.base + self.n))

    def end(self):
        assert self.per in (0, self.n), (self.per, self.n)
        return self.base + self.n


class Scope:

    def __init__(self, nc, ctx, phase):
        self.nc, self.ctx, self.phase, self.sems = nc, ctx, phase, []

    def sb(self, name, shape, dt=F32):
        return self.ctx.enter_context(self.nc.sbuf_tensor(f"{self.phase}_{name}", shape, dt))

    def ps(self, name, shape):
        return self.ctx.enter_context(self.nc.psum_tensor(f"{self.phase}_{name}", shape, F32))

    def sem(self, name):
        handle = self.ctx.enter_context(self.nc.semaphore(f"{self.phase}_{name}"))
        self.sems.append(handle.num)
        return handle

    def block(self):
        self.ctx.callback(self.clear)
        return self.ctx.enter_context(self.nc.Block())

    def clear(self):
        numbers = sorted(self.sems)
        while numbers:
            first = last = numbers.pop(0)
            while numbers and numbers[0] == last + 1:
                last = numbers.pop(0)
            self.nc.gpsimd.sem_clear(range(first, last + 1))
        self.nc.all_engine_barrier()


def third(b):
    return slice(b * TH, (b + 1) * TH)


class WeightStream:

    def __init__(self, s, slots):
        self.slots = slots
        self.raw = s.sb("w_raw", [P, slots, KC, P])
        self.hi = s.sb("w_hi", [P, slots, KC, P], F32R)
        self.lo = s.sb("w_lo", [P, slots, KC, P], F32R)
        self.raw_loaded = [s.sem(f"w_raw_loaded{k}") for k in range(slots)]
        self.raw_free = s.sem("w_raw_free")
        self.hi_done = s.sem("w_hi_done")
        self.lo_done = s.sem("w_lo_done")
        self.split_free = s.sem("w_split_free")

    def load(self, sp, i, per, j, src, shape=None):
        sp.wait_ge(self.raw_free, i * per + (j + 1))
        k = j % self.slots
        dst = self.raw[:, k, :, :]
        if shape is not None:
            dst = dst.rearrange("p k n -> p (k n)").rearrange("p (a b) -> p a b", a=shape)
        sp.dma_start(dst, src).then_inc(self.raw_loaded[k], 16)

    def split_hi(self, act, i, per, j):
        k = j % self.slots
        act.wait_ge(self.raw_loaded[k], i * (16 * per // self.slots) + 16 * (j // self.slots + 1))
        act.wait_ge(self.split_free, i * per + (j + 1))
        act.activation(self.hi[:, k, :, :], self.raw[:, k, :, :], ACT.Copy).then_inc(self.hi_done, 1)

    def split_lo(self, pool, i, per, j):
        k = j % self.slots
        pool.wait_ge(self.hi_done, i * per + (j + 1))
        pool.tensor_tensor(self.lo[:, k, :, :], self.raw[:, k, :, :], self.hi[:, k, :, :].bitcast(F32),
                           ALU.subtract).then_inc(self.lo_done, 1)
        pool.wait_ge(self.lo_done, i * per + (j + 1))
        pool.sem_inc(self.raw_free, 1)

    def credit_raw(self, pool):
        pool.sem_inc(self.raw_free, self.slots)

    def credit_split(self, pe):
        pe.sem_inc(self.split_free, self.slots - 1)


def three_passes(pe, out, w_hi, w_lo, x_hi, x_lo, first, last):
    pe.matmul(out, w_hi, x_hi, start=first, stop=False)
    pe.matmul(out, w_hi, x_lo, start=False, stop=False)
    return pe.matmul(out, w_lo, x_hi, start=False, stop=last)


def transpose_inputs(nc, c, x, rstd, ident, ones, eps, gains, taps, sc_hist, gc_hist):
    x_prompt, x_sample, meta = c["x_prompt"], c["x_sample"], c["meta_tokens"]
    state_sconv, state_gdn_conv = c["state_sconv"], c["state_gdn_conv"]
    with ExitStack() as ctx:
        s = Scope(nc, ctx, "tr")
        NJ = 9
        rows = s.sb("rows", [P, 3, D])
        hist = s.sb("hist", [P, QKV + D])
        sq = s.sb("sq", [P, 2, KC, P])
        ps = [s.ps(f"ps{k}", [P, 4, P]) for k in range(4)]
        sums = [s.ps(f"sums{k}", [P, 4, P]) for k in range(3)]
        rows_loaded = [s.sem(f"rows_loaded{k}") for k in range(3)]
        ident_loaded, hist_loaded, tables_loaded = s.sem("ident_loaded"), s.sem("hist_loaded"), s.sem("tables_loaded")
        turned = s.sem("turned")
        vec_out, act_out = s.sem("vec_out"), s.sem("act_out")
        squared, summed, logged = s.sem("squared"), s.sem("summed"), s.sem("logged")
        consts_set = s.sem("consts_set")
        NHIST = (QKV + D) // P
        tail_rows = N_META + NS * LS
        block = s.block()

        @block.sync
        def _(sp):
            sp.dma_start(ident[:], c["identity"]).then_inc(ident_loaded, 16)
            for j in range(NJ):
                if j >= 3:
                    sp.wait_ge(turned, 2 * (j - 2))
                if j < 8:
                    sp.dma_start(rows[:, j % 3, :], x_prompt[0, j * P:(j + 1) * P, :]).then_inc(rows_loaded[j % 3], 16)
                else:
                    sp.dma_start(rows[0:N_META, j % 3, :], meta).then_inc(rows_loaded[j % 3], 16)
                    sp.dma_start(rows[N_META:tail_rows, j % 3, :],
                                 x_sample.rearrange("b t d -> (b t) d")).then_inc(rows_loaded[j % 3], 16)
            sp.dma_start(hist[0:NS * (GC_T - 1), 0:QKV],
                         state_gdn_conv[0].rearrange("s t c -> (s t) c")).then_inc(hist_loaded, 16)
            sp.dma_start(hist[0:NS * (SC_T - 1), QKV:QKV + D],
                         state_sconv[0].rearrange("s t c -> (s t) c")).then_inc(hist_loaded, 16)
            sp.dma_start(gains[:, :, :], c["gains"].rearrange("p (a k) -> p a k", a=4)).then_inc(tables_loaded, 16)
            sp.dma_start(taps[:, :], c["taps"]).then_inc(tables_loaded, 16)
            sp.wait_ge(tables_loaded, 32)

        @block.tensor
        def _(pe):
            def tile_sums(j):
                n = P if j < 8 else tail_rows
                pe.wait_ge(consts_set, 2)
                pe.wait_ge(squared, j + 1)
                for k in range(KC):
                    mm = pe.matmul(sums[j // 4][:, j % 4, 0:n], ones[:, :], sq[:, j % 2, k, 0:n], start=(k == 0), stop=(k == KC - 1))
                mm.then_inc(summed, 1)

            pe.wait_ge(ident_loaded, 16)
            for j in range(NJ):
                n = P if j < 8 else tail_rows
                pe.wait_ge(rows_loaded[j % 3], 16 * (j // 3 + 1) + (16 if j == 8 else 0))
                for hf in range(2):
                    q = 2 * j + hf
                    if q >= 4:
                        pe.wait_ge(vec_out if hf == 0 else act_out, (q - 4) // 2 + 1)
                    for c in range(4):
                        k = 4 * hf + c
                        mm = pe.transpose(ps[q % 4][:, c, 0:n], rows[0:n, j % 3, k * P:(k + 1) * P], ident[0:n, 0:n])
                    mm.then_inc(turned, 1)
                if j:
                    tile_sums(j - 1)
            tile_sums(NJ - 1)
            pe.wait_ge(hist_loaded, 32)
            for g in range(NHIST // 4):
                q = 2 * NJ + g
                pe.wait_ge(vec_out if q % 2 == 0 else act_out, (q - 4) // 2 + 1)
                n = NS * (GC_T - 1) if g < 6 else NS * (SC_T - 1)
                for c in range(4):
                    k = 4 * g + c
                    mm = pe.transpose(ps[q % 4][:, c, 0:n], hist[0:n, k * P:(k + 1) * P], ident[0:n, 0:n])
                mm.then_inc(turned, 1)

        def copies(eng, odd, done):
            copy = eng.copy if odd else eng.tensor_copy
            for q in range(odd, 2 * NJ + NHIST // 4, 2):
                eng.wait_ge(turned, q + 1)
                b = ps[q % 4]
                if q < 2 * NJ:
                    j, k = q // 2, 4 * (q % 2)
                    if j < 8:
                        copy(x[:, k:k + 4, N_META + j * P:N_META + (j + 1) * P], b[:, :, :]).then_inc(done, 1)
                    else:
                        copy(x[:, k:k + 4, 0:N_META], b[:, :, 0:N_META])
                        copy(x[:, k:k + 4, PT:T], b[:, :, N_META:tail_rows]).then_inc(done, 1)
                elif q < 2 * NJ + 6:
                    g = q - 2 * NJ
                    copy(gc_hist[:, 4 * g:4 * g + 4, :], b[:, :, 0:NS * (GC_T - 1)]).then_inc(done, 1)
                else:
                    g = q - 2 * NJ - 6
                    copy(sc_hist[:, 4 * g:4 * g + 4, :], b[:, :, 0:NS * (SC_T - 1)]).then_inc(done, 1)

        @block.vector
        def _(dve):
            dve.memset(ones[:, :], 1.0).then_inc(consts_set, 1)
            dve.memset(eps[:, :], EPS).then_inc(consts_set, 1)
            copies(dve, 0, vec_out)

        @block.gpsimd
        def _(pool):
            for j in range(NJ):
                pool.wait_ge(vec_out, j + 1)
                pool.wait_ge(act_out, j + 1)
                if j >= 2:
                    pool.wait_ge(summed, j - 1)
                if j < 8:
                    cols = x[:, :, N_META + j * P:N_META + (j + 1) * P]
                    pool.tensor_tensor(sq[:, j % 2, :, :], cols, cols, ALU.mult).then_inc(squared, 1)
                else:
                    pool.tensor_tensor(sq[:, j % 2, :, 0:N_META], x[:, :, 0:N_META], x[:, :, 0:N_META], ALU.mult)
                    pool.tensor_tensor(sq[:, j % 2, :, N_META:tail_rows], x[:, :, PT:T], x[:, :, PT:T],
                                       ALU.mult).then_inc(squared, 1)

        @block.scalar
        def _(act):
            copies(act, 1, act_out)
            act.wait_ge(consts_set, 2)
            act.wait_ge(summed, NJ)
            log = {"func": ACT.Ln, "bias": eps[:, 0:1], "scale": 1.0 / D}
            for g in range(2):
                at = N_META + 4 * P * g
                act.activation(rstd[:, at:at + 4 * P], sums[g][:, :, :].rearrange("p a b -> p (a b)"), **log)
            act.activation(rstd[:, 0:N_META], sums[2][:, 0, 0:N_META], **log)
            act.activation(rstd[:, PT:T], sums[2][:, 0, N_META:tail_rows], **log).then_inc(logged, 1)
            act.wait_ge(logged, 1)
            act.activation(rstd[:, :], rstd[:, :], ACT.Exp, scale=-0.5)


class NextNorm:

    def __init__(self, s, rstd, ones, eps_col, sq):
        self.rstd, self.ones, self.eps_col, self.sq = rstd, ones, eps_col, sq
        self.squared = s.sem("nrm_squared")
        self.added = s.sem("nrm_added")
        self.summed = s.sem("nrm_summed")
        self.logged = s.sem("nrm_logged")
        self.factor = s.sem("nrm_factor")

    def clear(self, pool):
        pool.memset(self.rstd[:, :], 0.0).then_inc(self.added, NB)

    def square(self, act, x_part, i, per, n):
        act.wait_ge(self.added, i * per + (n + 1))
        act.activation(self.sq[:, third(n % NB)], x_part, ACT.Square).then_inc(self.squared, 1)

    def add(self, pool, i, per, n):
        pool.wait_ge(self.squared, i * per + (n + 1))
        pool.wait_ge(self.added, i * per + (n + 1))
        part = third(n % NB)
        pool.tensor_tensor(self.rstd[:, part], self.rstd[:, part], self.sq[:, part], ALU.add).then_inc(self.added, 1)

    def sum(self, pe, out, b):
        pe.wait_ge(self.added, NB * KC + b + 1)
        pe.matmul(out, self.ones, self.rstd[:, third(b)], start=True, stop=True).then_inc(self.summed, 1)

    def factors(self, act, ps):
        for b in range(NB):
            act.wait_ge(self.summed, b + 1)
            act.activation(self.rstd[:, third(b)], ps(b), ACT.Ln, bias=self.eps_col, scale=1.0 / D).then_inc(self.logged, 1)
        for b in range(NB):
            act.wait_ge(self.logged, b + 1)
            act.activation(self.rstd[:, third(b)], self.rstd[:, third(b)], ACT.Exp, scale=-0.5).then_inc(self.factor, 1)


def ffn(nc, name, x, rstd, gains, g_at, ones, eps_col, w_gate, w_up, w_down):
    GROUPS = FF // (2 * P)
    TURNS = (GROUPS - 1) // 2
    PER = 6
    with ExitStack() as ctx:
        s = Scope(nc, ctx, name)
        h_hi = s.sb("h_hi", [P, KC, T], F32R)
        h_lo = s.sb("h_lo", [P, KC, T], F32R)
        mid_hi = s.sb("mid_hi", [P, 2, 2, T], F32R)
        mid_lo = s.sb("mid_lo", [P, 2, 2, T], F32R)
        w = WeightStream(s, 3)
        hid = s.sb("hid", [P, 2, T])
        bank = [s.ps(f"bank{k}", [P, 512]) for k in range(6)]
        nrm = NextNorm(s, rstd, ones, eps_col, hid[:, 0, :])
        bank_free = [s.sem(f"bank_free{k}") for k in range(6)]
        h_scaled, h_hi_done, h_ready = s.sem("h_scaled"), s.sem("h_hi_done"), s.sem("h_ready")
        gu_done, down_done = s.sem("gu_done"), s.sem("down_done")
        mid_hi_done, mid_ready, x_final = s.sem("mid_hi_done"), s.sem("mid_ready"), s.sem("x_final")
        block = s.block()
        TURN = 12

        def first_block(par):
            return 0 if par == 0 else 4 + PER * (par - 1)

        def gu_use(par, a):
            return a if par == 0 else 6 * par - 4 + a

        @block.sync
        def _(sp):
            def gate_up(i, par):
                for a in range(2):
                    for q, src in enumerate((w_gate, w_up)):
                        w.load(sp, i, TURN, first_block(par) + 2 * a + q,
                               src[:, bass.ds(i * (4 * P) + (2 * par + a) * P, P)].rearrange("(k p) n -> p k n", p=P))

            def down(i, par, j0):
                for a in range(2):
                    w.load(sp, i, TURN, j0 + a,
                           w_down[bass.ds(i * (4 * P) + (2 * par + a) * P, P), :].rearrange("p (k n) -> p k n", n=P))

            gate_up(0, 0)
            with sp.Fori(0, TURNS) as i:
                for par in (1, 2):
                    gate_up(i, par)
                    down(i, par - 1, first_block(par) + 4)
            down(TURNS, 0, 4)

        @block.gpsimd
        def _(pool):
            w.credit_raw(pool)
            for j in range(4):
                w.split_lo(pool, 0, TURN, j)
            with pool.Fori(0, TURNS) as i:
                for j in range(4, 4 + TURN):
                    w.split_lo(pool, i, TURN, j)
            for j in (4, 5):
                w.split_lo(pool, TURNS, TURN, j)
            pool.wait_ge(h_ready, KC)
            nrm.clear(pool)
            for n in range(NB * KC):
                nrm.add(pool, 0, 0, n)

        @block.tensor
        def _(pe):
            w.credit_split(pe)
            for k in range(6):
                pe.sem_inc(bank_free[k], 1)

            pe.wait_ge(w.lo_done, 2)
            for k6 in range(6):
                pe.wait_ge(bank_free[k6], 1)
            for k in range(KC):
                pe.wait_ge(h_ready, k + 1)
                for k6 in range(6):
                    q, b = divmod(k6, NB)
                    mm = three_passes(pe, bank[k6][:, 0:TH], w.hi[:, q, k, :], w.lo[:, q, k, :],
                                      h_hi[:, k, third(b)], h_lo[:, k, third(b)], k == 0, k == KC - 1)
                    if k == KC - 1:
                        mm.then_inc(gu_done, 1)
            pe.wait_ge(gu_done, 4)
            pe.sem_inc(w.split_free, 1)

            def gate_up(i, par):
                for j in range(2 if par == 0 else 0, 4):
                    a, q = divmod(j, 2)
                    n = first_block(par) + j
                    pe.wait_ge(w.lo_done, i * TURN + (n + 1))
                    for b in range(NB):
                        k6 = 3 * q + b
                        pe.wait_ge(bank_free[k6], i * TURN + (gu_use(par, a) + 1))
                        for k in range(KC):
                            mm = three_passes(pe, bank[k6][:, 0:TH], w.hi[:, n % 3, k, :], w.lo[:, n % 3, k, :],
                                              h_hi[:, k, third(b)], h_lo[:, k, third(b)], k == 0, k == KC - 1)
                        mm.then_inc(gu_done, 1)
                        if b == 1:
                            pe.wait_ge(gu_done, i * 24 + (12 * par + 3 * j + 1))
                            pe.sem_inc(w.split_free, 1 if j else 2)

            def down(i, par, n, use, after):
                m = par % 2
                pe.wait_ge(w.lo_done, i * TURN + (n + 2))
                pe.wait_ge(mid_ready, i * 12 + (6 * par + 6))
                for c in range(KC):
                    for b in range(NB):
                        k6 = 3 * (c % 2) + b
                        pe.wait_ge(bank_free[k6], i * TURN + (use + c // 2 + 1))
                        for a in range(2):
                            mm = three_passes(pe, bank[k6][:, 0:TH], w.hi[:, (n + a) % 3, c, :],
                                              w.lo[:, (n + a) % 3, c, :], mid_hi[:, m, a, third(b)],
                                              mid_lo[:, m, a, third(b)], a == 0, a == 1)
                        mm.then_inc(down_done, 1)
                        if after and c == 0 and b == 0:
                            pe.wait_ge(gu_done, i * 24 + 12 * (par + 2))
                            pe.sem_inc(w.split_free, 1)

            gate_up(0, 0)
            with pe.Fori(0, TURNS) as i:
                gate_up(i, 1)
                down(i, 0, first_block(1) + 4, 4, True)
                gate_up(i, 2)
                down(i, 1, first_block(2) + 4, 10, True)
            pe.wait_ge(down_done, 24 * 2 * TURNS)
            pe.sem_inc(w.split_free, 2)
            down(TURNS, 0, 4, 2, False)
            for b in range(NB):
                pe.wait_ge(bank_free[b], TURNS * TURN + 2 + KC // 2 + 1)
                nrm.sum(pe, bank[b][:, 0:TH], b)

        @block.scalar
        def _(act):
            w.split_hi(act, 0, TURN, 0)
            w.split_hi(act, 0, TURN, 1)
            for k in range(KC):
                act.wait_ge(h_scaled, k + 1)
                act.copy(h_hi[:, k, :], hid[:, k % 2, :]).then_inc(h_hi_done, 1)

            def gate_up(i, par):
                n = first_block(par)
                for a in range(2):
                    if par or a:
                        w.split_hi(act, i, TURN, n + 2 * a + 1)
                    for b in range(NB):
                        act.wait_ge(gu_done, i * 24 + (12 * par + 6 * a + b + 1))
                        if par == 0:
                            act.wait_ge(h_ready, KC)
                        else:
                            act.wait_ge(mid_ready, i * 12 + (6 * (par - 1) + 3 * a + b + 1))
                        act.activation(hid[:, a, third(b)], bank[b][:, 0:TH], ACT.Silu).then_inc(bank_free[b], 1)
                    w.split_hi(act, i, TURN, n + 2 * a + 2)
                    for b in range(NB):
                        act.wait_ge(bank_free[3 + b], i * TURN + (gu_use(par, a) + 2))
                        act.copy(mid_hi[:, par % 2, a, third(b)], hid[:, a, third(b)]).then_inc(mid_hi_done, 1)

            gate_up(0, 0)
            with act.Fori(0, TURNS) as i:
                for par in (1, 2):
                    gate_up(i, par)
                    w.split_hi(act, i, TURN, first_block(par) + 5)
                    w.split_hi(act, i, TURN, first_block(par) + 6)
            w.split_hi(act, TURNS, TURN, 5)
            act.wait_ge(mid_ready, TURNS * 12 + 6)
            for n in range(NB * KC):
                c, b = divmod(n, NB)
                act.wait_ge(x_final, n + 1)
                nrm.square(act, x[:, c, third(b)], 0, 0, n)
            nrm.factors(act, lambda b: bank[b][:, 0:TH])

        @block.vector
        def _(dve):
            for k in range(KC):
                if k >= 2:
                    dve.wait_ge(h_ready, k - 1)
                dve.scalar_tensor_tensor(hid[:, k % 2, :], x[:, k, :], gains[:, g_at, k:k + 1], rstd[:, :],
                                         ALU.mult, ALU.mult).then_inc(h_scaled, 1)
                dve.wait_ge(h_hi_done, k + 1)
                dve.tensor_tensor(h_lo[:, k, :], hid[:, k % 2, :], h_hi[:, k, :].bitcast(F32),
                                  ALU.subtract).then_inc(h_ready, 1)

            def gate_up(i, par):
                for a in range(2):
                    for b in range(NB):
                        dve.wait_ge(gu_done, i * 24 + (12 * par + 6 * a + 3 + b + 1))
                        dve.wait_ge(bank_free[b], i * TURN + (gu_use(par, a) + 2))
                        dve.tensor_tensor(hid[:, a, third(b)], bank[3 + b][:, 0:TH], hid[:, a, third(b)],
                                          ALU.mult).then_inc(bank_free[3 + b], 1)
                        dve.wait_ge(mid_hi_done, i * 12 + (6 * par + 3 * a + b + 1))
                        dve.tensor_tensor(mid_lo[:, par % 2, a, third(b)], hid[:, a, third(b)],
                                          mid_hi[:, par % 2, a, third(b)].bitcast(F32),
                                          ALU.subtract).then_inc(mid_ready, 1)

            def down(i, par, last=False):
                for c in range(KC):
                    for b in range(NB):
                        k6 = 3 * (c % 2) + b
                        dve.wait_ge(down_done, i * 48 + (24 * par + 3 * c + b + 1))
                        ins = dve.scalar_tensor_tensor(x[:, c, third(b)], bank[k6][:, 0:TH], 0.5, x[:, c, third(b)],
                                                       ALU.mult, ALU.add)
                        if last:
                            ins.then_inc(x_final, 1)
                            dve.wait_ge(x_final, NB * c + b + 1)
                            dve.sem_inc(bank_free[k6], 1)
                        else:
                            ins.then_inc(bank_free[k6], 1)

            gate_up(0, 0)
            with dve.Fori(0, TURNS) as i:
                gate_up(i, 1)
                down(i, 0)
                gate_up(i, 2)
                down(i, 1)
            down(TURNS, 0, last=True)


def final_output(nc, x, rstd, gains, g_at, ident, y_prompt, y_sample):
    with ExitStack() as ctx:
        s = Scope(nc, ctx, "fin")
        y = s.sb("y", [P, KC, T])
        rows = s.sb("rows", [P, 3, D])
        bank = [s.ps(f"bank{k}", [P, 512]) for k in range(6)]
        scaled, turned = s.sem("scaled"), s.sem("turned")
        vec_out, act_out, stored = s.sem("vec_out"), s.sem("act_out"), [s.sem(f"stored{k}") for k in range(3)]
        block = s.block()
        NJ = 9

        @block.tensor
        def _(pe):
            for q in range(2 * NJ):
                j, k = q // 2, 4 * (q % 2)
                n = P if j < 8 else NS * LS
                if q < 2:
                    pe.wait_ge(scaled, 4 * (q + 1))
                if q >= 6:
                    pe.wait_ge(vec_out if q % 2 == 0 else act_out, (q - 6) // 2 + 1)
                for c in range(4):
                    mm = pe.transpose(bank[q % 6][0:n, c * P:(c + 1) * P],
                                      y[:, k + c, N_META + j * P:N_META + j * P + n], ident[:, :])
                mm.then_inc(turned, 1)

        def copies(eng, odd, done):
            copy = eng.copy if odd else eng.tensor_copy
            for q in range(odd, 2 * NJ, 2):
                j = q // 2
                n = P if j < 8 else NS * LS
                eng.wait_ge(turned, q + 1)
                if j >= 3:
                    eng.wait_ge(stored[j % 3], 16 * (j // 3))
                copy(rows[0:n, j % 3, 512 * odd:512 * odd + 512], bank[q % 6][0:n, :]).then_inc(done, 1)

        @block.scalar
        def _(act):
            copies(act, 1, act_out)

        @block.vector
        def _(dve):
            for k in range(KC):
                dve.scalar_tensor_tensor(y[:, k, :], x[:, k, :], gains[:, g_at, k:k + 1], rstd[:, :],
                                         ALU.mult, ALU.mult).then_inc(scaled, 1)
            copies(dve, 0, vec_out)

        @block.sync
        def _(sp):
            for j in range(NJ):
                sp.wait_ge(vec_out, j + 1)
                sp.wait_ge(act_out, j + 1)
                if j < 8:
                    sp.dma_start(y_prompt[0, j * P:(j + 1) * P, :], rows[:, j % 3, :]).then_inc(stored[j % 3], 16)
                else:
                    sp.dma_start(y_sample.rearrange("b t d -> (b t) d"),
                                 rows[0:NS * LS, j % 3, :]).then_inc(stored[j % 3], 16)
            for k in range(3):
                sp.wait_ge(stored[k], 16 * (NJ // 3))


def input_projections(nc, x, rstd, gains, w_in, sc_taps, gc_taps, sc_hist, gc_hist, sc_tail, gc_tail,
                      ab_rows, scratch):
    GP, SPD = GC_T - 1, SC_T - 1
    GL = GP + PT + NS * (GP + LS)
    SL = SPD + PT + NS * (SPD + LS)
    with ExitStack() as ctx:
        s = Scope(nc, ctx, "inp")
        h_hi = s.sb("h_hi", [P, KC, T], F32R)
        h_lo = s.sb("h_lo", [P, KC, T], F32R)
        w = WeightStream(s, 3)
        pre = s.sb("pre", [P, 3, GL])
        conv = s.sb("conv", [P, 3, GL])
        out = s.sb("out", [P, 3, T])
        sc_w = s.sb("sc_w", [P, SC_T])
        gc_w = s.sb("gc_w", [P, 3, GC_T])
        bank = [s.ps(f"bank{k}", [P, 512]) for k in range(3)]
        bank_free = [s.sem(f"bank_free{k}") for k in range(3)]
        unit_done = s.sem("unit_done")
        h_scaled, h_hi_done, h_ready = s.sem("h_scaled"), s.sem("h_hi_done"), s.sem("h_ready")
        stored = [s.sem(f"stored{k}") for k in range(3)]
        y_ready, conv_done, silu_done = s.sem("y_ready"), s.sem("conv_done"), s.sem("silu_done")
        zsig_done, z_ready, pads_zero = s.sem("zsig_done"), s.sem("z_ready"), s.sem("pads_zero")
        vec = s.sem("vec")
        block = s.block()
        NBLK = 72
        cols = lambda n0, i: w_in[:, bass.ds(n0 + i * P, P)].rearrange("(k p) n -> p k n", p=P)

        @block.sync
        def _(sp):
            for k in range(3):
                sp.sem_inc(stored[k], 16)

            def loads(loop, i, ahead):
                starts = ((COL_B, COL_C, COL_X), (COL_QKV, COL_QKV + D, COL_QKV + 2 * D), (COL_Z, COL_GA, COL_GB))
                for j in range(3):
                    w.load(sp, i, 3, 24 * loop + 3 * ahead + j, cols(starts[loop][j] + ahead * P, i))

            def store_y(i):
                sp.wait_ge(y_ready, i + 2)
                sp.dma_start(scratch["y_a"][bass.ds(i, 1)].rearrange("c p t -> p (c t)"), out[:, 0, :]).then_inc(stored[0], 16)

            def store_qkv(i):
                for j in range(3):
                    sp.wait_ge(silu_done, i * 3 + (j + 1 + 3))
                    sp.dma_start(scratch["qkv"][j][bass.ds(i, 1)].rearrange("c p t -> p (c t)"), out[:, j, :]).then_inc(stored[j], 16)

            def store_gates(i):
                sp.wait_ge(z_ready, i * 3 + 6)
                sp.dma_start(scratch["z"][bass.ds(i, 1)].rearrange("c p t -> p (c t)"), out[:, 0, :]).then_inc(stored[0], 16)
                for j, name in ((1, "sig_a"), (2, "sig_b")):
                    sp.wait_ge(bank_free[2], i * 3 + (48 + j + 2))
                    sp.dma_start(scratch[name][bass.ds(i, 1)].rearrange("c p t -> p (c t)"), out[:, j, :]).then_inc(stored[j], 16)

            loads(0, 0, 0)
            for loop, store in enumerate((store_y, store_qkv, store_gates)):
                with sp.Fori(0, KC - 1) as i:
                    loads(loop, i, 1)
                    store(i)
                if loop < 2:
                    loads(loop + 1, 0, 0)
                else:
                    w.load(sp, 0, 3, NBLK, cols(COL_AB, 0))
                store(KC - 1)
            for k in range(3):
                sp.wait_ge(stored[k], 16 * (1 + (3 if k == 0 else 2) * KC))

        @block.gpsimd
        def _(pool):
            w.credit_raw(pool)
            with pool.Fori(0, NBLK // 3) as i:
                for j in range(3):
                    w.split_lo(pool, i, 3, j)
            w.split_lo(pool, 0, 3, NBLK)

        @block.tensor
        def _(pe):
            w.credit_split(pe)
            for b in range(NB):
                pe.sem_inc(bank_free[b], 1)

            def project(i, j):
                pe.wait_ge(w.lo_done, i * 3 + (j + 1))
                for b in range(NB):
                    pe.wait_ge(bank_free[b], i * 3 + (j + 1))
                    for k in range(KC):
                        mm = three_passes(pe, bank[b][:, 0:TH], w.hi[:, j % 3, k, :], w.lo[:, j % 3, k, :],
                                          h_hi[:, k, third(b)], h_lo[:, k, third(b)], k == 0, k == KC - 1)
                    mm.then_inc(unit_done, 1)
                    if b == 1:
                        pe.wait_ge(unit_done, i * 9 + (3 * j + 1))
                        pe.sem_inc(w.split_free, 1)

            pe.wait_ge(w.lo_done, 1)
            for b in range(NB):
                pe.wait_ge(bank_free[b], 1)
            for k in range(KC):
                pe.wait_ge(h_ready, k + 1)
                for b in range(NB):
                    mm = three_passes(pe, bank[b][:, 0:TH], w.hi[:, 0, k, :], w.lo[:, 0, k, :],
                                      h_hi[:, k, third(b)], h_lo[:, k, third(b)], k == 0, k == KC - 1)
                    if k == KC - 1:
                        mm.then_inc(unit_done, 1)
            with pe.Fori(0, NBLK // 3) as i:
                for j in range(3):
                    project(i, j + 1)

        @block.scalar
        def _(act):
            w.split_hi(act, 0, 3, 0)
            for k in range(KC):
                act.wait_ge(h_scaled, k + 1)
                act.copy(h_hi[:, k, :], out[:, k % 2, :]).then_inc(h_hi_done, 1)
            act.wait_ge(h_ready, KC)

            def unit(i, n, b):
                act.wait_ge(unit_done, i * 9 + (3 * n + b + 1))
                return bank[b][:, 0:TH]

            with act.Fori(0, KC) as i:
                for j in range(2):
                    w.split_hi(act, i, 3, j + 1)
                    if j == 0:
                        act.wait_ge(y_ready, i + 1)
                    for b in range(NB):
                        src = unit(i, j, b)
                        act.copy(conv[:, 1 + j, third(b)], src).then_inc(bank_free[b], 1)
                w.split_hi(act, i, 3, 3)
            act.wait_ge(y_ready, KC + 1)

            with act.Fori(0, H) as i:
                def silu(j):
                    act.wait_ge(conv_done, i * 3 + (j + 1 + 3))
                    act.wait_ge(stored[j], i * 16 + (16 + (16 * KC if j == 0 else 0)))
                    act.activation(out[:, j, 0:PT], conv[:, j, 0:PT], ACT.Silu)
                    act.activation(out[:, j, PT:T].rearrange("p (s l) -> p s l", l=LS),
                                   conv[:, j, GP + PT:GL].rearrange("p (s l) -> p s l", l=GP + LS)[:, :, 0:LS],
                                   ACT.Silu).then_inc(silu_done, 1)

                for j in range(3):
                    n = 24 + j
                    w.split_hi(act, i, 3, n + 1)
                    act.wait_ge(conv_done, i * 3 + (j + 1))
                    for b in range(NB):
                        src = unit(i, n, b)
                        if b < 2:
                            act.copy(pre[:, j, GP + b * TH:GP + (b + 1) * TH], src).then_inc(bank_free[b], 1)
                        else:
                            act.copy(pre[:, j, GP + 2 * TH:GP + PT], src[:, 0:PT - 2 * TH])
                            act.copy(pre[:, j, GP + PT:GL].rearrange("p (s l) -> p s l", l=GP + LS)[:, :, GP:],
                                     src[:, PT - 2 * TH:TH].rearrange("p (s l) -> p s l", l=LS)).then_inc(bank_free[b], 1)
                    if j:
                        silu(j - 1)
                silu(2)

            with act.Fori(0, KC) as i:
                for j in range(3):
                    n = 48 + j
                    w.split_hi(act, i, 3, n + 1)
                    if j:
                        act.wait_ge(stored[j], i * 16 + 16 * (1 + KC))
                    for b in range(NB):
                        src = unit(i, n, b)
                        if j == 0:
                            act.wait_ge(z_ready, i * 3 + (b + 1))
                            act.activation(conv[:, 0, third(b)], src, ACT.Sigmoid).then_inc(zsig_done, 1)
                        else:
                            act.activation(out[:, j, third(b)], src, ACT.Sigmoid).then_inc(bank_free[b], 1)
            for b in range(NB):
                src = unit(0, NBLK, b)
                act.copy(ab_rows[:, third(b)], src[0:2 * H, :]).then_inc(bank_free[b], 1)

        @block.vector
        def _(dve):
            dve.memset(pre[:, :, 0:GP], 0.0).then_inc(pads_zero, 1)
            dve.sem_inc(conv_done, 3)
            dve.sem_inc(silu_done, 3)
            dve.sem_inc(z_ready, 3)
            dve.sem_inc(y_ready, 1)
            for k in range(KC):
                if k >= 2:
                    dve.wait_ge(h_ready, k - 1)
                dve.scalar_tensor_tensor(out[:, k % 2, :], x[:, k, :], gains[:, 1, k:k + 1], rstd[:, :],
                                         ALU.mult, ALU.mult).then_inc(h_scaled, 1)
                dve.wait_ge(h_hi_done, k + 1)
                dve.tensor_tensor(h_lo[:, k, :], out[:, k % 2, :], h_hi[:, k, :].bitcast(F32),
                                  ALU.subtract).then_inc(h_ready, 1)
            dve.wait_ge(pads_zero, 1)

            cx = pre[:, 0, GP - SPD:GP - SPD + SL]
            cx_sample = cx[:, SPD + PT:SL].rearrange("p (s l) -> p s l", l=SPD + LS)
            with dve.Fori(0, KC) as i:
                ch = Chain(vec, 0, i, 6)
                dve.tensor_copy(cx_sample[:, :, 0:SPD],
                                sc_hist[:, bass.ds(i, 1), :].rearrange("p o (s t) -> p (o s) t", t=SPD))
                ch.link(dve, dve.tensor_copy(sc_w[:, :], sc_taps[:, bass.ds(i, 1), :].rearrange("p o t -> p (o t)")))
                for b in range(NB):
                    dve.wait_ge(unit_done, i * 9 + (6 + b + 1))
                    dve.wait_ge(bank_free[b], i * 3 + 3)
                    if b < 2:
                        dve.tensor_tensor(cx[:, SPD + b * TH:SPD + (b + 1) * TH], bank[b][:, 0:TH],
                                          conv[:, 2, third(b)], ALU.mult).then_inc(bank_free[b], 1)
                    else:
                        dve.tensor_tensor(cx[:, SPD + 2 * TH:SPD + PT], bank[b][:, 0:PT - 2 * TH],
                                          conv[:, 2, 2 * TH:PT], ALU.mult)
                        dve.tensor_tensor(cx_sample[:, :, SPD:], bank[b][:, PT - 2 * TH:TH].rearrange("p (s l) -> p s l", l=LS),
                                          conv[:, 2, PT:T].rearrange("p (s l) -> p s l", l=LS),
                                          ALU.mult).then_inc(bank_free[b], 1)
                dve.wait_ge(bank_free[2], i * 3 + 4)
                W = SL - SPD
                ch.link(dve, dve.tensor_scalar(conv[:, 0, 0:W], cx[:, 0:W], sc_w[:, 0:1], None, ALU.mult))
                for t in range(1, SC_T):
                    ch.link(dve, dve.scalar_tensor_tensor(conv[:, 0, 0:W], cx[:, t:t + W], sc_w[:, t:t + 1],
                                                          conv[:, 0, 0:W], ALU.mult, ALU.add))
                dve.tensor_copy(sc_tail[:, bass.ds(i, 1), 0:SPD].rearrange("p o t -> p (o t)"), cx[:, PT:PT + SPD])
                ch.link(dve, dve.tensor_copy(sc_tail[:, bass.ds(i, 1), SPD:].rearrange("p o (s t) -> p (o s) t", t=SPD),
                                             cx_sample[:, :, LS:]))
                dve.wait_ge(stored[0], i * 16 + 16)
                ch.link(dve, dve.tensor_tensor(out[:, 0, 0:PT], conv[:, 0, 0:PT], conv[:, 1, 0:PT], ALU.mult))
                dve.tensor_tensor(out[:, 0, PT:T].rearrange("p (s l) -> p s l", l=LS),
                                  conv[:, 0, SPD + PT:SL].rearrange("p (s l) -> p s l", l=SPD + LS)[:, :, 0:LS],
                                  conv[:, 1, PT:T].rearrange("p (s l) -> p s l", l=LS), ALU.mult).then_inc(y_ready, 1)
                ch.end()
            base = ch.per * KC

            with dve.Fori(0, H) as i:
                ch = Chain(vec, base, i, 1 + 3 * GC_T)
                ch.link(dve, dve.tensor_copy(gc_w[:, :, :], gc_taps.rearrange("p (j h) t -> p j h t", h=H)[:, :, bass.ds(i, 1), :]
                                             .rearrange("p j o t -> p j (o t)")))
                for j in range(3):
                    row = pre[:, j, :]
                    row_sample = pre[:, j, GP + PT:GL].rearrange("p (s l) -> p s l", l=GP + LS)
                    dve.wait_ge(conv_done, i * 3 + (j + 3))
                    dve.tensor_copy(row_sample[:, :, 0:GP],
                                    gc_hist[:, bass.ds(i + j * H, 1), :].rearrange("p o (s t) -> p (o s) t", t=GP)).then_inc(pads_zero, 1)
                    dve.wait_ge(pads_zero, i * 3 + (j + 2))
                    dve.wait_ge(bank_free[2], i * 3 + (24 + j + 2))
                    dve.wait_ge(silu_done, i * 3 + (j + 1))
                    W = GL - GP
                    ch.link(dve, dve.tensor_scalar(conv[:, j, 0:W], row[:, 0:W], gc_w[:, j, 0:1], None, ALU.mult))
                    for t in range(1, GC_T):
                        ch.link(dve, dve.scalar_tensor_tensor(conv[:, j, 0:W], row[:, t:t + W], gc_w[:, j, t:t + 1],
                                                              conv[:, j, 0:W], ALU.mult, ALU.add))
                    tail = gc_tail[:, bass.ds(i + j * H, 1), :]
                    dve.tensor_copy(tail[:, :, 0:GP].rearrange("p o t -> p (o t)"), row[:, PT:PT + GP])
                    dve.tensor_copy(tail[:, :, GP:].rearrange("p o (s t) -> p (o s) t", t=GP),
                                    row_sample[:, :, LS:]).then_inc(conv_done, 1)
                ch.end()

            with dve.Fori(0, KC) as i:
                for b in range(NB):
                    dve.wait_ge(zsig_done, i * 3 + (b + 1))
                    if b == 0:
                        dve.wait_ge(stored[0], i * 16 + 16 * (1 + 2 * KC))
                    dve.tensor_tensor(out[:, 0, third(b)], bank[b][:, 0:TH], conv[:, 0, third(b)],
                                      ALU.mult).then_inc(z_ready, 1)
                    dve.wait_ge(z_ready, i * 3 + (b + 1 + 3))
                    dve.sem_inc(bank_free[b], 1)


class Units:

    def __init__(self, s, label, order, banks):
        self.order = order
        self.banks = banks
        self.at = {name: k for k, (name, _) in enumerate(order)}
        self.per = len(order)
        self.bank_per = [sum(b == k for _, b in order) for k in range(len(banks))]
        self.use = {name: sum(b == bank for _, b in order[:k]) for k, (name, bank) in enumerate(order)}
        self.done = s.sem(f"{label}_done")
        self.free = [s.sem(f"{label}_bank{k}_free") for k in range(len(banks))]

    def ps(self, name):
        return self.banks[self.order[self.at[name]][1]]

    def sem(self, name):
        return self.free[self.order[self.at[name]][1]]

    def wait_bank(self, pe, h, name):
        b = self.order[self.at[name]][1]
        pe.wait_ge(self.free[b], h * self.bank_per[b] + (self.use[name] + 1))

    def wait_done(self, eng, h, name):
        eng.wait_ge(self.done, h * self.per + (self.at[name] + 1))

    def wait_read(self, eng, h, name):
        b = self.order[self.at[name]][1]
        eng.wait_ge(self.free[b], h * self.bank_per[b] + (self.use[name] + 2))


CONST_COLS = {}
_at = 0
for _name, _width in (("upto", P), ("upto_tail", TAIL), ("after", P), ("after_tail", TAIL), ("level", LEVELS * P),
                      ("segment", NSEG)):
    CONST_COLS[_name] = (_at, _width)
    _at += _width
CONST_W = _at


def delta_constants():
    t = np.zeros((P, CONST_W), np.float32)
    m, i = np.arange(P)[:, None], np.arange(P)[None, :]
    seg = np.where(np.arange(TAIL) < PT_TAIL, 0, 1 + (np.arange(TAIL) - PT_TAIL) // LS)
    same = seg[:, None] == seg[None, :]
    mt, it = m[:TAIL], i[:, :TAIL]

    def put(name, a):
        t[:a.shape[0], CONST_COLS[name][0]:CONST_COLS[name][0] + a.shape[1]] = a

    put("upto", m <= i)
    put("upto_tail", (mt <= it) & same)
    put("after", m > i)
    put("after_tail", (mt > it) & same)
    put("level", np.concatenate([(m >> (k + 1) == i >> (k + 1)) & (m >> k & 1 == 0) & (i >> k & 1 == 1)
                                 for k in range(LEVELS)], 1))
    put("segment", seg[:, None] == np.arange(NSEG)[None, :])
    return t


GROUPS_OF_TILES = ((0, 4), (4, 4), (8, 1))


def delta_rule(nc, ones, ident, eps_col, consts_in, head_params, g_norm, ab_rows, state_in, scratch, prompt_state,
               sample_state):
    with ExitStack() as ctx:
        s = Scope(nc, ctx, "dr")
        con = s.sb("con", [P, CONST_W])
        hp = s.sb("head_params", [2 * H, 2])
        gn = s.sb("g_norm", [P, 1])

        def const(name, n=P):
            a, width = CONST_COLS[name]
            return con[0:n, a:a + width]

        level = const("level").rearrange("p (k i) -> p k i", i=P)
        per_token = s.sb("per_token", [P, 4, NT + 1, H])
        na = s.sb("neg_rate", [2 * H, 1])
        tok = [s.sb(f"tok{p}", [P, 4, NT + 1]) for p in range(2)]
        q = s.sb("q", [P, T])
        k_raw = s.sb("k_raw", [P, T])
        v = s.sb("v", [P, T])
        k_t = s.sb("k", [P, T])
        k_tail = [s.sb(f"k_tail{p}", [P, TAIL]) for p in range(2)]
        v_tail = [s.sb(f"v_tail{p}", [TAIL, P]) for p in range(2)]
        z = s.sb("z", [P, T])
        sq = s.sb("sq", [P, 2, T])
        lu = s.sb("lu", [P, T])
        dec = s.sb("dec", [P, T])
        bdec = s.sb("bdec", [P, T])
        raw = [buf[0:2 * H, :] for buf in (sq[:, 0, :], sq[:, 1, :], lu, dec)]
        bmat = s.sb("bmat", [P, T])
        bk = s.sb("bk", [P, 2, T])
        w_inv = s.sb("w_inv", [P, T])
        y_lev = s.sb("y_lev", [P, T])
        keg = y_lev[:, 0:NT * P].rearrange("p (t d) -> p t d", d=P)
        x_inv = s.sb("x_inv", [P, T])
        x_tail = [s.sb(f"x_tail{p}", [TAIL, TAIL]) for p in range(2)]
        eg = [s.sb(f"eg{p}", [P, T]) for p in range(2)]
        qd = [s.sb(f"qd{p}", [P, T]) for p in range(2)]
        aqk = [s.sb(f"aqk{p}", [P, T]) for p in range(2)]
        kdec = [s.sb(f"kdec{p}", [P, (NT + 1), P]) for p in range(2)]
        v_tok = s.sb("v_tok", [P, NT, P])
        u_beta = [s.sb(f"u_beta{p}", [P, NT, P]) for p in range(2)]
        w_t = [s.sb(f"w_t{p}", [P, NT * P]) for p in range(2)]
        state = s.sb("state", [P, NSEG, P])
        SPREAD = TAIL + LS
        late_k = s.sb("late_k", [P, NSEG * P])
        late_q = s.sb("late_q", [P, NSEG * P])
        st_out = late_q[:, :].rearrange("p (a b) -> p a b", b=P)
        k_seg, q_seg = [buf[:, 0:NSEG * TAIL].rearrange("p (a b) -> p a b", b=TAIL) for buf in (late_k, late_q)]
        resid = s.sb("resid", [TAIL, P])
        o_tok = s.sb("o_tok", [TAIL, P])
        nu = s.sb("nu", [P, P])
        nu_seg = late_k[0:TAIL, :].rearrange("p (a b) -> p a b", b=P)
        o = [s.sb(f"o{p}", [P, T]) for p in range(2)]
        o_sq = late_k[:, 0:T]

        level_steps = []
        a_names = [f"{name}{g}" for name in ("eg", "kk", "qk", "kt") for g in range(3)]
        a_names += ["vt0", "vt1", "vt2", "T00", "T01", "T02"]
        for k in range(1, LEVELS):
            gs = range(3 if k < TAIL_LEVELS else 2)
            level_steps += [("Y", k, g) for g in gs] + [("X", k, g) for g in gs]
            a_names += [f"Y{k}{g}" for g in gs]
            for g in gs:
                a_names += [f"X{k}{g}"] + ([f"T{k}{g}"] if k < LEVELS - 1 else [])
        a_names += [f"{name}{g}" for name in ("kw", "u", "w") for g in range(2)]
        A = Units(s, "a", [(n, k % 4) for k, n in enumerate(a_names)], [s.ps(f"a_bank{k}", [P, 512]) for k in range(4)])
        N = Units(s, "n", [(f"{name}{g}", 0) for name in ("dec", "sq", "sk") for g in range(3)], [s.ps("n_bank", [P, 512])])
        a_steps = [(("scale", 0, 0), 4), (("kk", 0, 0), 4), (("qk", 0, 0), 3), (("kt", 0, 0), 4), (("zero", 0, 0), 4)]
        a_steps += [(step, 1) for step in level_steps]
        a_steps += [((name, 0, g), 1) for name in ("kw", "u", "w") for g in range(2)]
        b_steps = [((name, t, 0), 3) for t in range(NT) for name in ("ks", "ds")]
        b_steps += [((f"tail{k}", 0, 0), 4) for k in range(1, 5)] + [(("out1", 0, 0), 9), (("out2", 0, 0), 9)]

        n_steps = [("lu", 0, 0), ("square", 0, 0), ("square", 0, 1)] + [("dec", 0, g) for g in range(3)]
        n_steps += [("mask", 0, 0), ("mask_beta", 0, 0)]
        n_steps += [(name, 0, b) for name in ("sq", "sk") for b in range(NB)]

        def starts(stage, steps):
            whole = sum(share for _, share in steps)
            return [(sum(share for _, share in steps[:k]) / whole, stage, step) for k, (step, _) in enumerate(steps)]

        TURN = sorted(starts("a", a_steps) + starts("b", b_steps)
                      + [(0.40 + 0.03 * k, "n", step) for k, step in enumerate(n_steps)])
        order = [step[0] for _, _, step in TURN]
        assert order.index("kt") < order.index("lu")
        b_order = []
        for t in range(NT):
            b_order += [(f"ks{t}", 0), (f"ds{t}", 0), (f"o{t}", 1 + t % 2)]
        b_order += [("ks8", 0), ("nu8", 0), ("ot8", 1), ("o8", 1), ("ds8_0", 0), ("ds8_1", 2), ("ds8_2", 0),
                    ("on0", 1), ("on1", 2), ("on2", 0)]
        B = Units(s, "b", b_order, [s.ps(f"b_bank{k}", [P, 512]) for k in range(3)])

        cons_loaded, prep = s.sem("cons_loaded"), s.sem("prep")
        prep_act, prep_pe, vec = s.sem("prep_act"), s.sem("prep_pe"), s.sem("vec")
        qk_loaded, v_loaded, z_loaded, st_loaded = s.sem("qk_loaded"), s.sem("v_loaded"), s.sem("z_loaded"), s.sem("st_loaded")
        a_inputs_used, b_inputs_used = s.sem("a_inputs_used"), s.sem("b_inputs_used")
        lu_ready, sq_ready, factor = s.sem("lu_ready"), s.sem("sq_ready"), s.sem("factor")
        qk_ready, dec_masked, bdec_ready, qd_ready = s.sem("qk_ready"), s.sem("dec_masked"), s.sem("bdec_ready"), s.sem("qd_ready")
        bk_ready, tok_ready, tails_ready, x_started = s.sem("bk_ready"), s.sem("tok_ready"), s.sem("tails_ready"), s.sem("x_started")
        x_tail_ready = s.sem("x_tail_ready")
        st_zeroed, segs_zeroed, segs_ready, nu_seg_ready, st_scaled = s.sem("st_zeroed"), s.sem("segs_zeroed"), s.sem("segs_ready"), s.sem("nu_seg_ready"), s.sem("st_scaled")
        o_sq_ready, o_rooted, o_scaled, y_ready = s.sem("o_sq_ready"), s.sem("o_rooted"), s.sem("o_scaled"), s.sem("y_ready")
        y_stored, st_stored = s.sem("y_stored"), s.sem("st_stored")
        block = s.block()

        def tile(t):
            return slice(t * P, min(t * P + P, T))

        def rows(t):
            return P if t < NT else TAIL

        def span(buf, g):
            t0, n = GROUPS_OF_TILES[g]
            return buf[0:rows(t0), t0 * P:min((t0 + n) * P, T)]

        def full(buf):
            return buf[:, 0:NT * P].rearrange("p (t i) -> p t i", i=P)

        def tail(buf):
            return buf[0:TAIL, NT * P:T]

        def psum(units, name, g):
            t0, n = GROUPS_OF_TILES[g]
            return units.ps(name)[0:rows(t0), 0:(n * P if t0 < NT else TAIL)]

        def halves(a, k, bit):
            return a.rearrange("p (a two b) -> p a two b", two=2, b=1 << k)[:, :, bit, :]

        def half_psum(name, k, g):
            t0, n = GROUPS_OF_TILES[g]
            r = rows(t0)
            return A.ps(name)[0:r, 0:n * r // 2].rearrange("p (a b) -> p a b", b=1 << k)

        def over_tiles(a, n=NT):
            return a.unsqueeze(1).broadcast_to([P, n, P])

        def per_row(a, width=P):
            return a.unsqueeze(2).broadcast_to([a.shape[0], a.shape[1], width])

        @block.sync
        def _(sp):
            sp.dma_start(con[:, :], consts_in).then_inc(cons_loaded, 16)
            sp.dma_start(hp[:, :], head_params).then_inc(cons_loaded, 16)
            sp.dma_start(gn[:, :], g_norm).then_inc(cons_loaded, 16)

            def load_a(h):
                sp.wait_ge(a_inputs_used, h + 1)
                for j, buf in ((0, q), (1, k_raw), (2, v)):
                    sp.dma_start(buf[:, :], scratch["qkv"][j][bass.ds(h, 1)].rearrange("c p t -> p (c t)")) \
                        .then_inc(v_loaded if j == 2 else qk_loaded, 16)

            def load_b(h):
                sp.wait_ge(b_inputs_used, h + 1)
                sp.dma_start(z[:, :], scratch["z"][bass.ds(h, 1)].rearrange("c p t -> p (c t)")).then_inc(z_loaded, 16)
                sp.dma_start(state[:, 1:NSEG, :], state_in[0][:, bass.ds(h, 1)].rearrange("s o k v -> k (s o) v")).then_inc(st_loaded, 16)

            def store(h, p):
                sp.wait_ge(y_ready, h + 1)
                sp.dma_start(scratch["y_b"][bass.ds(h, 1)].rearrange("c p t -> p (c t)"), o[p][:, :]).then_inc(y_stored, 16)
                sp.dma_start(prompt_state[0, 0, bass.ds(h, 1)].rearrange("o k v -> k (o v)"), st_out[:, 0, :]).then_inc(st_stored, 16)
                sp.dma_start(sample_state[0][:, bass.ds(h, 1)].rearrange("s o k v -> k (s o) v"), st_out[:, 1:NSEG, :]).then_inc(st_stored, 16)

            sp.sem_inc(y_stored, 32)
            sp.sem_inc(st_stored, 32)
            load_a(0)
            load_b(0)
            load_a(1)
            with sp.Fori(0, H // 2 - 1) as i:
                for p in range(2):
                    h = i * 2 + p
                    load_a(h + 2)
                    store(h, p)
                    load_b(h + 1)
            store(H - 2, 0)
            load_b(H - 1)
            store(H - 1, 1)
            sp.wait_ge(y_stored, 16 * (2 + H))
            sp.wait_ge(st_stored, 32 * (1 + H))

        def heads(eng, stages):
            def turn(heads_of):
                for _, stage, step in TURN:
                    if stage in heads_of:
                        h, p = heads_of[stage]
                        stages[stage](step, h, p)

            turn({"n": (0, 0)})
            turn({"n": (1, 1), "a": (0, 0)})
            with eng.Fori(0, H // 2 - 1) as i:
                turn({"n": (i * 2 + 2, 0), "a": (i * 2 + 1, 1), "b": (i * 2, 0)})
                turn({"n": (i * 2 + 3, 1), "a": (i * 2 + 2, 0), "b": (i * 2 + 1, 1)})
            turn({"a": (H - 1, 1), "b": (H - 2, 0)})
            turn({"b": (H - 1, 1)})

        @block.gpsimd
        def _(pool):
            def stage_n(step, h, p):
                if step[0] == "lu":
                    pool.wait_ge(qk_loaded, h * 32 + 32)
                    log_decay = per_token[:, 0, :, bass.ds(h, 1)]
                    pool.tensor_tensor(full(lu), over_tiles(const("upto")), log_decay[:, 0:NT].broadcast_to([P, NT, P]), ALU.mult)
                    pool.tensor_tensor(tail(lu), const("upto_tail", TAIL), log_decay[0:TAIL, NT].broadcast_to([TAIL, TAIL]),
                                       ALU.mult).then_inc(lu_ready, 1)
                elif step[0] == "mask":
                    N.wait_read(pool, h, "dec2")
                    pool.tensor_tensor(full(dec), full(dec), over_tiles(const("upto")), ALU.mult)
                    pool.tensor_tensor(tail(dec), tail(dec), const("upto_tail", TAIL), ALU.mult).then_inc(dec_masked, 1)
                elif step[0] == "mask_beta":
                    beta = per_token[:, 1, :, bass.ds(h, 1)]
                    pool.wait_ge(dec_masked, h + 1)
                    pool.tensor_tensor(full(bdec), full(dec), beta[:, 0:NT].broadcast_to([P, NT, P]), ALU.mult)
                    pool.tensor_tensor(tail(bdec), tail(dec), beta[0:TAIL, NT].broadcast_to([TAIL, TAIL]),
                                       ALU.mult).then_inc(bdec_ready, 1)

            def stage_a(step, h, p):
                name, k, g = step
                if name == "kt":
                    A.wait_read(pool, h, "eg2")
                    pool.wait_ge(qk_ready, h + 1)
                    pool.tensor_tensor(qd[p][:, :], q[:, :], eg[p][:, :], ALU.mult).then_inc(qd_ready, 1)
                elif name == "kk":
                    for gg in range(3):
                        A.wait_read(pool, h, f"kk{gg}")
                    mask_level(0)
                elif name == "qk":
                    mask_level(1)
                elif name == "Y" and g == 0 and k + 1 < LEVELS:
                    if k == 1:
                        A.wait_read(pool, h, "T02")
                    else:
                        A.wait_done(pool, h, f"Y{k - 1}{2 if k - 1 < TAIL_LEVELS else 1}")
                    mask_level(k + 1)

            def mask_level(k):
                if k < TAIL_LEVELS:
                    pool.tensor_tensor(tail(bk[:, k % 2, :]), tail(bmat), level[0:TAIL, k, 0:TAIL], ALU.mult)
                pool.tensor_tensor(full(bk[:, k % 2, :]), full(bmat), over_tiles(level[:, k, :]), ALU.mult).then_inc(bk_ready, 1)

            def stage_b(step, h, p):
                if step[0] == "ks" and step[1] == NT - 2:
                    pool.wait_ge(b_inputs_used, h + 1)
                    pool.tensor_tensor(late_k[:, 0:NSEG * TAIL], con[:, 0:NSEG * TAIL], con[:, 0:NSEG * TAIL], ALU.subtract).then_inc(segs_zeroed, 1)
                    pool.wait_ge(st_stored, h * 32 + 32)
                    pool.tensor_tensor(late_q[:, 0:NSEG * TAIL], con[:, 0:NSEG * TAIL], con[:, 0:NSEG * TAIL], ALU.subtract).then_inc(segs_zeroed, 1)
                    pool.wait_ge(segs_zeroed, h * 2 + 2)
                    pool.wait_ge(tails_ready, h + 1)
                    pool.wait_ge(qd_ready, h + 1)
                    for seg, flat, src in ((k_seg, late_k, k_tail[p][:, :]), (q_seg, late_q, qd[p][:, NT * P:T])):
                        pool.tensor_tensor(seg[:, 0, 0:PT_TAIL], src[:, 0:PT_TAIL], ones[:, 0:PT_TAIL], ALU.mult)
                        first = TAIL + PT_TAIL
                        ins = pool.tensor_tensor(
                            flat[:, first:first + NS * SPREAD].rearrange("p (s l) -> p s l", l=SPREAD)[:, :, 0:LS],
                            src[:, PT_TAIL:].rearrange("p (s l) -> p s l", l=LS),
                            ones[:, PT_TAIL:TAIL].rearrange("p (s l) -> p s l", l=LS), ALU.mult)
                    ins.then_inc(segs_ready, 1)
                elif step[0] == "out1":
                    B.wait_read(pool, h, "o7")
                    B.wait_read(pool, h, "o8")
                    B.wait_done(pool, h, "ds8_2")
                    pool.wait_ge(b_inputs_used, h + 1)
                    pool.tensor_tensor(o_sq[:, :], o[p][:, :], o[p][:, :], ALU.mult).then_inc(o_sq_ready, 1)

            pool.wait_ge(prep, 2)
            heads(pool, {"n": stage_n, "a": stage_a, "b": stage_b})

        @block.tensor
        def _(pe):
            ps = A.banks
            pe.wait_ge(prep, 1)
            for t in range(NT + 1):
                for r in range(2):
                    mm = pe.transpose(ps[0][0:rows(t), (2 * t + r) * 2 * H:(2 * t + r + 1) * 2 * H],
                                      raw[1 + r][:, tile(t)], ident[0:2 * H, 0:2 * H])
            mm.then_inc(prep_pe, 1)
            pe.wait_ge(prep, 2)
            pe.wait_ge(cons_loaded, 48)
            for r, name in ((1, "upto"), (2, "after")):
                pe.matmul(ps[r][:, 0:NT * H], const(name), per_token[:, 0, 0:NT, :].rearrange("p t h -> p (t h)"),
                          start=True, stop=True)
                mm = pe.matmul(ps[r][0:TAIL, NT * H:(NT + 1) * H], const(name + "_tail", TAIL),
                               per_token[0:TAIL, 0, NT, :], start=True, stop=True)
            mm.then_inc(prep_pe, 1)
            pe.wait_ge(prep_act, 5)
            for f in [*A.free, *N.free, *B.free]:
                pe.sem_inc(f, 1)

            def halved(out, k):
                return out.rearrange("p (a b) -> p a b", b=1 << k)

            def per_tile(h, name, g, product, parts=1):
                A.wait_bank(pe, h, f"{name}{g}")
                t0, n = GROUPS_OF_TILES[g]
                for t in range(t0, t0 + n):
                    r = rows(t)
                    at = (t - t0) * P // parts
                    mm = product(A.ps(f"{name}{g}")[0:r, at:at + r // parts], t)
                mm.then_inc(A.done, 1)

            def turned(h, name, g, src):
                A.wait_bank(pe, h, f"{name}{g}")
                t0, n = GROUPS_OF_TILES[g]
                for t in range(t0, t0 + n):
                    mm = pe.transpose(A.ps(f"{name}{g}")[0:rows(t), (t - t0) * P:(t - t0 + 1) * P], src[:, tile(t)], ident[:, :])
                mm.then_inc(A.done, 1)

            def running_sums(h, units, unit, g, full_w, tail_w, tail_rows):
                units.wait_bank(pe, h, f"{unit}{g}")
                n = P if g < 2 else tail_rows
                cols = span(lu, g).shape[1]
                pe.matmul(units.ps(f"{unit}{g}")[0:n, 0:cols], full_w if g < 2 else tail_w, span(lu, g),
                          start=True, stop=True).then_inc(units.done, 1)

            def stage_n(step, h, p):
                name, _, g = step
                if name == "dec":
                    pe.wait_ge(lu_ready, h + 1)
                    running_sums(h, N, "dec", g, const("after"), const("after_tail", TAIL), TAIL)
                elif name in ("sq", "sk"):
                    r = int(name == "sk")
                    pe.wait_ge(sq_ready, h * 2 + (r + 1))
                    N.wait_bank(pe, h, f"{name}{g}")
                    pe.matmul(N.ps(f"{name}{g}")[:, 0:TH], ones, sq[:, r, third(g)], start=True, stop=True).then_inc(N.done, 1)

            def stage_a(step, h, p):
                name, k, g = step
                kn, xi = k_t, x_inv
                if name == "scale":
                    pe.wait_ge(lu_ready, h + 1)
                    for gg in range(3):
                        running_sums(h, A, "eg", gg, ones, ones[0:TAIL, :], P)
                elif name == "kk":
                    pe.wait_ge(qk_ready, h + 1)
                    for gg in range(3):
                        per_tile(h, "kk", gg, lambda out, t: pe.matmul(out, kn[:, tile(t)], kn[:, tile(t)], start=True, stop=True))
                elif name == "qk":
                    for gg in range(3):
                        per_tile(h, "qk", gg, lambda out, t: pe.matmul(out, kn[:, tile(t)], q[:, tile(t)], start=True, stop=True))
                elif name == "kt":
                    for gg in range(3):
                        turned(h, "kt", gg, kn)
                    pe.wait_ge(v_loaded, h * 16 + 16)
                    for gg in range(3):
                        turned(h, "vt", gg, v)
                elif name == "zero":
                    pe.wait_ge(bk_ready, h * LEVELS + 1)
                    b0 = bk[:, 0, :]
                    for gg in range(3):
                        per_tile(h, "T0", gg, lambda out, t: pe.transpose(out, b0[0:rows(t), tile(t)], ident[0:rows(t), 0:rows(t)]))
                elif name == "Y":
                    if g == 0:
                        pe.wait_ge(bk_ready, h * LEVELS + (k + 1))
                    cur = bk[:, k % 2, :]
                    A.wait_read(pe, h, f"T{k - 1}{g}")
                    per_tile(h, f"Y{k}", g, lambda out, t: pe.matmul(out, cur[0:rows(t), tile(t)], w_inv[0:rows(t), tile(t)],
                                                                     start=True, stop=True))
                elif name == "X":
                    A.wait_read(pe, h, f"Y{k}{g}")
                    per_tile(h, f"X{k}", g, lambda out, t: pe.matmul(
                        halved(out, k), y_lev[0:rows(t), tile(t)], halves(xi[0:rows(t), tile(t)], k, 1), start=True, stop=True), 2)
                    if k < LEVELS - 1:
                        per_tile(h, f"T{k}", g, lambda out, t: pe.matmul(
                            halved(out, k), xi[0:rows(t), tile(t)], halves(y_lev[0:rows(t), tile(t)], k, 0), start=True, stop=True), 2)

                elif name == "kw":
                    turned(h, "kw", g, kn)
                elif name == "u":
                    for gg in range(2):
                        A.wait_read(pe, h, f"X{LEVELS - 1}{gg}")
                    per_tile(h, "u", g, lambda out, t: pe.matmul(out, xi[:, tile(t)], v_tok[:, t, :], start=True, stop=True))
                elif name == "w":
                    A.wait_read(pe, h, f"kw{g}")
                    per_tile(h, "w", g, lambda out, t: pe.matmul(out, keg[:, t, :], xi[:, tile(t)], start=True, stop=True))

            def stage_b(step, h, p):
                name, t, _ = step
                kn, xi, qdp, aq, kd = k_tail[p], x_tail[p], qd[p], aqk[p], kdec[p]
                if name == "ks":
                    if t == 0:
                        pe.wait_ge(st_zeroed, h + 1)
                        pe.wait_ge(qd_ready, h + 1)
                        A.wait_read(pe, h, "w0")
                        A.wait_read(pe, h, "w1")
                        pe.wait_ge(tails_ready, h + 1)
                        pe.wait_ge(x_tail_ready, h + 1)
                    else:
                        B.wait_read(pe, h, f"ds{t - 1}")
                    B.wait_bank(pe, h, f"ks{t}")
                    pe.matmul(B.ps(f"ks{t}")[:, 0:P], w_t[p][:, tile(t)], state[:, 0, :], start=True, stop=True).then_inc(B.done, 1)
                    B.wait_bank(pe, h, f"o{t}")
                    pe.matmul(B.ps(f"o{t}")[:, 0:P], state[:, 0, :], qdp[:, tile(t)], start=True, stop=False)
                elif name == "ds":
                    B.wait_read(pe, h, f"ks{t}")
                    pe.matmul(B.ps(f"ds{t}")[:, 2 * P:3 * P], kd[:, t, :], nu[:, :], start=True, stop=True).then_inc(B.done, 1)
                    pe.matmul(B.ps(f"o{t}")[:, 0:P], nu[:, :], aq[:, tile(t)], start=False, stop=True).then_inc(B.done, 1)
                elif name == "tail1":
                    pe.wait_ge(st_loaded, h * 16 + 16)
                    B.wait_read(pe, h, f"ds{NT - 1}")
                    pe.wait_ge(segs_ready, h + 1)
                    B.wait_bank(pe, h, "ks8")
                    for r in range(NSEG):
                        mm = pe.matmul(B.ps("ks8")[0:TAIL, 0:P], k_seg[:, r, :], state[:, r, :], start=(r == 0), stop=(r == NSEG - 1))
                    mm.then_inc(B.done, 1)
                elif name == "tail2":
                    B.wait_bank(pe, h, "ot8")
                    for r in range(NSEG):
                        pe.matmul(B.ps("ot8")[0:TAIL, 0:P], q_seg[:, r, :], state[:, r, :], start=(r == 0), stop=False)
                    B.wait_read(pe, h, "ks8")
                    pe.matmul(B.ps("nu8")[0:TAIL, 2 * P:3 * P], xi[:, :], resid[:, :], start=True, stop=True).then_inc(B.done, 1)
                elif name == "tail3":
                    B.wait_read(pe, h, "nu8")
                    pe.matmul(B.ps("ot8")[0:TAIL, 0:P], aq[0:TAIL, tile(NT)], nu[0:TAIL, :], start=False, stop=True).then_inc(B.done, 1)
                elif name == "tail4":
                    B.wait_read(pe, h, "ot8")
                    pe.transpose(B.ps("o8")[:, P:P + TAIL], o_tok[:, :], ident[0:TAIL, 0:TAIL]).then_inc(B.done, 1)
                    pe.wait_ge(nu_seg_ready, h + 1)
                    for u in range(3):
                        B.wait_bank(pe, h, f"ds8_{u}")
                        pe.matmul(B.ps(f"ds8_{u}")[:, 0:3 * P], kd[0:TAIL, NT, :],
                                  nu_seg[:, 3 * u:3 * u + 3, :].rearrange("p a b -> p (a b)"), start=True, stop=True).then_inc(B.done, 1)
                elif name == "out2":
                    pe.wait_ge(o_sq_ready, h + 1)
                    for b in range(NB):
                        B.wait_bank(pe, h, f"on{b}")
                        pe.matmul(B.ps(f"on{b}")[:, 0:TH], ones, o_sq[:, third(b)], start=True, stop=True).then_inc(B.done, 1)

            heads(pe, {"n": stage_n, "a": stage_a, "b": stage_b})

        @block.scalar
        def _(act):
            act.wait_ge(cons_loaded, 48)
            act.activation(na[:, :], hp[:, 1:2], ACT.Exp).then_inc(prep_act, 1)
            act.activation(raw[2], ab_rows[:, :], ACT.Exp, scale=-1.0).then_inc(prep_act, 1)
            act.wait_ge(vec, 2)
            act.activation(raw[3], raw[3], ACT.Exp, scale=-1.0).then_inc(prep_act, 1)
            act.wait_ge(prep_act, 3)
            act.activation(raw[3], raw[3], ACT.Ln, bias=ones[0:2 * H, 0:1]).then_inc(prep_act, 1)
            act.wait_ge(prep_pe, 2)
            for r in (1, 2):
                act.activation(per_token[:, 1 + r, 0:NT, :], A.banks[r][:, 0:NT * H].rearrange("p (t h) -> p t h", h=H), ACT.Exp)
                ins = act.activation(per_token[0:TAIL, 1 + r, NT, :], A.banks[r][0:TAIL, NT * H:(NT + 1) * H], ACT.Exp)
            ins.then_inc(prep_act, 1)

            def stage_n(step, h, p):
                name, _, g = step
                if name == "square":
                    if g == 0:
                        act.wait_ge(qk_loaded, h * 32 + 32)
                    act.activation(sq[:, g, :], (q, k_raw)[g][:, :], ACT.Square).then_inc(sq_ready, 1)
                elif name == "dec":
                    N.wait_done(act, h, f"dec{g}")
                    act.activation(span(dec, g), psum(N, f"dec{g}", g), ACT.Exp).then_inc(N.sem(f"dec{g}"), 1)
                elif name in ("sq", "sk"):
                    r = int(name == "sk")
                    N.wait_done(act, h, f"{name}{g}")
                    act.activation(sq[:, r, third(g)], N.ps(f"{name}{g}")[:, 0:TH], ACT.Ln, bias=eps_col).then_inc(N.sem(f"{name}{g}"), 1)
                    if r and g == NB - 1:
                        N.wait_read(act, h, f"{name}{g}")
                        for rr in range(2):
                            act.activation(sq[:, rr, :], sq[:, rr, :], ACT.Exp, scale=-0.5).then_inc(factor, 1)

            def stage_a(step, h, p):
                name, k, g = step
                if name == "scale":
                    for gg in range(3):
                        A.wait_done(act, h, f"eg{gg}")
                        t0, n = GROUPS_OF_TILES[gg]
                        c = slice(t0 * P, min((t0 + n) * P, T))
                        act.activation(eg[p][:, c], A.ps(f"eg{gg}")[:, 0:c.stop - c.start], ACT.Exp).then_inc(A.sem(f"eg{gg}"), 1)
                elif name == "kt":
                    for gg in range(2):
                        A.wait_done(act, h, f"vt{gg}")
                        act.copy(v_tok[:, 4 * gg:4 * gg + 4, :], A.ps(f"vt{gg}").rearrange("p (t d) -> p t d", d=P)) \
                            .then_inc(A.sem(f"vt{gg}"), 1)
                    A.wait_done(act, h, "vt2")
                    act.copy(v_tail[p][:, :], A.ps("vt2")[0:TAIL, 0:P]).then_inc(A.sem("vt2"), 1)
                elif name == "w":
                    A.wait_done(act, h, f"w{g}")
                    act.copy(w_t[p][:, 4 * P * g:4 * P * (g + 1)], A.ps(f"w{g}")[:, :]).then_inc(A.sem(f"w{g}"), 1)
                elif name == "Y":
                    A.wait_done(act, h, f"Y{k}{g}")
                    act.copy(span(y_lev, g), psum(A, f"Y{k}{g}", g)).then_inc(A.sem(f"Y{k}{g}"), 1)

            def stage_b(step, h, p):
                name, t, _ = step
                if name == "ds":
                    if t == 0:
                        act.wait_ge(y_stored, h * 16 + 16)
                    B.wait_done(act, h, f"o{t}")
                    act.copy(o[p][:, tile(t)], B.ps(f"o{t}")[:, 0:P]).then_inc(B.sem(f"o{t}"), 1)
                elif name == "tail3":
                    B.wait_done(act, h, "ot8")
                    act.copy(o_tok[:, :], B.ps("ot8")[0:TAIL, 0:P]).then_inc(B.sem("ot8"), 1)
                elif name == "tail4":
                    B.wait_done(act, h, "o8")
                    act.copy(o[p][:, tile(NT)], B.ps("o8")[:, P:P + TAIL]).then_inc(B.sem("o8"), 1)
                elif name == "out2":
                    B.wait_done(act, h, "on2")
                    for b in range(NB):
                        act.activation(o_sq[:, third(b)], B.ps(f"on{b}")[:, 0:TH], ACT.Ln, bias=eps_col,
                                       scale=1.0 / P).then_inc(B.sem(f"on{b}"), 1)
                    for b in range(NB):
                        B.wait_read(act, h, f"on{b}")
                    act.activation(o_sq[:, :], o_sq[:, :], ACT.Exp, scale=-0.5).then_inc(o_rooted, 1)

            heads(act, {"n": stage_n, "a": stage_a, "b": stage_b})

        @block.vector
        def _(dve):
            ch = Chain(vec)
            dve.sem_inc(a_inputs_used, 1)
            dve.sem_inc(b_inputs_used, 1)
            dve.wait_ge(cons_loaded, 48)
            ch.link(dve, dve.tensor_scalar(raw[0], ab_rows[:, :], hp[:, 0:1], None, ALU.add))
            ch.link(dve, dve.scalar_tensor_tensor(raw[3], raw[0], -1.0, raw[0], ALU.mult, ALU.max))
            ch.link(dve, dve.memset(per_token[:, :, :, :], 0.0))
            dve.wait_ge(prep_act, 1)
            ch.link(dve, dve.tensor_scalar(na[:, :], na[:, :], -1.0, None, ALU.mult))
            dve.wait_ge(prep_act, 4)
            ch.link(dve, dve.scalar_tensor_tensor(raw[1], raw[0], 0.0, raw[3], ALU.max, ALU.add))
            ch.link(dve, dve.tensor_scalar(raw[1], raw[1], na[:, 0:1], None, ALU.mult))
            ch.link(dve, dve.tensor_scalar(raw[2], raw[2], 1.0, None, ALU.add))
            dve.reciprocal(raw[2], raw[2]).then_inc(prep, 1)
            dve.wait_ge(prep_pe, 1)
            tr = A.banks[0][:, 0:(NT + 1) * 4 * H].rearrange("p (t r h) -> p t r h", r=2, h=2 * H)
            for r in range(2):
                cols = slice(r * H, (r + 1) * H)
                dve.tensor_copy(per_token[:, r, 0:NT, :], tr[:, 0:NT, r, cols])
                ins = dve.tensor_copy(per_token[0:TAIL, r, NT, :], tr[0:TAIL, NT, r, cols])
            ins.then_inc(prep, 1)
            dve.wait_ge(prep_act, 5)
            ch.link(dve, dve.tensor_scalar(per_token[:, 2, :, :], per_token[:, 2, :, :], -1.0, None, ALU.mult))

            def per_head(h):
                return [per_token[:, r, :, bass.ds(h, 1)].rearrange("p t o -> p (t o)") for r in range(4)]

            def stage_a(step, h, p):
                name, k, g = step
                if name == "scale":
                    for r, row in enumerate(per_head(h)):
                        ins = dve.tensor_copy(tok[p][:, r, :], row)
                    ins.then_inc(tok_ready, 1)
                    dve.wait_ge(tok_ready, h + 1)
                    dve.wait_ge(factor, h * 2 + 1)
                    dve.scalar_tensor_tensor(q[:, :], q[:, :], float(P) ** -0.5, sq[:, 0, :], ALU.mult, ALU.mult)
                    dve.wait_ge(factor, h * 2 + 2)
                    dve.tensor_tensor(k_t[:, :], k_raw[:, :], sq[:, 1, :], ALU.mult).then_inc(qk_ready, 1)
                elif name == "kk":
                    dve.wait_ge(bdec_ready, h + 1)
                    for gg in range(3):
                        A.wait_done(dve, h, f"kk{gg}")
                        dve.tensor_tensor(span(bmat, gg), psum(A, f"kk{gg}", gg), span(bdec, gg), ALU.mult).then_inc(A.sem(f"kk{gg}"), 1)
                elif name == "qk":
                    for gg in range(3):
                        A.wait_done(dve, h, f"qk{gg}")
                        dve.tensor_tensor(span(aqk[p], gg), psum(A, f"qk{gg}", gg), span(dec, gg), ALU.mult).then_inc(A.sem(f"qk{gg}"), 1)
                elif name == "kt":
                    for gg in range(3):
                        t0, n = GROUPS_OF_TILES[gg]
                        r = rows(t0)
                        A.wait_done(dve, h, f"kt{gg}")
                        dve.tensor_tensor(kdec[p][0:r, t0:t0 + n, :], A.ps(f"kt{gg}")[0:r, 0:n * P].rearrange("p (t d) -> p t d", d=P),
                                          per_row(tok[p][0:r, 3, t0:t0 + n]), ALU.mult).then_inc(A.sem(f"kt{gg}"), 1)
                    dve.tensor_copy(k_tail[p][:, :], k_t[:, NT * P:T]).then_inc(tails_ready, 1)
                    dve.wait_ge(qd_ready, h + 1)
                    A.wait_done(dve, h, "vt2")
                    dve.wait_ge(tails_ready, h + 1)
                    dve.sem_inc(a_inputs_used, 1)
                elif name == "zero":
                    dve.wait_ge(bk_ready, h * LEVELS + 1)
                    b0 = bk[:, 0, :]
                    dve.tensor_tensor(full(x_inv), over_tiles(ident[:, :]), full(b0), ALU.subtract)
                    dve.tensor_tensor(tail(x_inv), ident[0:TAIL, 0:TAIL], tail(b0), ALU.subtract).then_inc(x_started, 1)
                    for gg in range(3):
                        t0, n = GROUPS_OF_TILES[gg]
                        eye = over_tiles(ident[:, :], n) if gg < 2 else ident[0:TAIL, 0:TAIL]
                        split = (lambda a: a.rearrange("p (t i) -> p t i", i=P)) if gg < 2 else (lambda a: a)
                        A.wait_done(dve, h, f"T0{gg}")
                        dve.tensor_tensor(split(span(w_inv, gg)), eye, split(psum(A, f"T0{gg}", gg)), ALU.subtract).then_inc(A.sem(f"T0{gg}"), 1)
                    dve.wait_ge(x_started, h + 1)
                elif name == "kw":
                    A.wait_done(dve, h, f"kw{g}")
                    dve.tensor_tensor(keg[:, 4 * g:4 * g + 4, :], A.ps(f"kw{g}").rearrange("p (t d) -> p t d", d=P),
                                      per_row(tok[p][:, 2, 4 * g:4 * g + 4]), ALU.mult).then_inc(A.sem(f"kw{g}"), 1)
                elif name == "u":
                    if g == 0:
                        A.wait_read(dve, h, f"X{TAIL_LEVELS - 1}2")
                        dve.tensor_copy(x_tail[p][:, :], tail(x_inv)).then_inc(x_tail_ready, 1)
                    A.wait_done(dve, h, f"u{g}")
                    dve.tensor_tensor(u_beta[p][:, 4 * g:4 * g + 4, :], A.ps(f"u{g}").rearrange("p (t d) -> p t d", d=P),
                                      per_row(tok[p][:, 1, 4 * g:4 * g + 4]), ALU.mult).then_inc(A.sem(f"u{g}"), 1)
                elif name == "X":
                    A.wait_done(dve, h, f"T{k}{g}" if k < LEVELS - 1 else f"X{k}{g}")
                    later = halves(span(x_inv, g), k, 1)
                    dve.tensor_tensor(later, later, half_psum(f"X{k}{g}", k, g), ALU.subtract).then_inc(A.sem(f"X{k}{g}"), 1)
                    if k < LEVELS - 1:
                        former = halves(span(w_inv, g), k, 0)
                        dve.tensor_tensor(former, former, half_psum(f"T{k}{g}", k, g), ALU.subtract).then_inc(A.sem(f"T{k}{g}"), 1)

            def stage_b(step, h, p):
                name, t, _ = step
                tk = tok[p]
                if name == "ks":
                    if t == 0:
                        dve.memset(state[:, 0, :], 0.0).then_inc(st_zeroed, 1)
                        A.wait_read(dve, h, "u0")
                        A.wait_read(dve, h, "u1")
                    B.wait_done(dve, h, f"ks{t}")
                    dve.scalar_tensor_tensor(nu[:, :], B.ps(f"ks{t}")[:, 0:P], tk[:, 1, t:t + 1], u_beta[p][:, t, :],
                                             ALU.mult, ALU.add).then_inc(B.sem(f"ks{t}"), 1)
                elif name == "ds":
                    B.wait_done(dve, h, f"ds{t}")
                    dve.scalar_tensor_tensor(state[:, 0, :], state[:, 0, :], eg[p][:, t * P + P - 1:t * P + P],
                                             B.ps(f"ds{t}")[:, 2 * P:3 * P], ALU.mult, ALU.add).then_inc(B.sem(f"ds{t}"), 1)
                elif name == "tail1":
                    B.wait_done(dve, h, "ks8")
                    A.wait_read(dve, h, "vt2")
                    dve.scalar_tensor_tensor(resid[:, :], B.ps("ks8")[0:TAIL, 0:P], tk[0:TAIL, 2, NT:NT + 1], v_tail[p][:, :],
                                             ALU.mult, ALU.add).then_inc(B.sem("ks8"), 1)
                elif name == "tail2":
                    B.wait_done(dve, h, "nu8")
                    dve.tensor_scalar(nu[0:TAIL, :], B.ps("nu8")[0:TAIL, 2 * P:3 * P], tk[0:TAIL, 1, NT:NT + 1], None, ALU.mult) \
                        .then_inc(B.sem("nu8"), 1)
                    B.wait_read(dve, h, "nu8")
                    dve.tensor_tensor(nu_seg[:, :, :], nu[0:TAIL, :].unsqueeze(1).broadcast_to([TAIL, NSEG, P]),
                                      per_row(const("segment", TAIL)), ALU.mult).then_inc(nu_seg_ready, 1)
                elif name == "tail4":
                    B.wait_done(dve, h, "ot8")
                    last = eg[p][:, NT * P + PT_TAIL - 1:T:LS]
                    dve.tensor_tensor(st_out[:, :, :], state[:, :, :], per_row(last), ALU.mult).then_inc(st_scaled, 1)
                    dve.wait_ge(st_scaled, h + 1)
                    for u in range(3):
                        B.wait_done(dve, h, f"ds8_{u}")
                        dve.tensor_tensor(st_out[:, 3 * u:3 * u + 3, :], st_out[:, 3 * u:3 * u + 3, :],
                                          B.ps(f"ds8_{u}")[:, 0:3 * P].rearrange("p (a b) -> p a b", b=P), ALU.add).then_inc(B.sem(f"ds8_{u}"), 1)
                elif name == "out2":
                    dve.wait_ge(o_rooted, h + 1)
                    dve.scalar_tensor_tensor(o[p][:, :], o[p][:, :], gn[:, 0:1], o_sq[:, :], ALU.mult, ALU.mult).then_inc(o_scaled, 1)
                    dve.wait_ge(o_scaled, h + 1)
                    dve.wait_ge(z_loaded, h * 16 + 16)
                    dve.tensor_tensor(o[p][:, :], o[p][:, :], z[:, :], ALU.mult).then_inc(y_ready, 1)
                    dve.wait_ge(y_ready, h + 1)
                    dve.sem_inc(b_inputs_used, 1)

            heads(dve, {"n": lambda step, h, p: None, "a": stage_a, "b": stage_b})


def merge_outputs(nc, x, rstd, ones, eps_col, ident, w_a, w_b, w_o, scratch, sc_tail, gc_tail, prompt_sconv, sample_sconv, prompt_gconv,
                  sample_gconv):
    with ExitStack() as ctx:
        s = Scope(nc, ctx, "mrg")
        y_hi = s.sb("y_hi", [P, KC, T], F32R)
        y_lo = s.sb("y_lo", [P, KC, T], F32R)
        merged = s.sb("merged", [P, KC, T])
        w = WeightStream(s, 2)
        y_raw = s.sb("y_raw", [P, 2, T])
        sig = s.sb("sig", [P, 2, T])
        t_rows = s.sb("tail_rows", [(1 + NS) * (GC_T - 1), 2, 4 * P])
        bank = [s.ps(f"bank{k}", [P, 512]) for k in range(8)]
        nrm = NextNorm(s, rstd, ones, eps_col, y_raw[:, 0, :])
        x_final = s.sem("x_final")
        bank_free = [s.sem(f"bank_free{k}") for k in range(6)]
        unit_done = s.sem("unit_done")
        y_loaded = [s.sem(f"y_loaded{k}") for k in range(2)]
        sig_loaded = [s.sem(f"sig_loaded{k}") for k in range(2)]
        y_hi_done, y_ready, sig_used, merged_done = s.sem("y_hi_done"), s.sem("y_ready"), s.sem("sig_used"), s.sem("merged_done")
        t_turned, t_copied = s.sem("t_turned"), s.sem("t_copied")
        t_stored = [s.sem(f"t_stored{k}") for k in range(2)]
        block = s.block()
        weights = (w_a, w_b, w_o)
        jobs = [("gc", c) for c in range(0, 3 * H, 4)] + [("sc", c) for c in range(0, KC, 4)]

        @block.sync
        def _(sp):
            def loads(r, i):
                for j in range(2):
                    w.load(sp, i, 2, KC * r + j, weights[r][:, bass.ds(i * (2 * P) + j * P, P)].rearrange("(k p) n -> p k n", p=P))

            def load_y(r, c):
                if r or c >= 2:
                    sp.wait_ge(y_ready, KC * r + c - 1)
                sp.dma_start(y_raw[:, c % 2, :], scratch["y_a" if r == 0 else "y_b"][c]).then_inc(y_loaded[c % 2], 16)

            load_y(0, 0)
            load_y(0, 1)
            loads(0, 0)
            for c in range(2, KC):
                load_y(0, c)
            for r in range(3):
                def gates(i):
                    for j in range(2):
                        sp.wait_ge(sig_used, i * 2 + (KC * r + j + 1))
                        sp.dma_start(sig[:, j, :], scratch["sig_a" if r == 0 else "sig_b"][bass.ds(i * 2 + j, 1)]
                                     .rearrange("c p t -> p (c t)")).then_inc(sig_loaded[j], 16)
                with sp.Fori(0, KC // 2 - 1) as i:
                    if r < 2:
                        gates(i)
                    for j in range(2):
                        w.load(sp, i, 2, KC * r + 2 + j,
                               weights[r][:, bass.ds(i * (2 * P) + (2 + j) * P, P)].rearrange("(k p) n -> p k n", p=P))
                if r < 2:
                    gates(KC // 2 - 1)
                    if r == 0:
                        for c in range(2):
                            load_y(1, c)
                    loads(r + 1, 0)
                    if r == 0:
                        for c in range(2, KC):
                            load_y(1, c)

        @block.gpsimd
        def _(pool):
            w.credit_raw(pool)
            nrm.clear(pool)
            with pool.Fori(0, KC) as i:
                for j in range(2):
                    w.split_lo(pool, i, 2, j)
            for j in range(2):
                w.split_lo(pool, 0, 2, 2 * KC + j)
            with pool.Fori(0, KC // 2 - 1) as i:
                for j in range(2):
                    w.split_lo(pool, i, 2, 2 * KC + 2 + j)
                    for b in range(NB):
                        nrm.add(pool, i, 2 * NB, NB * j + b)
            for n in range(NB * (KC - 2), NB * KC):
                nrm.add(pool, 0, 0, n)

        @block.tensor
        def _(pe):
            w.credit_split(pe)
            for k in range(6):
                pe.sem_inc(bank_free[k], 1)
            for n, (which, c) in enumerate(jobs):
                src = gc_tail if which == "gc" else sc_tail
                if n >= 2:
                    pe.wait_ge(t_copied, n - 1)
                for k in range(4):
                    mm = pe.transpose(bank[6 + n % 2][0:src.shape[2], k * P:(k + 1) * P], src[:, c + k, :], ident[:, :])
                mm.then_inc(t_turned, 1)

            def product(j, b, k):
                return three_passes(pe, bank[3 * j + b][:, 0:TH], w.hi[:, j, k, :], w.lo[:, j, k, :],
                                    y_hi[:, k, third(b)], y_lo[:, k, third(b)], k == 0, k == KC - 1)

            def weight_block(r, i, ahead, j):
                n = KC * r + 2 * ahead + j
                pe.wait_ge(w.lo_done, i * 2 + (n + 1))
                for b in range(NB):
                    pe.wait_ge(bank_free[3 * j + b], i + (KC // 2 * r + ahead + 1))
                    for k in range(KC):
                        mm = product(j, b, k)
                    mm.then_inc(unit_done, 1)
                    if b == 1:
                        pe.wait_ge(unit_done, i * 6 + (3 * n + 1))
                        pe.sem_inc(w.split_free, 1)

            for r in range(3):
                pe.wait_ge(w.lo_done, KC * r + 1)
                for b in range(NB):
                    pe.wait_ge(bank_free[b], KC // 2 * r + 1)
                if r:
                    pe.wait_ge(unit_done, NB * KC * r)
                pe.sem_inc(w.split_free, 1)
                for k in range(KC):
                    pe.wait_ge(y_ready, KC * r + k + 1)
                    for b in range(NB):
                        mm = product(0, b, k)
                        if k == KC - 1:
                            mm.then_inc(unit_done, 1)
                weight_block(r, 0, 0, 1)
                with pe.Fori(0, KC // 2 - 1) as i:
                    for j in range(2):
                        weight_block(r, i, 1, j)
            for b in range(NB):
                pe.wait_ge(bank_free[b], 3 * KC // 2 + 1)
                nrm.sum(pe, bank[b][:, 0:TH], b)

        @block.scalar
        def _(act):
            w.split_hi(act, 0, 2, 0)
            for n, (which, c) in enumerate(jobs):
                act.wait_ge(t_turned, n + 1)
                if n >= 2:
                    act.wait_ge(t_stored[n % 2], 32 * (n // 2))
                rows = (gc_tail if which == "gc" else sc_tail).shape[2]
                act.copy(t_rows[0:rows, n % 2, :], bank[6 + n % 2][0:rows, :]).then_inc(t_copied, 1)
                act.wait_ge(t_copied, n + 1)
                g = (GC_T if which == "gc" else SC_T) - 1
                p_out, s_out = (prompt_gconv, sample_gconv) if which == "gc" else (prompt_sconv, sample_sconv)
                act.dma_start(p_out[0, 0][:, c * P:(c + 4) * P], t_rows[0:g, n % 2, :]).then_inc(t_stored[n % 2], 16)
                act.dma_start(s_out[0][:, :, c * P:(c + 4) * P].rearrange("s t c -> (s t) c"),
                              t_rows[g:(1 + NS) * g, n % 2, :]).then_inc(t_stored[n % 2], 16)
            for r in range(3):
                for c in range(KC):
                    if r and c == 0:
                        act.wait_ge(unit_done, 3 * KC * r)
                    if r < 2:
                        act.wait_ge(y_loaded[c % 2], 16 * (KC // 2 * r + c // 2 + 1))
                    else:
                        act.wait_ge(merged_done, 2 * NB * KC)
                    act.copy(y_hi[:, c, :], y_raw[:, c % 2, :] if r < 2 else merged[:, c, :]).then_inc(y_hi_done, 1)
                if r < 2:
                    with act.Fori(0, KC // 2) as i:
                        for j in range(2):
                            w.split_hi(act, i, 2, KC * r + j + 1)

            def squares(i, j):
                for b in range(NB):
                    act.wait_ge(x_final, i * 6 + (NB * j + b + 1))
                    nrm.square(act, x[:, bass.ds(i * 2 + j, 1), third(b)].rearrange("p o t -> p (o t)"), i, 6, NB * j + b)

            w.split_hi(act, 0, 2, 2 * KC + 1)
            with act.Fori(0, KC // 2 - 1) as i:
                for j in range(2):
                    w.split_hi(act, i, 2, 2 * KC + 2 + j)
                    squares(i, j)
            for j in range(2):
                squares(KC // 2 - 1, j)
            nrm.factors(act, lambda b: bank[b][:, 0:TH])
            for k in range(2):
                act.wait_ge(t_stored[k], 16 * len(jobs))

        @block.vector
        def _(dve):
            dve.sem_inc(sig_used, 2)
            for r in range(3):
                for c in range(KC):
                    dve.wait_ge(y_hi_done, KC * r + c + 1)
                    dve.tensor_tensor(y_lo[:, c, :], y_raw[:, c % 2, :] if r < 2 else merged[:, c, :],
                                      y_hi[:, c, :].bitcast(F32), ALU.subtract).then_inc(y_ready, 1)
                with dve.Fori(0, KC // 2) as i:
                    for j in range(2):
                        if r < 2:
                            dve.wait_ge(sig_loaded[j], i * 16 + 16 * (KC // 2 * r + 1))
                        for b in range(NB):
                            dve.wait_ge(unit_done, i * 6 + (3 * (KC * r + j) + b + 1))
                            ps = bank[3 * j + b][:, 0:TH]
                            m = merged[:, bass.ds(i * 2 + j, 1), third(b)].rearrange("p o t -> p (o t)")
                            xc = x[:, bass.ds(i * 2 + j, 1), third(b)].rearrange("p o t -> p (o t)")
                            g = sig[:, j, third(b)]
                            if r == 0:
                                dve.tensor_tensor(m, ps, g, ALU.mult).then_inc(bank_free[3 * j + b], 1)
                                dve.wait_ge(bank_free[3 * j + b], i + 2)
                                dve.sem_inc(merged_done, 1)
                            elif r == 1:
                                dve.tensor_tensor(g, ps, g, ALU.mult).then_inc(bank_free[3 * j + b], 1)
                                dve.wait_ge(bank_free[3 * j + b], i + (KC // 2 + 2))
                                dve.tensor_tensor(m, m, g, ALU.add).then_inc(merged_done, 1)
                            else:
                                dve.tensor_tensor(xc, ps, xc, ALU.add).then_inc(x_final, 1)
                                dve.wait_ge(x_final, i * 6 + (NB * j + b + 1))
                                dve.sem_inc(bank_free[3 * j + b], 1)
                        if r < 2:
                            dve.wait_ge(merged_done, i * 6 + (3 * (KC * r + j) + NB))
                            dve.sem_inc(sig_used, 1)


def build(nc, c, out):
    scratch = {}
    for name, shape in (("y_a", (KC, P, T)), ("y_b", (H, P, T)), ("qkv", (3, H, P, T)), ("z", (H, P, T)),
                        ("sig_a", (KC, P, T)), ("sig_b", (KC, P, T))):
        scratch[name] = nc.dram_tensor(f"scratch_{name}", shape, F32, kind="Internal").ap()
    with ExitStack() as ctx:
        s = Scope(nc, ctx, "g")
        x = s.sb("x", [P, KC, T])
        ident = s.sb("ident", [P, P])
        ones = s.sb("ones", [P, P])
        gains = s.sb("gains", [P, 4, KC])
        taps = s.sb("taps", [P, KC * SC_T + 3 * H * GC_T])
        eps = s.sb("eps", [P, 1])
        sc_hist = s.sb("sc_hist", [P, KC, NS * (SC_T - 1)])
        gc_hist = s.sb("gc_hist", [P, 3 * H, NS * (GC_T - 1)])
        sc_tail = s.sb("sc_tail", [P, KC, NSEG * (SC_T - 1)])
        gc_tail = s.sb("gc_tail", [P, 3 * H, NSEG * (GC_T - 1)])
        ab_rows = s.sb("ab_rows", [2 * H, T])
        eps_col = eps[:, 0:1]
        with nc.sbuf_tensor("rstd_1", [P, T], F32) as rstd:
            transpose_inputs(nc, c, x, rstd, ident, ones, eps, gains, taps, sc_hist, gc_hist)
            ffn(nc, "ffn1", x, rstd, gains, 0, ones[:, :], eps_col, c["ffn1_w_gate"][0], c["ffn1_w_up"][0], c["ffn1_w_down"][0])
            input_projections(nc, x, rstd, gains, c["w_in"][0],
                              taps[:, 0:KC * SC_T].rearrange("p (c t) -> p c t", t=SC_T),
                              taps[:, KC * SC_T:].rearrange("p (c t) -> p c t", t=GC_T),
                              sc_hist, gc_hist, sc_tail, gc_tail, ab_rows, scratch)
        delta_rule(nc, ones[:, :], ident, eps_col, c["delta_consts"], c["head_params"], c["g_norm"], ab_rows,
                   c["state_gdn"], scratch, out["prompt_gdn"], out["sample_gdn"])
        with nc.sbuf_tensor("rstd_2", [P, T], F32) as rstd:
            merge_outputs(nc, x, rstd, ones[:, :], eps_col, ident, c["w_a_out"][0], c["w_b_out"][0], c["w_o"][0], scratch,
                          sc_tail, gc_tail, out["prompt_sconv"], out["sample_sconv"], out["prompt_gdn_conv"],
                          out["sample_gdn_conv"])
            ffn(nc, "ffn2", x, rstd, gains, 2, ones[:, :], eps_col, c["ffn2_w_gate"][0], c["ffn2_w_up"][0], c["ffn2_w_down"][0])
            final_output(nc, x, rstd, gains, 3, ident, out["y_prompt"], out["y_sample"])


OUTPUTS = {
    "y_prompt": (1, SEQ, D), "y_sample": (NS, LS, D), "prompt_sconv": (1, 1, SC_T - 1, D),
    "prompt_gdn_conv": (1, 1, GC_T - 1, QKV), "prompt_gdn": (1, 1, H, P, P), "sample_sconv": (1, NS, SC_T - 1, D),
    "sample_gdn_conv": (1, NS, GC_T - 1, QKV), "sample_gdn": (1, NS, H, P, P),
}


def laid_out(inputs):
    a = {name: np.ascontiguousarray(v) for name, v in inputs.items()}

    def features_first(v):
        v = v.reshape(-1, v.shape[-1] // P, P).transpose(2, 1, 0)
        return v

    gains = [features_first(a.pop(n)).reshape(P, KC) for n in ("norm_ffn1", "norm_mix", "norm_ffn2", "norm_final")]
    taps = [features_first(a.pop(n)).reshape(P, -1) for n in ("sconv_w", "gdn_conv_w")]
    a["gains"] = np.concatenate(gains, 1)
    a["taps"] = np.concatenate(taps, 1)
    empty = np.zeros((1, H), np.float32)
    a["head_params"] = np.concatenate([np.stack([a.pop("gdn_dt_bias")[0], a.pop("gdn_a_log")[0]], 1),
                                       np.concatenate([empty, empty]).T], 0)
    a["g_norm"] = a.pop("gdn_norm").reshape(P, 1)
    a["delta_consts"] = delta_constants()
    a["identity"] = np.eye(P, dtype=np.float32)
    return a


def kernel(**inputs):
    from concourse import bacc
    from concourse.bass_utils import run_bass_kernel_spmd

    nc = bacc.Bacc("TRN2", target_bir_lowering=False, num_devices=1)
    arrays, args = {}, {}
    for name, a in laid_out(inputs).items():
        arrays[f"in_{name}"] = np.ascontiguousarray(a)
        args[name] = nc.dram_tensor(f"in_{name}", a.shape, F32, kind="ExternalInput").ap()
    outs = {n: nc.dram_tensor(f"out_{n}", shape, F32, kind="ExternalOutput").ap() for n, shape in OUTPUTS.items()}
    build(nc, args, outs)
    r = run_bass_kernel_spmd(nc, [arrays], core_ids=[0])
    return tuple(r.results[0][f"out_{n}"] for n in OUTPUTS)
```
